# Optimizing a Trainium2 kernel written in Bass

```python
import math
import jax
import jax.numpy as jnp
from jax import lax
import numpy as np

D_MODEL = 1024
BATCH = 1
SEQ = 1024
DEPTH = 1
DEC_BATCH = 8
DEC_SEQ = 16
PAST_LEN = 256

CHUNK = 64
N_HEADS_A = 8
N_KV_A = 2
GROUP_A = N_HEADS_A // N_KV_A
HEAD_DIM_A = 64
N_IDX_HEADS = 4
IDX_DIM = 64
TOPK_MAX = 256
Q_BLOCK = 128
N_HEADS_B = 4
DK_B = 128
DV_B = 128
CONV_W = 4
D_FF = 2816
EPS = 1e-6

WIDTH_A = N_HEADS_A * HEAD_DIM_A
WIDTH_KV_A = N_KV_A * HEAD_DIM_A
WIDTH_IDX_Q = N_IDX_HEADS * IDX_DIM
WIDTH_QK_B = N_HEADS_B * DK_B
WIDTH_V_B = N_HEADS_B * DV_B
CONV_CH = 2 * WIDTH_QK_B + WIDTH_V_B
SPLITS = (WIDTH_A, WIDTH_KV_A, WIDTH_KV_A, WIDTH_IDX_Q, IDX_DIM, N_IDX_HEADS,
          WIDTH_QK_B, WIDTH_QK_B, WIDTH_V_B, WIDTH_V_B, N_HEADS_B, N_HEADS_B,
          D_MODEL, D_MODEL)
D_IN = (WIDTH_A + 2 * WIDTH_KV_A + WIDTH_IDX_Q + IDX_DIM + N_IDX_HEADS
        + 2 * WIDTH_QK_B + 2 * WIDTH_V_B + 2 * N_HEADS_B + 2 * D_MODEL)

kernel_name = 'hybrid_dsa_gdn_macaron_stream_step'

def rms_norm(x, g):
    xf = x.astype(jnp.float32)
    y = xf * lax.rsqrt(jnp.mean(xf * xf, axis=-1, keepdims=True) + EPS)
    return (y * g.astype(jnp.float32)).astype(x.dtype)

def l2norm(x):
    return x * lax.rsqrt(jnp.sum(x * x, axis=-1, keepdims=True) + EPS)

def swiglu(x, w_gate, w_up, w_down):
    return (jax.nn.silu(x @ w_gate) * (x @ w_up)) @ w_down

def split_columns(p):
    offsets = np.cumsum(np.array(SPLITS))[:-1].tolist()
    return jnp.split(p, offsets, axis=-1)

def dsa_block(q, qi, wi, pos, k, v, ki, n_sel):
    f32 = jnp.float32
    n_keys = k.shape[1]
    limit = jnp.minimum((pos // CHUNK + 1) * CHUNK, n_keys)
    admissible = jnp.arange(n_keys)[None, :] < limit[:, None]
    logits = jnp.einsum('bthd,bsd->bths', qi.astype(f32), ki.astype(f32))
    score = jnp.einsum('bths,bth->bts', jax.nn.relu(logits), wi.astype(f32))
    score = jnp.where(admissible[None], score, -jnp.inf)
    _, sel = lax.top_k(score, n_sel)
    sel_ok = sel < limit[None, :, None]
    kv = jnp.concatenate([k, v], axis=-1)
    kv_sel = jax.vmap(lambda rows, idx: rows[idx])(kv, sel).astype(f32)
    k_sel = kv_sel[..., :HEAD_DIM_A]
    v_sel = kv_sel[..., HEAD_DIM_A:]
    s = jnp.einsum('btngd,btknd->btngk', q.astype(f32), k_sel) * (HEAD_DIM_A ** -0.5)
    s = jnp.where(sel_ok[:, :, None, None, :], s, -jnp.inf)
    p = jax.nn.softmax(s, axis=-1)
    o = jnp.einsum('btngk,btknd->btngd', p, v_sel)
    return o.astype(q.dtype)

def dsa_prompt(q, qi, wi, k, v, ki):
    b, t = q.shape[0], q.shape[1]
    nb = t // Q_BLOCK
    n_sel = min(TOPK_MAX, k.shape[1] // 4)

    def to_blocks(a):
        return jnp.moveaxis(a.reshape((b, nb, Q_BLOCK) + a.shape[2:]), 1, 0)

    pos = jnp.arange(t, dtype=jnp.int32).reshape(nb, Q_BLOCK)

    def one_block(args):
        qb, qib, wib, posb = args
        return dsa_block(qb, qib, wib, posb, k, v, ki, n_sel)

    o = lax.map(one_block, (to_blocks(q), to_blocks(qi), to_blocks(wi), pos))
    return jnp.moveaxis(o, 0, 1).reshape((b, t) + o.shape[3:])

def dsa_step(q, qi, wi, k_all, v_all, ki_all, past_len):
    t = q.shape[1]
    n_sel = min(TOPK_MAX, k_all.shape[1] // 4)
    pos = past_len + jnp.arange(t, dtype=jnp.int32)
    return dsa_block(q, qi, wi, pos, k_all, v_all, ki_all, n_sel)

def delta_chunk(state, inputs):
    q, k, v, g, beta = inputs
    c = q.shape[2]
    tri = jnp.tril(jnp.ones((c, c), dtype=bool))
    strict = jnp.tril(jnp.ones((c, c), dtype=bool), k=-1)
    gc = jnp.cumsum(g, axis=-1)
    decay = jnp.exp(jnp.where(tri, gc[..., :, None] - gc[..., None, :], -jnp.inf))
    k_beta = k * beta[..., None]
    lower = jnp.where(strict, jnp.einsum('bhid,bhjd->bhij', k_beta, k) * decay, 0.0)
    a = jnp.eye(c, dtype=q.dtype) + lower
    rhs = jnp.concatenate([v * beta[..., None], k_beta * jnp.exp(gc)[..., None]], axis=-1)
    sol = lax.linalg.triangular_solve(a, rhs, left_side=True, lower=True, unit_diagonal=True)
    u = sol[..., :DV_B]
    w = sol[..., DV_B:]
    v_new = u - jnp.einsum('bhcd,bhde->bhce', w, state)
    attn = jnp.where(tri, jnp.einsum('bhid,bhjd->bhij', q, k) * decay, 0.0)
    o = (jnp.einsum('bhcd,bhde->bhce', q * jnp.exp(gc)[..., None], state)
         + jnp.einsum('bhij,bhje->bhie', attn, v_new))
    g_last = gc[..., -1:]
    new_state = (state * jnp.exp(g_last)[..., None]
                 + jnp.einsum('bhcd,bhce->bhde', k * jnp.exp(g_last - gc)[..., None], v_new))
    return new_state, o

def gated_deltanet(qb, kb, vb, zb, bb, ab, conv_state, state, conv_w, a_log, dt_bias, norm_g, chunk):
    f32 = jnp.float32
    b, t, _ = qb.shape
    xc = jnp.concatenate([qb, kb, vb], axis=-1)
    xpad = jnp.concatenate([conv_state.astype(xc.dtype), xc], axis=1)
    yc = xpad[:, 0:t] * conv_w[0]
    for j in range(1, CONV_W):
        yc = yc + xpad[:, j:j + t] * conv_w[j]
    new_conv = xpad[:, t:]
    yc = jax.nn.silu(yc).astype(f32)
    q, k, v = jnp.split(yc, [WIDTH_QK_B, 2 * WIDTH_QK_B], axis=-1)

    def heads(a, d):
        return jnp.transpose(a.reshape(b, t, N_HEADS_B, d), (0, 2, 1, 3))

    q = l2norm(heads(q, DK_B)) * (DK_B ** -0.5)
    k = l2norm(heads(k, DK_B))
    v = heads(v, DV_B)
    beta = jnp.transpose(jax.nn.sigmoid(bb.astype(f32)), (0, 2, 1))
    g = -jnp.exp(a_log.astype(f32)) * jax.nn.softplus(ab.astype(f32) + dt_bias.astype(f32))
    g = jnp.transpose(g, (0, 2, 1))
    nc = t // chunk

    def to_chunks(a):
        return jnp.moveaxis(a.reshape((b, N_HEADS_B, nc, chunk) + a.shape[3:]), 2, 0)

    s_final, o = lax.scan(delta_chunk, state.astype(f32),
                          (to_chunks(q), to_chunks(k), to_chunks(v), to_chunks(g), to_chunks(beta)))
    o = jnp.moveaxis(o, 0, 2).reshape(b, N_HEADS_B, t, DV_B)
    o = jnp.transpose(o, (0, 2, 1, 3))
    z = zb.reshape(b, t, N_HEADS_B, DV_B).astype(f32)
    o = rms_norm(o, norm_g) * jax.nn.silu(z)
    return o.reshape(b, t, WIDTH_V_B).astype(qb.dtype), new_conv, s_final

def layer(x, w, past):
    b, t, _ = x.shape
    x = x + 0.5 * swiglu(rms_norm(x, w['ffn1_norm']), w['ffn1_w_gate'], w['ffn1_w_up'], w['ffn1_w_down'])
    h = rms_norm(x, w['mix_norm'])
    (qa, ka, va, qi, ki, wi, qb, kb, vb, zb, bb, ab, gate_a, gate_b) = split_columns(h @ w['w_in'])
    qa = qa.reshape(b, t, N_KV_A, GROUP_A, HEAD_DIM_A)
    ka = ka.reshape(b, t, N_KV_A, HEAD_DIM_A)
    va = va.reshape(b, t, N_KV_A, HEAD_DIM_A)
    qi = qi.reshape(b, t, N_IDX_HEADS, IDX_DIM) * (IDX_DIM ** -0.5)
    wi = wi * (N_IDX_HEADS ** -0.5)
    if past is None:
        oa = dsa_prompt(qa, qi, wi, ka, va, ki)
        conv0 = jnp.zeros((b, CONV_W - 1, CONV_CH), x.dtype)
        s0 = jnp.zeros((b, N_HEADS_B, DK_B, DV_B), jnp.float32)
        chunk = CHUNK
    else:
        ck, cv, cki, conv0, s0 = past
        oa = dsa_step(qa, qi, wi,
                      jnp.concatenate([ck, ka], axis=1),
                      jnp.concatenate([cv, va], axis=1),
                      jnp.concatenate([cki, ki], axis=1),
                      ck.shape[1])
        chunk = t
    ob, conv_new, s_new = gated_deltanet(qb, kb, vb, zb, bb, ab, conv0, s0, w['conv_w'],
                                         w['a_log'], w['dt_bias'], w['delta_norm'], chunk)
    ya = oa.reshape(b, t, WIDTH_A) @ w['w_branch_a']
    yb = ob @ w['w_branch_b']
    merged = jax.nn.sigmoid(gate_a) * ya + jax.nn.sigmoid(gate_b) * yb
    x = x + merged @ w['w_out']
    x = x + 0.5 * swiglu(rms_norm(x, w['ffn2_norm']), w['ffn2_w_gate'], w['ffn2_w_up'], w['ffn2_w_down'])
    return x, (ka, va, ki, conv_new, s_new.astype(x.dtype))

def setup_inputs(seed: int = 0) -> dict:
    key = jax.random.key(seed)
    ks = jax.random.split(key, 26)
    f32 = jnp.float32

    def normal(k, shape, scale=1.0):
        return scale * jax.random.normal(k, shape, f32)

    def gain(k, shape):
        return 1.0 + 0.02 * jax.random.normal(k, shape, f32)

    dt = jnp.exp(jax.random.uniform(ks[15], (DEPTH, N_HEADS_B), f32, math.log(1e-3), math.log(1e-1)))
    return {
        'x_prompt': normal(ks[0], (BATCH, SEQ, D_MODEL)),
        'x_sample': normal(ks[1], (DEC_BATCH, DEC_SEQ, D_MODEL)),
        'cache_attn_k': normal(ks[2], (DEPTH, DEC_BATCH, PAST_LEN, N_KV_A, HEAD_DIM_A)),
        'cache_attn_v': normal(ks[3], (DEPTH, DEC_BATCH, PAST_LEN, N_KV_A, HEAD_DIM_A)),
        'cache_idx_k': normal(ks[4], (DEPTH, DEC_BATCH, PAST_LEN, IDX_DIM)),
        'state_conv': normal(ks[5], (DEPTH, DEC_BATCH, CONV_W - 1, CONV_CH)),
        'state_delta': normal(ks[6], (DEPTH, DEC_BATCH, N_HEADS_B, DK_B, DV_B), 0.5),
        'ffn1_norm': gain(ks[7], (DEPTH, D_MODEL)),
        'ffn1_w_gate': normal(ks[8], (DEPTH, D_MODEL, D_FF), D_MODEL ** -0.5),
        'ffn1_w_up': normal(ks[9], (DEPTH, D_MODEL, D_FF), D_MODEL ** -0.5),
        'ffn1_w_down': normal(ks[10], (DEPTH, D_FF, D_MODEL), D_FF ** -0.5),
        'mix_norm': gain(ks[11], (DEPTH, D_MODEL)),
        'w_in': normal(ks[12], (DEPTH, D_MODEL, D_IN), D_MODEL ** -0.5),
        'conv_w': normal(ks[13], (DEPTH, CONV_W, CONV_CH), CONV_W ** -0.5),
        'a_log': jnp.log(jax.random.uniform(ks[14], (DEPTH, N_HEADS_B), f32, 1.0, 16.0)),
        'dt_bias': dt + jnp.log(-jnp.expm1(-dt)),
        'delta_norm': gain(ks[16], (DEPTH, DV_B)),
        'w_branch_a': normal(ks[17], (DEPTH, WIDTH_A, D_MODEL), WIDTH_A ** -0.5),
        'w_branch_b': normal(ks[18], (DEPTH, WIDTH_V_B, D_MODEL), WIDTH_V_B ** -0.5),
        'w_out': normal(ks[19], (DEPTH, D_MODEL, D_MODEL), D_MODEL ** -0.5),
        'ffn2_norm': gain(ks[20], (DEPTH, D_MODEL)),
        'ffn2_w_gate': normal(ks[21], (DEPTH, D_MODEL, D_FF), D_MODEL ** -0.5),
        'ffn2_w_up': normal(ks[22], (DEPTH, D_MODEL, D_FF), D_MODEL ** -0.5),
        'ffn2_w_down': normal(ks[23], (DEPTH, D_FF, D_MODEL), D_FF ** -0.5),
        'final_norm': gain(ks[24], (D_MODEL,)),
    }

def reference(x_prompt, x_sample, cache_attn_k, cache_attn_v, cache_idx_k, state_conv, state_delta,
              ffn1_norm, ffn1_w_gate, ffn1_w_up, ffn1_w_down, mix_norm, w_in, conv_w, a_log, dt_bias,
              delta_norm, w_branch_a, w_branch_b, w_out, ffn2_norm, ffn2_w_gate, ffn2_w_up, ffn2_w_down,
              final_norm):
    xp = x_prompt
    xs = x_sample
    st_p = []
    st_s = []
    for l in range(DEPTH):
        w = {
            'ffn1_norm': ffn1_norm[l], 'ffn1_w_gate': ffn1_w_gate[l], 'ffn1_w_up': ffn1_w_up[l],
            'ffn1_w_down': ffn1_w_down[l], 'mix_norm': mix_norm[l], 'w_in': w_in[l], 'conv_w': conv_w[l],
            'a_log': a_log[l], 'dt_bias': dt_bias[l], 'delta_norm': delta_norm[l],
            'w_branch_a': w_branch_a[l], 'w_branch_b': w_branch_b[l], 'w_out': w_out[l],
            'ffn2_norm': ffn2_norm[l], 'ffn2_w_gate': ffn2_w_gate[l], 'ffn2_w_up': ffn2_w_up[l],
            'ffn2_w_down': ffn2_w_down[l],
        }
        xp, sp = layer(xp, w, None)
        xs, ss = layer(xs, w, (cache_attn_k[l], cache_attn_v[l], cache_idx_k[l], state_conv[l], state_delta[l]))
        st_p.append(sp)
        st_s.append(ss)
    y_prompt = rms_norm(xp, final_norm)
    y_sample = rms_norm(xs, final_norm)

    def stacked(states, i):
        return jnp.stack([s[i] for s in states], axis=0)

    return (y_prompt, y_sample,
            stacked(st_p, 0), stacked(st_p, 1), stacked(st_p, 2), stacked(st_p, 3), stacked(st_p, 4),
            stacked(st_s, 0), stacked(st_s, 1), stacked(st_s, 2), stacked(st_s, 3), stacked(st_s, 4))


_drawn_inputs = setup_inputs


def setup_inputs(seed=0):
    import zlib

    import numpy as np

    out = dict(_drawn_inputs(seed))
    spreads = {}
    factors = {'ffn1_norm': 4.232,
     'delta_norm': 41.289,
     'ffn2_norm': 7.78,
     'final_norm': 8.125,
     'cache_attn_k': 3.548,
     'cache_attn_v': 2.754,
     'cache_idx_k': 3.139,
     'w_branch_a': 2.681}
    for name, (base, spread) in spreads.items():
        noise = np.random.default_rng([zlib.crc32(name.encode()), seed]).standard_normal(out[name].shape)
        drawn = base * np.exp(spread * noise) if base else spread * noise
        out[name] = jnp.asarray(drawn.astype(out[name].dtype))
    for name, factor in factors.items():
        out[name] = (out[name] * factor).astype(out[name].dtype)
    return out
```

```python
from contextlib import ExitStack

import numpy as np

import concourse.bass as bass
from concourse import mybir

F32 = mybir.dt.float32
F32R = mybir.dt.float32r
ALU = mybir.AluOpType
ACT = mybir.ActivationFunctionType
AX = mybir.AxisListType

P = 128
D = 1024
KD = D // P
DFF = 2816
NF = DFF // P
SEQ = 1024
BATCH_S, SEQ_S, PAST = 8, 16, 256
TOK = SEQ + BATCH_S * SEQ_S
NT = TOK // P
NTP = SEQ // P
TG = 384
NG = TOK // TG
EPS = 1e-6

HEADS, KV, HD = 8, 2, 64
IH = 4
CHUNK = 64
TOPK_P, TOPK_S = 256, 68
KEYS_S = PAST + SEQ_S
HB, DK = 4, 128
CONV_CH, CONV_W = 1536, 4
NC = CONV_CH // P
C_Q, C_K, C_V, C_QI, C_KI, C_WI = 0, 512, 640, 768, 1024, 1088
C_CONV, C_Z, C_BB, C_GATE = 1092, 2628, 3140, 3148
D_IN = 5196
SMALL = 256 + 68 + 8
S_V, S_KI, S_WI, S_BB = 128, 256, 320, 324

TAKEN, INADMISSIBLE, FILL, UNSELECTED = -3.0e38, -2.0e38, -1.0e38, -1.0e30
WIDTH = [P * (t + 1) for t in range(NTP)] + [KEYS_S]
PAD_S = 8
AT = [sum(WIDTH[:t]) for t in range(NT)]
SCORES = sum(WIDTH) + PAD_S

ONES, IDENT, UPTO, UPTO_S, SAME_S, BATCH_OF, LEVEL = range(7)
LEVELS_P, LEVELS_S = 7, 4
CONSTS = LEVEL + LEVELS_P


def constants():
    i, j = np.arange(P)[:, None], np.arange(P)[None, :]
    same = i // SEQ_S == j // SEQ_S
    planes = [np.ones((P, P)), i == j, i <= j, (i <= j) & same, same, (i // SEQ_S == j)]
    for level in range(LEVELS_P):
        m = 1 << level
        planes.append((i // (2 * m) == j // (2 * m)) & (i % (2 * m) >= m) & (j % (2 * m) < m))
    return np.ascontiguousarray(np.stack([np.asarray(p, np.float32) for p in planes], 1))


def known(n, below):
    return isinstance(n, int) and n < below


def in_steps(eng, step, first, last, lead=1):
    n = first
    while n < min(first + lead, last):
        step(n, n % 2)
        n += 1
    pairs = (last - n) // 2
    if pairs > 1:
        with eng.Fori(0, pairs) as j:
            step(2 * j + n, n % 2)
            step(2 * j + n + 1, (n + 1) % 2)
        n += 2 * pairs
    while n < last:
        step(n, n % 2)
        n += 1


class Scope:

    def __init__(self, nc, name):
        self.nc, self.name, self.stack, self.sems = nc, name, ExitStack(), []

    def __enter__(self):
        return self

    def __exit__(self, *what):
        left = self.stack.__exit__(*what)
        if self.sems:
            self.nc.clear_and_free_semaphores(self.sems)
            self.nc.all_engine_barrier()
        return left

    def sbuf(self, name, shape, dt=F32):
        return self.stack.enter_context(self.nc.sbuf_tensor(self.name + name, shape, dt))

    def psum(self, name, shape=(P, 512)):
        return self.stack.enter_context(self.nc.psum_tensor(self.name + name, list(shape), F32))

    def sem(self, name):
        self.sems.append(self.nc.alloc_semaphore(self.name + name))
        return self.sems[-1]

    def block(self):
        return self.stack.enter_context(self.nc.Block())


def three_passes(nc, out, stationary, moving, ks):
    n, mm = 3 * len(ks), None
    for at, k in enumerate(ks):
        for i, (a, b) in enumerate(((0, 0), (0, 1), (1, 0))):
            mm = nc.tensor.matmul(out, stationary(k)[a], moving(k)[b], start=(at == 0 and i == 0),
                                  stop=(3 * at + i == n - 1))
    return mm


def load_start(nc, x, const, x_prompt, x_sample, const_in):
    with Scope(nc, "in_") as s:
        x_in, const_ready = s.sem("x_in"), s.sem("const_in")
        block = s.block()

        @block.sync
        def _(sp):
            sp.dma_start(x[:, 0:NTP, :], x_prompt[0].rearrange("(t p) d -> p t d", p=P)).then_inc(x_in, 16)
            sp.wait_ge(x_in, 16)

        @block.scalar
        def _(act):
            act.dma_start(x[:, NTP, :], x_sample.rearrange("b s d -> (b s) d")).then_inc(const_ready, 16)
            act.dma_start(const[:], const_in).then_inc(const_ready, 16)
            act.wait_ge(const_ready, 32)


def norm_turn(nc, x, const, hT_hi, hT_lo, gain, name):
    with Scope(nc, name) as s:
        gain_b = s.sbuf("gain_b", [P, D])
        sumsq, mean, root, rstd = (s.sbuf(n, [P, NT]) for n in ("sumsq", "mean", "root", "rstd"))
        h = s.sbuf("h", [P, 2, D])
        pT = [s.psum(f"pT{i}", (P, 4, P)) for i in range(4)]
        gain_in, squared, mean_ready, rooted, rstd_ready = (
            s.sem(n) for n in ("gain_in", "squared", "mean_ready", "rooted", "rstd_ready"))
        h_ready, turned, hi_ready, lo_ready = (s.sem(n) for n in ("h_ready", "turned", "hi_ready", "lo_ready"))
        block = s.block()

        def part(i):
            return slice(None), slice(4 * (i % 2), 4 * (i % 2) + 4), slice((i // 2) * P, (i // 2 + 1) * P)

        @block.sync
        def _(sp):
            sp.dma_start(gain_b[:], gain.rearrange("(a d) -> a d", a=1).to_broadcast([P, D])).then_inc(gain_in, 16)

        @block.scalar
        def _(act):
            for t in range(NT):
                if t >= 2:
                    act.wait_ge(squared, t - 1)
                nc.scalar.activation(h[:, t % 2, :], x[:, t, :], ACT.Square,
                                     accum_out=sumsq[:, t:t + 1]).then_inc(squared, 1)
            act.wait_ge(mean_ready, 1)
            nc.scalar.activation(root[:], mean[:], ACT.Sqrt).then_inc(rooted, 1)
            for i in range(2 * NT):
                act.wait_ge(turned, i + 1)
                nc.scalar.copy(hT_hi[part(i)], pT[i % 4][:]).then_inc(hi_ready, 1)

        @block.vector
        def _(dve):
            dve.wait_ge(squared, NT)
            nc.vector.tensor_scalar(mean[:], sumsq[:], 1.0 / D, EPS, ALU.mult, ALU.add).then_inc(mean_ready, 1)
            dve.wait_ge(rooted, 1)
            nc.vector.reciprocal(rstd[:], root[:]).then_inc(rstd_ready, 1)
            dve.wait_ge(rstd_ready, 1)
            dve.wait_ge(gain_in, 16)
            for t in range(NT + 1):
                if t < NT:
                    if t >= 2:
                        dve.wait_ge(turned, 2 * (t - 1))
                    nc.vector.scalar_tensor_tensor(out=h[:, t % 2, :], in0=x[:, t, :], scalar=rstd[:, t:t + 1],
                                                   in1=gain_b[:], op0=ALU.mult, op1=ALU.mult).then_inc(h_ready, 1)
                if t >= 1:
                    for i in (2 * t - 2, 2 * t - 1):
                        dve.wait_ge(hi_ready, i + 1)
                        nc.vector.tensor_tensor(hT_lo[part(i)], pT[i % 4][:], hT_hi[part(i)].bitcast(F32),
                                                ALU.subtract).then_inc(lo_ready, 1)

        @block.tensor
        def _(pe):
            for i in range(2 * NT):
                pe.wait_ge(h_ready, i // 2 + 1)
                if i >= 4:
                    pe.wait_ge(lo_ready, i - 3)
                for k in range(4):
                    kk = 4 * (i % 2) + k
                    mm = nc.tensor.transpose(pT[i % 4][:, k, :], h[:, (i // 2) % 2, kk * P:(kk + 1) * P],
                                             const[:, IDENT, :])
                mm.then_inc(turned, 1)


def ffn(nc, x, hT_hi, hT_lo, w_gate, w_up, w_down, name):
    with Scope(nc, name) as s:
        raw_g, raw_u, raw_d = s.sbuf("raw_g", [P, KD, P]), s.sbuf("raw_u", [P, KD, P]), s.sbuf("raw_d", [P, D])
        g_hi, g_lo, u_hi, u_lo = (s.sbuf(n, [P, 2, KD, P], F32R) for n in ("g_hi", "g_lo", "u_hi", "u_lo"))
        d_hi, d_lo = (s.sbuf(n, [P, 2, D], F32R) for n in ("d_hi", "d_lo"))
        a_hi, a_lo = (s.sbuf(n, [P, 2, TOK], F32R) for n in ("a_hi", "a_lo"))
        silu, prod = s.sbuf("silu", [P, 2, TG]), s.sbuf("prod", [P, 2, TG])
        p_gate = [s.psum(f"p_gate{i}") for i in range(2)]
        p_up = [s.psum(f"p_up{i}") for i in range(2)]
        p_down = [s.psum(f"p_down{i}") for i in range(4)]
        g_in, u_in, d_in = s.sem("g_in"), s.sem("u_in"), s.sem("d_in")
        gu_hi, gu_lo = s.sem("gu_hi"), s.sem("gu_lo")
        dn_hi, dn_lo = s.sem("dn_hi"), s.sem("dn_lo")
        gate_up, silu_done, prod_done, act_hi, act_lo = (
            s.sem(n) for n in ("gate_up", "silu_done", "prod_done", "act_hi", "act_lo"))
        down, added = s.sem("down"), s.sem("added")
        wg, wu = (w.rearrange("(k p) f -> p k f", p=P) for w in (w_gate, w_up))
        NO = 2 * NT
        block = s.block()

        @block.sync
        def _(sp):
            def load(n, q):
                if not known(n, 1):
                    sp.wait_ge(gu_lo, 2 * n - 1)
                sp.dma_start(raw_g[:], wg[:, :, bass.ts(n, P)]).then_inc(g_in, 16)
                if not known(n, 1):
                    sp.wait_ge(gu_lo, 2 * n)
                sp.dma_start(raw_u[:], wu[:, :, bass.ts(n, P)]).then_inc(u_in, 16)
                if not known(n, 1):
                    sp.wait_ge(dn_lo, n)
                sp.dma_start(raw_d[:], w_down[bass.ts(n, P), :]).then_inc(d_in, 16)

            in_steps(sp, load, 0, NF)

        @block.scalar
        def _(act):
            def split_gate_up(n, q):
                if not known(n, 2):
                    act.wait_ge(gate_up, NG * (n - 1))
                act.wait_ge(g_in, 16 * n + 16)
                nc.scalar.copy(g_hi[:, q], raw_g[:]).then_inc(gu_hi, 1)
                act.wait_ge(u_in, 16 * n + 16)
                nc.scalar.copy(u_hi[:, q], raw_u[:]).then_inc(gu_hi, 1)

            def split_down(n, q):
                if not known(n, 2):
                    act.wait_ge(down, NO * (n - 1))
                act.wait_ge(d_in, 16 * n + 16)
                nc.scalar.copy(d_hi[:, q], raw_d[:]).then_inc(dn_hi, 1)

            def step(n, q):
                for g in range(NG):
                    slot = (NG * q + g) % 2
                    act.wait_ge(gate_up, NG * n + g + 1)
                    if not (known(n, 1) and g < 2):
                        act.wait_ge(prod_done, NG * n + g - 1)
                    nc.scalar.activation(silu[:, slot], p_gate[slot][:, 0:TG], ACT.Silu).then_inc(silu_done, 1)
                    act.wait_ge(prod_done, NG * n + g + 1)
                    if g == 0 and not known(n, 2):
                        act.wait_ge(down, NO * (n - 1))
                    nc.scalar.copy(a_hi[:, q, g * TG:(g + 1) * TG], prod[:, slot]).then_inc(act_hi, 1)
                if not known(n, NF) or n + 2 < NF:
                    split_gate_up(n + 2, q)
                if not known(n, NF) or n + 1 < NF:
                    split_down(n + 1, 1 - q)

            split_gate_up(0, 0)
            split_gate_up(1, 1)
            split_down(0, 0)
            in_steps(act, step, 0, NF - 2, lead=2)
            in_steps(act, step, NF - 2, NF)

        @block.vector
        def _(dve):
            def split_gate_up(n, q):
                dve.wait_ge(gu_hi, 2 * n + 1)
                nc.vector.tensor_tensor(g_lo[:, q], raw_g[:], g_hi[:, q].bitcast(F32), ALU.subtract).then_inc(gu_lo, 1)
                dve.wait_ge(gu_hi, 2 * n + 2)
                nc.vector.tensor_tensor(u_lo[:, q], raw_u[:], u_hi[:, q].bitcast(F32), ALU.subtract).then_inc(gu_lo, 1)

            def split_down(n, q):
                dve.wait_ge(dn_hi, n + 1)
                nc.vector.tensor_tensor(d_lo[:, q], raw_d[:], d_hi[:, q].bitcast(F32), ALU.subtract).then_inc(dn_lo, 1)

            def add_down(n, q):
                for o in range(NO):
                    dve.wait_ge(down, NO * n + o + 1)
                    if not known(n, 1):
                        dve.wait_ge(added, NO * (n - 1) + o + 1)
                    xs = x[:, o // 2, (o % 2) * 512:(o % 2) * 512 + 512]
                    nc.vector.scalar_tensor_tensor(out=xs, in0=p_down[(NO * q + o) % 4][:], scalar=0.5, in1=xs,
                                                   op0=ALU.mult, op1=ALU.add).then_inc(added, 1)

            def step(n, q):
                for g in range(NG):
                    slot = (NG * q + g) % 2
                    dve.wait_ge(silu_done, NG * n + g + 1)
                    if not (known(n, 1) and g < 2):
                        dve.wait_ge(act_lo, NG * n + g - 1)
                    nc.vector.tensor_tensor(prod[:, slot], silu[:, slot], p_up[slot][:, 0:TG],
                                            ALU.mult).then_inc(prod_done, 1)
                    dve.wait_ge(act_hi, NG * n + g + 1)
                    mine = slice(g * TG, (g + 1) * TG)
                    nc.vector.tensor_tensor(a_lo[:, q, mine], prod[:, slot], a_hi[:, q, mine].bitcast(F32),
                                            ALU.subtract).then_inc(act_lo, 1)
                if not known(n, 1):
                    add_down(n - 1, 1 - q)
                if not known(n, NF) or n + 2 < NF:
                    split_gate_up(n + 2, q)
                if not known(n, NF) or n + 1 < NF:
                    split_down(n + 1, 1 - q)

            split_gate_up(0, 0)
            split_gate_up(1, 1)
            split_down(0, 0)
            in_steps(dve, step, 0, NF - 2, lead=2)
            in_steps(dve, step, NF - 2, NF)
            add_down(NF - 1, (NF - 1) % 2)

        @block.tensor
        def _(pe):
            def gate_and_up(n, q):
                for g in range(NG):
                    slot, mine = (NG * q + g) % 2, slice(g * TG, (g + 1) * TG)
                    if g == 0:
                        pe.wait_ge(gu_lo, 2 * n + 1)
                    if not (known(n, 1) and g < 2):
                        pe.wait_ge(silu_done, NG * n + g - 1)
                    three_passes(nc, p_gate[slot][:, 0:TG], lambda k: (g_hi[:, q, k, :], g_lo[:, q, k, :]),
                                 lambda k: (hT_hi[:, k, mine], hT_lo[:, k, mine]), range(KD))
                    if g == 0:
                        pe.wait_ge(gu_lo, 2 * n + 2)
                    if not (known(n, 1) and g < 2):
                        pe.wait_ge(prod_done, NG * n + g - 1)
                    three_passes(nc, p_up[slot][:, 0:TG], lambda k: (u_hi[:, q, k, :], u_lo[:, q, k, :]),
                                 lambda k: (hT_hi[:, k, mine], hT_lo[:, k, mine]), range(KD)).then_inc(gate_up, 1)

            def down_proj(n, q):
                pe.wait_ge(dn_lo, n + 1)
                for o in range(NO):
                    tokens, cols = slice(o // 2 * P, (o // 2 + 1) * P), slice(o % 2 * 512, o % 2 * 512 + 512)
                    if o % 6 == 0:
                        pe.wait_ge(act_lo, NG * n + o // 6 + 1)
                    if not (known(n, 1) and o < 4):
                        pe.wait_ge(added, NO * n + o - 3)
                    three_passes(nc, p_down[(NO * q + o) % 4][:], lambda k: (a_hi[:, q, tokens], a_lo[:, q, tokens]),
                                 lambda k: (d_hi[:, q, cols], d_lo[:, q, cols]), [0]).then_inc(down, 1)

            def step(n, q):
                gate_and_up(n, q)
                if not known(n, 1):
                    down_proj(n - 1, 1 - q)

            in_steps(pe, step, 0, NF, lead=2)
            down_proj(NF - 1, (NF - 1) % 2)


def diagonal(flat):
    return flat.rearrange("p (b c) -> p b c", b=BATCH_S)[:, :, 0:SEQ_S]


def project_small(nc, hT_hi, hT_lo, w_in, va, small, new_k, new_v, new_ki, new_ks, new_vs, new_kis):
    with Scope(nc, "ps_") as s:
        raw = s.sbuf("raw", [P, KD, SMALL])
        w_hi, w_lo = s.sbuf("w_hi", [P, KD, SMALL], F32R), s.sbuf("w_lo", [P, KD, SMALL], F32R)
        out = s.sbuf("out", [P, 2, SMALL])
        p_out = [s.psum(f"p_out{i}") for i in range(2)]
        w_raw, w_split_hi, w_split_lo, projected, kept, copied = (
            s.sem(n) for n in ("w_raw", "w_split_hi", "w_split_lo", "projected", "kept", "copied"))
        stored = s.sem("stored0"), s.sem("stored1")
        w = w_in.rearrange("(k p) c -> p k c", p=P)
        block = s.block()
        spans = ((0, C_K, S_KI), (S_KI, C_KI, S_BB - S_KI), (S_BB, C_BB, SMALL - S_BB))

        @block.sync
        def _(sp):
            for at, column, n in spans:
                sp.dma_start(raw[:, :, at:at + n], w[:, :, column:column + n]).then_inc(w_raw, 16)
            for t in range(NT):
                sp.wait_ge(copied, t + 1)
                if t < NTP:
                    rows = slice(t * P, (t + 1) * P)
                    outs = (new_k[0, 0, rows, :, :].rearrange("s n d -> s (n d)"),
                            new_v[0, 0, rows, :, :].rearrange("s n d -> s (n d)"), new_ki[0, 0, rows, :])
                else:
                    outs = (new_ks[0].rearrange("b s n d -> (b s) (n d)"), new_vs[0].rearrange("b s n d -> (b s) (n d)"),
                            new_kis[0].rearrange("b s d -> (b s) d"))
                for dst, cols in zip(outs, (slice(0, S_V), slice(S_V, S_KI), slice(S_KI, S_WI))):
                    sp.dma_start(dst, out[:, t % 2, cols]).then_inc(stored[t % 2], 16)
            for q in range(2):
                sp.wait_ge(stored[q], 48 * ((NT + 1 - q) // 2))

        @block.scalar
        def _(act):
            act.wait_ge(w_raw, 16 * len(spans))
            nc.scalar.copy(w_hi[:], raw[:]).then_inc(w_split_hi, 1)
            for t in range(NT):
                act.wait_ge(projected, t + 1)
                if t >= 2:
                    act.wait_ge(stored[t % 2], 48 * (t // 2))
                    act.wait_ge(kept, t - 1)
                nc.scalar.copy(out[:, t % 2, :], p_out[t % 2][:, 0:SMALL]).then_inc(copied, 1)

        @block.vector
        def _(dve):
            dve.wait_ge(w_split_hi, 1)
            nc.vector.tensor_tensor(w_lo[:], raw[:], w_hi[:].bitcast(F32), ALU.subtract).then_inc(w_split_lo, 1)
            for t in range(NT):
                dve.wait_ge(copied, t + 1)
                nc.vector.tensor_copy(va[:, t, :], out[:, t % 2, S_V:S_KI])
                nc.vector.tensor_copy(small[:, t, :], out[:, t % 2, S_WI:SMALL]).then_inc(kept, 1)

        @block.tensor
        def _(pe):
            pe.wait_ge(w_split_lo, 1)
            for t in range(NT):
                if t >= 2:
                    pe.wait_ge(copied, t - 1)
                tokens = slice(t * P, (t + 1) * P)
                three_passes(nc, p_out[t % 2][:, 0:SMALL], lambda k: (hT_hi[:, k, tokens], hT_lo[:, k, tokens]),
                             lambda k: (w_hi[:, k, :], w_lo[:, k, :]), range(KD)).then_inc(projected, 1)


def project_turned(nc, hT_hi, hT_lo, w_in, qkT, qiT):
    with Scope(nc, "pt_") as s:
        raw = s.sbuf("raw", [P, KD, P])
        w_hi, w_lo = s.sbuf("w_hi", [P, 2, KD, P], F32R), s.sbuf("w_lo", [P, 2, KD, P], F32R)
        p_out = [s.psum(f"p_out{i}") for i in range(2 * NG)]
        w_raw, w_split_hi, w_split_lo, projected, copied, upper_zero = (
            s.sem(n) for n in ("w_raw", "w_split_hi", "w_split_lo", "projected", "copied", "upper_zero"))
        w = w_in.rearrange("(k p) c -> p k c", p=P)
        block = s.block()

        @block.gpsimd
        def _(pool):
            nc.gpsimd.memset(qiT[HD:P, 2, :], 0.0).then_inc(upper_zero, 1)
            pool.wait_ge(upper_zero, 1)
            nc.gpsimd.memset(qiT[0:HD, 3, :], 0.0)

        starts = [(C_Q + HD * j, C_Q + HD * (4 + j)) for j in range(4)]
        starts += [(C_K, C_K + HD), (C_QI, C_QI + HD), (C_QI + 2 * HD, C_QI + 3 * HD), (C_KI, C_KI)]
        NB = len(starts)

        @block.sync
        def _(sp):
            for n, pair in enumerate(starts):
                if n:
                    sp.wait_ge(w_split_lo, n)
                for i, c in enumerate(pair):
                    sp.dma_start(raw[:, :, i * HD:(i + 1) * HD], w[:, :, c:c + HD]).then_inc(w_raw, 16)

        @block.scalar
        def _(act):
            def split(n):
                act.wait_ge(w_raw, 32 * (n + 1))
                if n >= 2:
                    act.wait_ge(projected, NG * (n - 1))
                nc.scalar.copy(w_hi[:, n % 2], raw[:]).then_inc(w_split_hi, 1)

            split(0)
            split(1)
            for n in range(NB):
                for g in range(NG):
                    act.wait_ge(projected, NG * n + g + 1)
                    mine, bank = slice(g * TG, (g + 1) * TG), p_out[NG * (n % 2) + g]
                    if n < NB - 1:
                        dst = qkT[:, n, mine] if n < 5 else qiT[:, n - 5, mine]
                        nc.scalar.copy(dst, bank[:, 0:TG]).then_inc(copied, 1)
                    else:
                        nc.scalar.copy(qiT[0:HD, 2, mine], bank[0:HD, 0:TG])
                        nc.scalar.copy(qiT[HD:P, 3, mine], bank[HD:P, 0:TG]).then_inc(copied, 1)
                if n + 2 < NB:
                    split(n + 2)

        @block.vector
        def _(dve):
            for n in range(NB):
                dve.wait_ge(w_split_hi, n + 1)
                nc.vector.tensor_tensor(w_lo[:, n % 2], raw[:], w_hi[:, n % 2].bitcast(F32),
                                        ALU.subtract).then_inc(w_split_lo, 1)

        @block.tensor
        def _(pe):
            for n in range(NB):
                pe.wait_ge(w_split_lo, n + 1)
                for g in range(NG):
                    if n >= 2:
                        pe.wait_ge(copied, NG * (n - 2) + g + 1)
                    mine = slice(g * TG, (g + 1) * TG)
                    three_passes(nc, p_out[NG * (n % 2) + g][:, 0:TG],
                                 lambda k: (w_hi[:, n % 2, k, :], w_lo[:, n % 2, k, :]),
                                 lambda k: (hT_hi[:, k, mine], hT_lo[:, k, mine]), range(KD)).then_inc(projected, 1)


def score(nc, const, qiT, small, cache_idx_k, scores):
    with Scope(nc, "sc_") as s:
        weight = s.sbuf("weight", [P, NT, IH])
        cache = s.sbuf("cache", [P, 2, 2, P])
        keysT = s.sbuf("keysT", [P, BATCH_S, KEYS_S])
        spread = s.sbuf("spread", [P, 2, BATCH_S * (P + SEQ_S)])
        relu = s.sbuf("relu", [P, 2, 512])
        p_logit = [s.psum(f"p_logit{i}") for i in range(4)]
        p_keys = [s.psum(f"p_keys{i}", (P, 2, PAST)) for i in range(2)]
        names = ("cache_in0", "cache_in1", "weighted", "cleared", "spread_ready", "keys_turned", "keys_ready",
                 "new_keys", "logits", "rectified", "summed", "masked")
        (cache_in0, cache_in1, weighted, cleared, spread_ready, keys_turned, keys_ready, new_keys, logits, rectified,
         summed, masked) = (
            s.sem(n) for n in names)
        cache_in = (cache_in0, cache_in1)
        units = [(t, c, min(512, WIDTH[t] - c), h) for t in range(2, NTP) for c in range(0, WIDTH[t], 512)
                 for h in range(IH)] + [(NTP, 0, KEYS_S, h) for h in range(IH)]
        block = s.block()

        @block.sync
        def _(sp):
            for b in range(BATCH_S):
                if b >= 2:
                    sp.wait_ge(keys_turned, b - 1)
                for i in range(2):
                    sp.dma_start(cache[:, b % 2, :, i * HD:(i + 1) * HD],
                                 cache_idx_k[0, b].rearrange("(c p) d -> p c d", p=P)).then_inc(cache_in[b % 2], 16)

        @block.gpsimd
        def _(pool):
            nc.gpsimd.tensor_scalar(weight[:], small[:, :, 0:IH], 1.0 / 16.0, None, ALU.mult).then_inc(weighted, 1)
            nc.gpsimd.memset(spread[:], 0.0).then_inc(cleared, 1)
            pool.wait_ge(weighted, 1)
            pool.wait_ge(cleared, 1)
            for i in range(2):
                rows = slice(HD * i, HD * i + HD)
                if i:
                    pool.wait_ge(new_keys, i)
                nc.gpsimd.tensor_copy(keysT[rows, :, PAST:KEYS_S], qiT[rows, 2 + i, SEQ:TOK].rearrange(
                    "p (b j) -> p b j", b=BATCH_S)).then_inc(new_keys, 1)
            pool.wait_ge(new_keys, 2)
            for h in range(IH):
                if h:
                    pool.wait_ge(spread_ready, h)
                if h >= 2:
                    pool.wait_ge(logits, len(units) - IH + h - 1)
                rows = slice(HD * (h % 2), HD * (h % 2) + HD)
                nc.gpsimd.tensor_copy(diagonal(spread[rows, h % 2, :]), qiT[rows, h // 2, SEQ:TOK].rearrange(
                    "p (b j) -> p b j", b=BATCH_S)).then_inc(spread_ready, 1)

        @block.scalar
        def _(act):
            for i in range(BATCH_S // 2):
                act.wait_ge(keys_turned, 2 * i + 2)
                nc.scalar.copy(keysT[:, 2 * i:2 * i + 2, 0:PAST], p_keys[i % 2][:]).then_inc(keys_ready, 1)
            for u, (t, c, n, h) in enumerate(units):
                act.wait_ge(logits, u + 1)
                if u >= 2:
                    act.wait_ge(summed, u - 1)
                nc.scalar.activation(relu[:, u % 2, 0:n], p_logit[u % 4][:, 0:n], ACT.Relu).then_inc(rectified, 1)

        @block.vector
        def _(dve):
            nc.vector.memset(scores[:, AT[0]:AT[2]], 0.0).then_inc(masked, 1)
            nc.vector.memset(scores[:, AT[NTP] + KEYS_S:SCORES], FILL)
            dve.wait_ge(masked, 1)
            for t in range(2):
                nc.vector.memset(scores[0:CHUNK, AT[t] + WIDTH[t] - CHUNK:AT[t] + WIDTH[t]], UNSELECTED)
            dve.wait_ge(weighted, 1)
            for u, (t, c, n, h) in enumerate(units):
                dve.wait_ge(rectified, u + 1)
                dst, w = scores[:, AT[t] + c:AT[t] + c + n], weight[:, t, h:h + 1]
                if h == 0:
                    nc.vector.tensor_scalar(dst, relu[:, u % 2, 0:n], w, None, ALU.mult).then_inc(summed, 1)
                else:
                    dve.wait_ge(summed, u)
                    nc.vector.scalar_tensor_tensor(out=dst, in0=relu[:, u % 2, 0:n], scalar=w, in1=dst,
                                                   op0=ALU.mult, op1=ALU.add).then_inc(summed, 1)
            dve.wait_ge(summed, len(units))
            for t in range(2, NTP):
                nc.vector.memset(scores[0:CHUNK, AT[t] + WIDTH[t] - CHUNK:AT[t] + WIDTH[t]], INADMISSIBLE)

        @block.tensor
        def _(pe):
            for b in range(BATCH_S):
                pe.wait_ge(cache_in[b % 2], 32 * (b // 2 + 1))
                if b % 2 == 0 and b >= 4:
                    pe.wait_ge(keys_ready, b // 2 - 1)
                for c in range(2):
                    mm = nc.tensor.transpose(p_keys[(b // 2) % 2][:, b % 2, c * P:(c + 1) * P], cache[:, b % 2, c, :],
                                             const[:, IDENT, :])
                mm.then_inc(keys_turned, 1)
            for u, (t, c, n, h) in enumerate(units):
                if u >= 4:
                    pe.wait_ge(rectified, u - 3)
                if t < NTP:
                    nc.tensor.matmul(p_logit[u % 4][:, 0:n], qiT[:, h // 2, t * P:(t + 1) * P],
                                     qiT[:, 2 + h % 2, c:c + n], start=True, stop=True).then_inc(logits, 1)
                else:
                    pe.wait_ge(spread_ready, h + 1)
                    pe.wait_ge(keys_ready, BATCH_S // 2)
                    pe.wait_ge(new_keys, 2)
                    for b in range(BATCH_S):
                        mm = nc.tensor.matmul(p_logit[u % 4][:, 0:n], spread[:, h % 2, b * P:(b + 1) * P],
                                              keysT[:, b, :], start=(b == 0), stop=(b == BATCH_S - 1))
                    mm.then_inc(logits, 1)


def select_and_project(nc, hT_hi, hT_lo, w_in, scores, projected_d):
    NB = NC + HB + 2 * KD
    with Scope(nc, "sp_") as s:
        raw = s.sbuf("raw", [P, KD, P])
        w_hi, w_lo = s.sbuf("w_hi", [P, 2, KD, P], F32R), s.sbuf("w_lo", [P, 2, KD, P], F32R)
        stage = s.sbuf("stage", [P, 2, TOK])
        best = s.sbuf("best", [P, NT, 8])
        p_out = [s.psum(f"p_out{i}") for i in range(2 * NG)]
        names = ("w_raw", "w_split_hi", "w_split_lo", "projected", "copied", "stored0", "stored1")
        w_raw, w_split_hi, w_split_lo, projected, copied, stored0, stored1 = (
            s.sem(n) for n in names)
        stored = (stored0, stored1)
        w = w_in.rearrange("(k p) c -> p k c", p=P)
        block = s.block()
        first_gate = NC + HB

        @block.sync
        def _(sp):
            def load(n, column):
                if not known(n, 1):
                    sp.wait_ge(w_split_lo, n)
                sp.dma_start(raw[:], w[:, :, bass.ds(column, P)]).then_inc(w_raw, 16)

            in_steps(sp, lambda n, q: load(n, n * P + C_CONV), 0, first_gate)
            in_steps(sp, lambda n, q: load(n, (n - first_gate) * P + C_GATE), first_gate, NB)
            for q in range(2):
                sp.wait_ge(stored[q], 16 * (NB // 2))

        @block.scalar
        def _(act):
            def split(n, q):
                act.wait_ge(w_raw, 16 * n + 16)
                if not known(n, 2):
                    act.wait_ge(projected, NG * (n - 1))
                nc.scalar.copy(w_hi[:, q], raw[:]).then_inc(w_split_hi, 1)

            def step(n, q, func):
                if not known(n, 2):
                    act.wait_ge(stored[q], 8 * (n - q))
                for g in range(NG):
                    act.wait_ge(projected, NG * n + g + 1)
                    nc.scalar.activation(stage[:, q, g * TG:(g + 1) * TG], p_out[NG * q + g][:, 0:TG],
                                         func).then_inc(copied, 1)
                act.wait_ge(copied, NG * n + NG)
                act.dma_start(projected_d[bass.ds(n, 1)].rearrange("a p t -> p (a t)"), stage[:, q]).then_inc(stored[q], 16)
                if not known(n, NB) or n + 2 < NB:
                    split(n + 2, q)

            split(0, 0)
            split(1, 1)
            in_steps(act, lambda n, q: step(n, q, ACT.Copy), 0, NC, lead=2)
            in_steps(act, lambda n, q: step(n, q, ACT.Silu), NC, first_gate, lead=0)
            in_steps(act, lambda n, q: step(n, q, ACT.Sigmoid), first_gate, NB - 2, lead=0)
            in_steps(act, lambda n, q: step(n, q, ACT.Sigmoid), NB - 2, NB)

        @block.gpsimd
        def _(pool):
            def split(n, q):
                pool.wait_ge(w_split_hi, n + 1)
                nc.gpsimd.tensor_tensor(w_lo[:, q], raw[:], w_hi[:, q].bitcast(F32), ALU.subtract).then_inc(w_split_lo, 1)

            in_steps(pool, split, 0, NB)

        @block.vector
        def _(dve):
            def row(t):
                return scores[:, AT[t]:AT[t] + WIDTH[t] + (PAD_S if t == NTP else 0)]

            def find(tiles):
                for t in tiles:
                    nc.vector.max(best[:, t, :], row(t))
                dve.drain()

            def take(tiles):
                for t in tiles:
                    nc.vector.match_replace(row(t), best[:, t, :], row(t), TAKEN)
                dve.drain()

            for tiles in ((2, 3), (4, 5), (6, 7)):
                with dve.Fori(0, TOPK_P // 8):
                    find(tiles)
                    take(tiles)
            with dve.Fori(0, TOPK_S // 8):
                find([NTP])
                take([NTP])
            find([NTP])
            nc.vector.memset(best[:, NTP, TOPK_S % 8:8], FILL)
            dve.drain()
            take([NTP])
            todo = scores[:, AT[2]:SCORES]
            nc.vector.tensor_scalar(todo, todo, TAKEN, UNSELECTED, ALU.not_equal, ALU.mult)

        @block.tensor
        def _(pe):
            def step(n, q):
                pe.wait_ge(w_split_lo, n + 1)
                for g in range(NG):
                    if not known(n, 2):
                        pe.wait_ge(copied, NG * (n - 2) + g + 1)
                    mine = slice(g * TG, (g + 1) * TG)
                    three_passes(nc, p_out[NG * q + g][:, 0:TG], lambda k: (w_hi[:, q, k, :], w_lo[:, q, k, :]),
                                 lambda k: (hT_hi[:, k, mine], hT_lo[:, k, mine]), range(KD)).then_inc(projected, 1)

            in_steps(pe, step, 0, NB, lead=2)


def attend(nc, const, qkT, va, scores, cache_k, cache_v, attended_d):
    with Scope(nc, "at_") as s:
        parts, swapped = s.sbuf("parts", [P, KV, 5, SEQ], F32R), s.sbuf("swapped", [P, KV, SEQ], F32R)
        cache, keysT = s.sbuf("cache", [P, 2, 2, 2, P]), s.sbuf("keysT", [P, BATCH_S, KEYS_S])
        values, own_values = s.sbuf("values", [P, BATCH_S, 2, P]), s.sbuf("own_values", [SEQ_S, BATCH_S, P])
        spread = s.sbuf("spread", [P, BATCH_S, P])
        pick = s.sbuf("pick", [P, BATCH_S, P])
        masked, prob, probT = (s.sbuf(n, [P, 2 * SEQ]) for n in ("masked", "prob", "probT"))
        o_tok, oT = s.sbuf("o_tok", [P, 2, 512]), s.sbuf("oT", [P, 2, 4, P])
        o_dec, oT_dec = s.sbuf("o_dec", [P, 2, HD]), s.sbuf("oT_dec", [HD, HEADS, P])
        top, shift, total, rtotal = (s.sbuf(n, [P, 4]) for n in ("top", "shift", "total", "rtotal"))
        p_s = s.psum("p_s", (P, 2 * SEQ))
        p_pT = [s.psum(f"p_pT{i}", (P, 4, P)) for i in range(2)]
        p_o, p_oT = s.psum("p_o"), s.psum("p_oT", (P, 4, P))
        names = ("cache_in0", "cache_in1", "values_in", "own_in", "cleared", "spread_ready", "picks_ready", "keys_turned",
                 "keys_ready", "new_keys", "split_hi", "split_lo", "scored", "topped", "shifted", "exped", "prob_turned",
                 "probT_ready", "weighed", "inverted", "normed", "o_turned", "oT_ready", "stored0", "stored1", "stored_dec")
        (cache_in0, cache_in1, values_in, own_in, cleared, spread_ready, picks_ready, keys_turned, keys_ready, new_keys, split_hi,
         split_lo, scored, topped, shifted, exped, prob_turned, probT_ready, weighed, inverted, normed, o_turned,
         oT_ready, stored0, stored1, stored_dec) = (s.sem(n) for n in names)
        cache_in, stored = (cache_in0, cache_in1), (stored0, stored1)
        units = [(t, j, kv) for t in range(NTP) for j in range(4) for kv in range(KV)] + [
            (NTP, b, 0) for b in range(BATCH_S)]
        U, DEC = len(units), HEADS * NTP

        def cols(u):
            width = WIDTH[units[u][0]]
            at = (u % 2) * SEQ if width > 512 else (u % 4) * 512
            return at, width

        def same_place(u):
            def place(v):
                at, width = cols(v)
                return set(range(at // 512, (at + width + 511) // 512))
            return max([v + 1 for v in range(u) if place(v) & place(u)], default=0)

        def coming(slot):
            return [v for v in range(U) if max(v - (1 if cols(v)[1] > 512 else 2), -1) == slot]

        groups = [(1 if t == NTP else (WIDTH[t] // P + 3) // 4) for t, _, _ in units]
        before = [sum(groups[:u]) for u in range(U + 1)]
        own, other = (slice(0, HD), slice(HD, P)), (slice(HD, P), slice(0, HD))
        block = s.block()

        @block.sync
        def _(sp):
            for i in range(BATCH_S // 2):
                if i >= 2:
                    sp.wait_ge(keys_turned, i - 1)
                sp.dma_start(cache[:, i % 2], cache_k[0, 2 * i:2 * i + 2].rearrange(
                    "b (c p) n d -> p b c (n d)", p=P)).then_inc(cache_in[i % 2], 16)
            sp.dma_start(values[:], cache_v[0].rearrange("b (c p) n d -> p b c (n d)", p=P)).then_inc(values_in, 16)
            for b in range(BATCH_S):
                sp.dma_start(own_values[:, b, :], va[b * SEQ_S:(b + 1) * SEQ_S, NTP, :]).then_inc(own_in, 16)
            for t in range(NTP):
                sp.wait_ge(oT_ready, t + 1)
                sp.dma_start(attended_d[:, :, t * P:(t + 1) * P].rearrange("j p t -> p j t"), oT[:, t % 2]).then_inc(
                    stored[t % 2], 16)
            sp.wait_ge(oT_ready, NTP + 2)
            for i in range(HEADS):
                sp.dma_start(attended_d[i // 2, (i % 2) * HD:(i % 2 + 1) * HD, SEQ:TOK], oT_dec[:, i, :]).then_inc(
                    stored_dec, 16)
            for q in range(2):
                sp.wait_ge(stored[q], 16 * (NTP // 2))
            sp.wait_ge(stored_dec, 16 * HEADS)

        @block.gpsimd
        def _(pool):
            def split(t):
                mine = slice(t * P, (t + 1) * P)
                for kv in range(KV):
                    pool.wait_ge(split_hi, 2 * t + kv + 1)
                    if t or kv:
                        pool.wait_ge(split_lo, 4 * t + 2 * kv)
                    hi = parts[own[kv], kv, :, mine].bitcast(F32)
                    nc.gpsimd.tensor_tensor(parts[other[kv], kv, :, mine], qkT[own[kv], :, mine], hi,
                                            ALU.subtract).then_inc(split_lo, 1)
                    pool.wait_ge(split_lo, 4 * t + 2 * kv + 1)
                    nc.gpsimd.tensor_tensor(swapped[own[kv], kv, mine], qkT[own[kv], 4, mine],
                                            parts[own[kv], kv, 4, mine].bitcast(F32), ALU.subtract).then_inc(split_lo, 1)

            split(0)
            split(1)
            pool.wait_ge(split_lo, 8)
            nc.gpsimd.memset(spread[:], 0.0).then_inc(cleared, 1)
            pool.wait_ge(cleared, 1)
            for kv in range(KV):
                if kv:
                    pool.wait_ge(spread_ready, kv)
                nc.gpsimd.tensor_copy(
                    spread[own[kv], :, own[kv]].rearrange("p b (j c) -> p b j c", j=4),
                    qkT[own[kv], 0:4, SEQ:TOK].rearrange("p j (b c) -> p b j c", b=BATCH_S)).then_inc(spread_ready, 1)
            pool.wait_ge(spread_ready, KV)
            nc.gpsimd.tensor_copy(keysT[:, :, PAST:KEYS_S], qkT[:, 4, SEQ:TOK].rearrange(
                "p (b c) -> p b c", b=BATCH_S)).then_inc(new_keys, 1)
            nc.gpsimd.tensor_copy(pick[:].rearrange("p b (h c) -> p b h c", h=HEADS), const[:, IDENT, :].rearrange(
                "p (b a c) -> p b a c", b=BATCH_S, a=1).to_broadcast([P, BATCH_S, HEADS, SEQ_S])).then_inc(picks_ready, 1)
            pool.wait_ge(new_keys, 1)
            pool.wait_ge(picks_ready, 1)
            for t in range(2, NTP):
                split(t)

        @block.tensor
        def _(pe):
            def turn_cache(i):
                pe.wait_ge(cache_in[i % 2], 16 * (i // 2 + 1))
                if i:
                    pe.wait_ge(keys_ready, i)
                for k in range(4):
                    mm = nc.tensor.transpose(p_oT[:, k, :], cache[:, i % 2, k // 2, k % 2, :], const[:, IDENT, :])
                mm.then_inc(keys_turned, 1)

            def query_keys(u):
                t, j, kv = units[u]
                at, width = cols(u)
                if same_place(u):
                    pe.wait_ge(topped, same_place(u))
                    if same_place(u) > DEC:
                        pe.wait_ge(exped, same_place(u))
                if t < NTP:
                    pe.wait_ge(split_lo, 4 * t + 4)
                    queries = parts[:, kv, j, t * P:(t + 1) * P]
                    for c in range(0, width, 512):
                        keys = slice(c, min(c + 512, width))
                        out = p_s[:, at + keys.start:at + keys.stop]
                        nc.tensor.matmul(out, queries, parts[:, kv, 4, keys], start=True, stop=False)
                        mm = nc.tensor.matmul(out, queries, swapped[:, kv, keys], start=False, stop=True)
                else:
                    pe.wait_ge(spread_ready, KV)
                    pe.wait_ge(new_keys, 1)
                    pe.wait_ge(keys_ready, BATCH_S // 2)
                    out = p_s[:, at:at + KEYS_S]
                    nc.tensor.matmul(out, spread[:, j, :], keysT[:, j, :], start=True, stop=False)
                    pe.wait_ge(picks_ready, 1)
                    mm = nc.tensor.matmul(out, pick[:, j, :],
                        scores[:, AT[NTP]:AT[NTP] + KEYS_S], start=False, stop=True)
                mm.then_inc(scored, 1)

            def turn(u):
                at, width = cols(u)
                pe.wait_ge(exped, u + 1)
                n = (width + P - 1) // P
                for g in range(groups[u]):
                    if before[u] + g >= 2:
                        pe.wait_ge(probT_ready, before[u] + g - 1)
                    for k in range(4 * g, min(4 * g + 4, n)):
                        rows = min(P, width - k * P)
                        mm = nc.tensor.transpose(p_pT[(before[u] + g) % 2][0:rows, k - 4 * g, :],
                                                 prob[:, at + k * P:at + k * P + rows], const[:, IDENT, :])
                    mm.then_inc(prob_turned, 1)

            def weigh(u):
                t, j, kv = units[u]
                at, width = cols(u)
                pe.wait_ge(probT_ready, before[u + 1])
                if u >= 1:
                    pe.wait_ge(normed, u)
                if t == NTP:
                    pe.wait_ge(values_in, 16)
                    pe.wait_ge(own_in, 16 * BATCH_S)
                n = (width + P - 1) // P
                for k in range(n):
                    rows = min(P, width - k * P)
                    v = va[:, k, :] if t < NTP else values[:, j, k, :] if k < 2 else own_values[:, j, :]
                    mm = nc.tensor.matmul(p_o[:, 0:P], probT[0:rows, at + k * P:at + (k + 1) * P], v, start=(k == 0),
                                          stop=(k == n - 1))
                mm.then_inc(weighed, 1)

            def turn_out(t):
                pe.wait_ge(normed, HEADS * (t + 1))
                if t == 0:
                    pe.wait_ge(keys_ready, BATCH_S // 2)
                else:
                    pe.wait_ge(oT_ready, t)
                for j in range(4):
                    mm = nc.tensor.transpose(p_oT[:, j, :], o_tok[:, t % 2, j * P:(j + 1) * P], const[:, IDENT, :])
                mm.then_inc(o_turned, 1)

            def turn_out_dec(b):
                pe.wait_ge(normed, DEC + b + 1)
                if b % 4 == 0:
                    pe.wait_ge(oT_ready, NTP + b // 4)
                nc.tensor.transpose(p_oT[0:HD, b % 4, :], o_dec[:, b % 2, :], const[:, IDENT, :]).then_inc(o_turned, 1)

            for v in coming(-1):
                query_keys(v)
            for u in range(U):
                for v in coming(u):
                    query_keys(v)
                turn(u)
                if u >= 1:
                    weigh(u - 1)
                if 1 <= u <= BATCH_S // 2:
                    turn_cache(u - 1)
                if u % HEADS == 2 and HEADS < u <= DEC + 2:
                    turn_out(u // HEADS - 1)
                if u >= DEC + 3:
                    turn_out_dec(u - DEC - 3)
            weigh(U - 1)
            for b in range(BATCH_S - 3, BATCH_S):
                turn_out_dec(b)

        @block.vector
        def _(dve):
            def mask_and_top(u):
                t = units[u][0]
                at, width = cols(u)
                q = slice(u % 4, u % 4 + 1)
                dve.wait_ge(scored, u + 1)
                if max(same_place(u), u - 3) > 0:
                    dve.wait_ge(exped, max(same_place(u), u - 3))
                if t < NTP:
                    nc.vector.tensor_tensor_reduce(masked[:, at:at + width], p_s[:, at:at + width],
                                                   scores[:, AT[t]:AT[t] + width], 1.0, -3.4e38, ALU.add, ALU.max,
                                                   top[:, q]).then_inc(topped, 1)
                else:
                    nc.vector.tensor_reduce(top[:, q], p_s[:, at:at + width], AX.X, ALU.max).then_inc(topped, 1)
                dve.wait_ge(topped, u + 1)
                nc.vector.tensor_scalar(shift[:, q], top[:, q], -HD ** -0.5, None, ALU.mult).then_inc(shifted, 1)

            def norm(u):
                t, j, kv = units[u]
                q = slice(u % 4, u % 4 + 1)
                dve.wait_ge(exped, u + 1)
                nc.vector.reciprocal(rtotal[:, q], total[:, q]).then_inc(inverted, 1)
                dve.wait_ge(inverted, u + 1)
                dve.wait_ge(weighed, u + 1)
                if t < NTP:
                    head = j + 4 * kv
                    if u % HEADS == 0 and t >= 2:
                        dve.wait_ge(o_turned, t - 1)
                    nc.vector.tensor_scalar(o_tok[:, t % 2, head * HD:(head + 1) * HD], p_o[:, own[kv]], rtotal[:, q],
                                            None, ALU.mult).then_inc(normed, 1)
                else:
                    if j >= 2:
                        dve.wait_ge(o_turned, NTP + j - 1)
                    for half in own:
                        mul = nc.vector.tensor_scalar(o_dec[half, j % 2, :], p_o[half, half], rtotal[half, q], None,
                                                      ALU.mult)
                    mul.then_inc(normed, 1)

            for v in coming(-1):
                mask_and_top(v)
            for u in range(U):
                for v in coming(u):
                    mask_and_top(v)
                if u >= 1:
                    norm(u - 1)
            norm(U - 1)

        @block.scalar
        def _(act):
            def split(t):
                mine = slice(t * P, (t + 1) * P)
                for kv in range(KV):
                    nc.scalar.copy(swapped[other[kv], kv, mine], qkT[own[kv], 4, mine])
                    nc.scalar.copy(parts[own[kv], kv, :, mine], qkT[own[kv], :, mine]).then_inc(split_hi, 1)

            def exp(u):
                at, width = cols(u)
                q = slice(u % 4, u % 4 + 1)
                act.wait_ge(shifted, u + 1)
                if same_place(u):
                    act.wait_ge(prob_turned, before[same_place(u)])
                if u >= 4:
                    act.wait_ge(inverted, u - 3)
                src = masked if units[u][0] < NTP else p_s
                nc.scalar.activation(prob[:, at:at + width], src[:, at:at + width], ACT.Exp, bias=shift[:, q],
                                     scale=HD ** -0.5, accum_out=total[:, q]).then_inc(exped, 1)

            def keep_turned(u):
                at, width = cols(u)
                if same_place(u):
                    act.wait_ge(weighed, same_place(u))
                for g in range(groups[u]):
                    act.wait_ge(prob_turned, before[u] + g + 1)
                    bank = p_pT[(before[u] + g) % 2]
                    full = min(4, width // P - 4 * g)
                    first = at + 4 * g * P
                    if units[u][0] < NTP:
                        nc.scalar.copy(probT[:, first:first + full * P].rearrange("p (k q) -> p k q", k=full),
                                       bank[:, 0:full, :]).then_inc(probT_ready, 1)
                    else:
                        nc.scalar.copy(probT[:, first:first + full * P].rearrange("p (k q) -> p k q", k=full),
                                       bank[:, 0:full, :])
                        nc.scalar.copy(probT[0:SEQ_S, first + full * P:first + (full + 1) * P],
                                       bank[0:SEQ_S, full, :]).then_inc(probT_ready, 1)

            def keep_out(t):
                act.wait_ge(o_turned, t + 1)
                if t >= 2:
                    act.wait_ge(stored[t % 2], 16 * (t // 2))
                nc.scalar.copy(oT[:, t % 2], p_oT[:]).then_inc(oT_ready, 1)

            def keep_out_dec(i):
                act.wait_ge(o_turned, NTP + 4 * i + 4)
                nc.scalar.copy(oT_dec[:, :, 4 * i * SEQ_S:4 * (i + 1) * SEQ_S].rearrange("p h (b c) -> p b h c", b=4),
                               p_oT[0:HD].rearrange("p b (h c) -> p b h c", h=HEADS)).then_inc(oT_ready, 1)

            split(0)
            split(1)
            exp(0)
            for u in range(U):
                if u + 1 < U:
                    exp(u + 1)
                keep_turned(u)
                if 1 <= u <= BATCH_S // 2:
                    act.wait_ge(keys_turned, u)
                    nc.scalar.copy(keysT[:, 2 * u - 2:2 * u, 0:PAST].rearrange("p b (c s) -> p b c s", c=2),
                                   p_oT[:].rearrange("p (b c) s -> p b c s", b=2)).then_inc(keys_ready, 1)
                if u % HEADS == 0 and 2 <= u // HEADS + 2 < NTP:
                    split(u // HEADS + 2)
                if u % HEADS == 3 and HEADS < u <= DEC + 3:
                    keep_out(u // HEADS - 1)
                if u == DEC + 7:
                    keep_out_dec(0)
            keep_out_dec(1)


def convolve(nc, const, conv_w, state_conv, projected_d, conv_d, inv_norm, new_conv, new_conv_s):
    HIST = CONV_W - 1
    RUN_S = HIST + SEQ_S
    PAD = HIST + SEQ
    with Scope(nc, "cv_") as s:
        padded = s.sbuf("padded", [P, 2, PAD + BATCH_S * RUN_S])
        decode = s.sbuf("decode", [P, 2, P])
        acc, out, square = s.sbuf("acc", [P, 2, TOK]), s.sbuf("out", [P, 2, TOK]), s.sbuf("square", [P, 2, TOK])
        taps_in, state_in = s.sbuf("taps_in", [CONV_W * NC, P]), s.sbuf("state_in", [BATCH_S * HIST, CONV_CH])
        taps, state = s.sbuf("taps", [P, CONV_W, NC]), s.sbuf("state", [P, NC, BATCH_S * HIST])
        tail = s.sbuf("tail", [P, NC, HIST * (1 + BATCH_S)])
        tail_tok = s.sbuf("tail_tok", [HIST * (1 + BATCH_S), CONV_CH])
        mean, root = s.sbuf("mean", [P, NT, 2 * HB]), s.sbuf("root", [P, NT, 2 * HB])
        p_taps, p_state, p_sum = s.psum("p_taps"), s.psum("p_state"), s.psum("p_sum")
        p_tail = [s.psum(f"p_tail{i}") for i in range(3)]
        names = ("small_in", "small_turned", "small_ready", "raw_in0", "raw_in1", "cleared", "filled", "tailed", "conv_done",
                 "silu_done", "squared", "summed", "mean_ready", "rooted", "stored0", "stored1", "tail_turned", "tail_ready",
                 "tail_stored", "scaled")
        (small_in, small_turned, small_ready, raw_in0, raw_in1, cleared, filled, tailed, conv_done, silu_done, squared,
         summed, mean_ready, rooted, stored0, stored1, tail_turned, tail_ready, tail_stored, scaled) = (
            s.sem(n) for n in names)
        raw_in, stored = (raw_in0, raw_in1), (stored0, stored1)
        TAPS = CONV_W * 2
        block = s.block()

        def decode_part(n):
            return padded[:, n % 2, PAD:].rearrange("p (b c) -> p b c", b=BATCH_S)

        @block.sync
        def _(sp):
            sp.dma_start(taps_in[:], conv_w.rearrange("j (n p) -> (j n) p", p=P)).then_inc(small_in, 16)
            sp.dma_start(state_in[:], state_conv[0].rearrange("b j c -> (b j) c")).then_inc(small_in, 16)
            for n in range(NC):
                if n >= 2:
                    sp.wait_ge(conv_done, TAPS * (n - 1))
                    sp.wait_ge(tailed, n - 1)
                sp.dma_start(padded[:, n % 2, HIST:PAD], projected_d[n, :, 0:SEQ]).then_inc(raw_in[n % 2], 16)
                sp.dma_start(decode[:, n % 2], projected_d[n, :, SEQ:TOK]).then_inc(raw_in[n % 2], 16)
            sp.wait_ge(tail_ready, 3)
            sp.dma_start(new_conv[0, 0], tail_tok[0:HIST, :]).then_inc(tail_stored, 16)
            sp.dma_start(new_conv_s[0].rearrange("b j c -> (b j) c"), tail_tok[HIST:, :]).then_inc(tail_stored, 16)
            sp.wait_ge(tail_stored, 32)

        @block.gpsimd
        def _(pool):
            nc.gpsimd.memset(padded[:, :, 0:HIST], 0.0).then_inc(cleared, 1)
            pool.wait_ge(small_ready, 2)
            for n in range(NC):
                pool.wait_ge(raw_in[n % 2], 32 * (n // 2 + 1))
                dst = decode_part(n)
                nc.gpsimd.tensor_copy(dst[:, :, 0:HIST], state[:, n, :].rearrange("p (b j) -> p b j", b=BATCH_S))
                nc.gpsimd.tensor_copy(dst[:, :, HIST:RUN_S], decode[:, n % 2].rearrange(
                    "p (b c) -> p b c", b=BATCH_S)).then_inc(filled, 1)
                pool.wait_ge(filled, n + 1)
                nc.gpsimd.tensor_copy(tail[:, n, 0:HIST], padded[:, n % 2, PAD - HIST:PAD])
                nc.gpsimd.tensor_copy(tail[:, n, HIST:].rearrange("p (b j) -> p b j", b=BATCH_S),
                                      dst[:, :, SEQ_S:RUN_S]).then_inc(tailed, 1)

        @block.vector
        def _(dve):
            dve.wait_ge(small_turned, 2)
            nc.vector.tensor_copy(taps[:], p_taps[:, 0:CONV_W * NC].rearrange("p (j n) -> p j n", n=NC)).then_inc(
                small_ready, 1)
            nc.vector.tensor_copy(state[:], p_state[:, 0:NC * BATCH_S * HIST].rearrange(
                "p (n c) -> p n c", n=NC)).then_inc(small_ready, 1)
            dve.wait_ge(small_ready, 2)
            dve.wait_ge(cleared, 1)
            done = 0
            for n in range(NC):
                dve.wait_ge(filled, n + 1)
                if n >= 2:
                    dve.wait_ge(silu_done, n - 1)
                for j in range(CONV_W):
                    w = taps[:, j, n:n + 1]
                    pairs = ((acc[:, n % 2, 0:SEQ], padded[:, n % 2, j:j + SEQ]),
                             (acc[:, n % 2, SEQ:TOK].rearrange("p (b c) -> p b c", b=BATCH_S),
                              decode_part(n)[:, :, j:j + SEQ_S]))
                    for dst, src in pairs:
                        if j == 0:
                            nc.vector.tensor_scalar(dst, src, w, None, ALU.mult).then_inc(conv_done, 1)
                        else:
                            dve.wait_ge(conv_done, done - 1)
                            nc.vector.scalar_tensor_tensor(out=dst, in0=src, scalar=w, in1=dst, op0=ALU.mult,
                                                           op1=ALU.add).then_inc(conv_done, 1)
                        done += 1
            for i in range(3):
                dve.wait_ge(tail_turned, i + 1)
                nc.vector.tensor_copy(tail_tok[:, i * 512:(i + 1) * 512], p_tail[i][0:HIST * (1 + BATCH_S), :]).then_inc(
                    tail_ready, 1)
            dve.wait_ge(summed, 2 * HB)
            nc.vector.tensor_scalar(mean[:], p_sum[:, 0:NT * 2 * HB].rearrange("p (n t) -> p t n", t=NT), EPS, None,
                                    ALU.add).then_inc(mean_ready, 1)
            dve.wait_ge(rooted, 1)
            nc.vector.reciprocal(inv_norm[:], root[:]).then_inc(scaled, 1)
            dve.wait_ge(scaled, 1)
            nc.vector.tensor_scalar(inv_norm[:, :, 0:HB], inv_norm[:, :, 0:HB], DK ** -0.5, None, ALU.mult)

        @block.scalar
        def _(act):
            for n in range(NC):
                act.wait_ge(conv_done, TAPS * (n + 1))
                if n >= 2:
                    act.wait_ge(stored[n % 2], 16 * (n // 2))
                nc.scalar.activation(out[:, n % 2], acc[:, n % 2], ACT.Silu).then_inc(silu_done, 1)
                act.wait_ge(silu_done, n + 1)
                if n < 2 * HB:
                    if n >= 2:
                        act.wait_ge(summed, n - 1)
                    nc.scalar.activation(square[:, n % 2], out[:, n % 2], ACT.Square).then_inc(squared, 1)
                act.dma_start(conv_d[n], out[:, n % 2]).then_inc(stored[n % 2], 16)
            act.wait_ge(mean_ready, 1)
            nc.scalar.activation(root[:], mean[:], ACT.Sqrt).then_inc(rooted, 1)
            for q in range(2):
                act.wait_ge(stored[q], 16 * (NC // 2))

        @block.tensor
        def _(pe):
            pe.wait_ge(small_in, 32)
            nc.tensor.transpose(p_taps[:, 0:CONV_W * NC], taps_in[:], const[0:CONV_W * NC, IDENT, 0:CONV_W * NC]).then_inc(
                small_turned, 1)
            H = BATCH_S * HIST
            for n in range(NC):
                mm = nc.tensor.transpose(p_state[:, n * H:(n + 1) * H], state_in[:, n * P:(n + 1) * P],
                                         const[0:H, IDENT, 0:H])
            mm.then_inc(small_turned, 1)
            for n in range(2 * HB):
                pe.wait_ge(squared, n + 1)
                for t in range(NT):
                    mm = nc.tensor.matmul(p_sum[:, n * NT + t:n * NT + t + 1], square[:, n % 2, t * P:(t + 1) * P],
                                          const[:, ONES, 0:1], start=True, stop=True)
                mm.then_inc(summed, 1)
            pe.wait_ge(tailed, NC)
            for i in range(3):
                for n in range(4):
                    mm = nc.tensor.transpose(p_tail[i][0:HIST * (1 + BATCH_S), n * P:(n + 1) * P], tail[:, 4 * i + n, :],
                                             const[:, IDENT, :])
                mm.then_inc(tail_turned, 1)


def decays(nc, const, small, a_log, dt_bias, beta, g, cum, c_key, c_last, last_p, last_s):
    with Scope(nc, "dc_") as s:
        bias, rate = s.sbuf("bias", [P, HB]), s.sbuf("rate", [P, HB])
        a, absa, e, ln = (s.sbuf(n, [P, NT, HB]) for n in ("a", "absa", "e", "ln"))
        g_of = s.sbuf("g_of", [P, HB, BATCH_S])
        e_cum, diff = s.sbuf("e_cum", [P, NT, HB]), s.sbuf("diff", [P, NT, HB])
        p_cum, p_last, p_last_s = s.psum("p_cum"), s.psum("p_last"), s.psum("p_last_s")
        param_in, done_v, done_a, done_p = (s.sem(n) for n in ("param_in", "done_v", "done_a", "done_p"))
        NP = NTP * HB
        block = s.block()

        @block.sync
        def _(sp):
            sp.dma_start(bias[:], dt_bias.to_broadcast([P, HB])).then_inc(param_in, 16)
            sp.dma_start(rate[:], a_log.to_broadcast([P, HB])).then_inc(param_in, 16)

        @block.vector
        def _(dve):
            count = [0]

            def then(ins):
                count[0] += 1
                ins.then_inc(done_v, 1)
                dve.wait_ge(done_v, count[0])

            dve.wait_ge(param_in, 32)
            then(nc.vector.tensor_tensor(a[:], small[:, :, 8:12], bias[:].rearrange("p (a h) -> p a h", a=1).to_broadcast(
                [P, NT, HB]), ALU.add))
            then(nc.vector.scalar_tensor_tensor(out=absa[:], in0=a[:], scalar=-1.0, in1=a[:], op0=ALU.mult, op1=ALU.max))
            dve.wait_ge(done_a, 2)
            then(nc.vector.tensor_scalar(e[:], e[:], 1.0, None, ALU.add))
            then(nc.vector.tensor_scalar(a[:], a[:], 0.0, None, ALU.max))
            dve.wait_ge(done_a, 3)
            then(nc.vector.tensor_tensor(a[:], a[:], ln[:], ALU.add))
            then(nc.vector.tensor_scalar(rate[:], rate[:], -1.0, None, ALU.mult))
            then(nc.vector.tensor_tensor(g[:], a[:], rate[:].rearrange("p (a h) -> p a h", a=1).to_broadcast(
                [P, NT, HB]), ALU.mult))
            then(nc.vector.tensor_tensor(g_of[:], g[:, NTP, :].rearrange("p (h a) -> p h a", a=1).to_broadcast(
                [P, HB, BATCH_S]), const[:, BATCH_OF, 0:BATCH_S].rearrange("p (a b) -> p a b", a=1).to_broadcast(
                [P, HB, BATCH_S]), ALU.mult))
            dve.wait_ge(done_p, 1)
            then(nc.vector.tensor_copy(cum[:], p_cum[:, 0:NT * HB].rearrange("p (t h) -> p t h", h=HB)))
            then(nc.vector.tensor_tensor(diff[:], p_last[:, 0:NT * HB].rearrange("p (t h) -> p t h", h=HB), cum[:],
                                         ALU.subtract))
            dve.wait_ge(done_a, 5)
            nc.vector.scalar_tensor_tensor(out=c_key[:], in0=beta[:], scalar=-1.0, in1=e_cum[:], op0=ALU.mult,
                                           op1=ALU.mult)

        @block.scalar
        def _(act):
            act.wait_ge(param_in, 32)
            act.wait_ge(done_v, 2)
            nc.scalar.activation(e[:], absa[:], ACT.Exp, scale=-1.0).then_inc(done_a, 1)
            nc.scalar.activation(rate[:], rate[:], ACT.Exp).then_inc(done_a, 1)
            act.wait_ge(done_v, 3)
            nc.scalar.activation(ln[:], e[:], ACT.Ln).then_inc(done_a, 1)
            act.wait_ge(done_v, 9)
            nc.scalar.activation(e_cum[:], cum[:], ACT.Exp).then_inc(done_a, 1)
            act.wait_ge(done_v, 10)
            nc.scalar.activation(c_last[:], diff[:], ACT.Exp)
            nc.scalar.activation(last_p[:], p_last[:, 0:NP].rearrange("p (t h) -> p t h", h=HB), ACT.Exp)
            nc.scalar.activation(last_s[:], p_last_s[:, 0:HB * BATCH_S].rearrange("p (h b) -> p h b", h=HB), ACT.Exp)
            nc.scalar.activation(beta[:], small[:, :, 4:8], ACT.Sigmoid).then_inc(done_a, 1)

        @block.tensor
        def _(pe):
            pe.wait_ge(done_v, 8)
            prompt, own = g[:, 0:NTP, :].rearrange("p t h -> p (t h)"), g[:, NTP, :]
            nc.tensor.matmul(p_cum[:, 0:NP], const[:, UPTO, :], prompt, start=True, stop=True)
            nc.tensor.matmul(p_cum[:, NP:NP + HB], const[:, UPTO_S, :], own, start=True, stop=True)
            nc.tensor.matmul(p_last[:, 0:NP], const[:, ONES, :], prompt, start=True, stop=True)
            nc.tensor.matmul(p_last[:, NP:NP + HB], const[:, SAME_S, :], own, start=True, stop=True)
            nc.tensor.matmul(p_last_s[:, 0:HB * BATCH_S], const[:, ONES, :], g_of[:].rearrange("p h b -> p (h b)"),
                             start=True, stop=True).then_inc(done_p, 1)


def over_heads(ap, n=P):
    return ap.rearrange("p (h a) -> p h a", a=1).to_broadcast([P, ap.shape[-1], n])


def for_heads(ap, n):
    return ap.rearrange("p (a c) -> p a c", a=1).to_broadcast([P, n, ap.shape[-1]])


def delta(nc, const, beta, g, cum, c_key, c_last, last_p, last_s, inv_norm, conv_d, state_delta, out_d,
          new_state, new_state_s):
    with Scope(nc, "dl_") as s:
        H2 = HB // 2
        qkv = s.sbuf("qkv", [P, 2, NC, P])
        pair = [P, 2, H2, P]
        khat, qhat, kT, qT, e_row, gap, E_up, E_low, low, X, Z, g_cols = (s.sbuf(n, pair) for n in (
            "khat", "qhat", "kT", "qT", "e_row", "gap", "E_up", "E_low", "low", "X", "Z", "g_cols"))
        below = s.sbuf("below", [P, LEVELS_P, 2, H2, P])
        vb, kbg, kdec, qTe, attn, Y, wT = (s.sbuf(n, [P, 2, 2, H2, P]) for n in (
            "vb", "kbg", "kdec", "qTe", "attn", "Y", "wT"))
        V, S = s.sbuf("V", [P, HB, P]), s.sbuf("S", [P, HB, P])
        outT = s.sbuf("outT", [P, 2, HB, P])
        S_s = s.sbuf("S_s", [P, BATCH_S, HB, P])
        VT, V_of = s.sbuf("VT", [P, HB, P]), s.sbuf("V_of", [P, 2, BATCH_S, P])
        S_new = s.sbuf("S_new", [P, 2, BATCH_S, P])
        bank = [[s.psum(f"p_{p}{i}") for i in range(3)] for p in range(2)]
        p_v, p_o = s.psum("p_v"), s.psum("p_o")

        def sems(names):
            return {n: [s.sem(f"{n}{p}") for p in range(2)] for n in names.split()}

        sm = sems("turned hats scaled hats_turned gap_ready clamped rows_kept e_done grams low_ready attn_ready "
                  "attn_masked low_scaled x0 b0_turned w_done w_kept b_first b_all q_scaled g_spread qkv_in out_stored")
        lv = sems("z_done z_kept y_done y_kept x_done x_kept")
        v_done, v_kept, o_done, o_kept, s_done, s_kept, cleared, final_stored = (s.sem(n) for n in (
            "v_done", "v_kept", "o_done", "o_kept", "s_done", "s_kept", "cleared", "final_stored"))
        state_in, vt_done, vt_kept, v_spread, ss_done, ss_kept = (s.sem(n) for n in (
            "state_in", "vt_done", "vt_kept", "v_spread", "ss_done", "ss_kept"))
        new_stored = [s.sem("new_stored0"), s.sem("new_stored1")]
        LP, LS = LEVELS_P, LEVELS_S
        block = s.block()

        def view(b):
            return b[:, 0:H2 * P].rearrange("p (h c) -> p h c", h=H2)

        @block.sync
        def _(sp):
            def load(n, q):
                if not known(n, 2):
                    for p in range(2):
                        sp.wait_ge(sm["turned"][p], n - 1)
                sp.dma_start(qkv[:, q], conv_d[:, :, bass.ts(n, P)].rearrange("n p t -> p n t")).then_inc(
                    sm["qkv_in"][q], 16)

            def store(n, q):
                sp.wait_ge(o_kept, n + 1)
                sp.dma_start(out_d[:, :, bass.ts(n, P)].rearrange("n p t -> p n t"), outT[:, q]).then_inc(
                    sm["out_stored"][q], 16)

            load(0, 0)
            sp.dma_start(S_s[:], state_delta[0].rearrange("b h k v -> k b h v")).then_inc(state_in, 16)

            def step(n, q):
                load(n, q)
                store(n - 1, 1 - q)

            in_steps(sp, step, 1, NTP)
            load(NTP, 0)
            store(NTP - 1, 1)
            sp.wait_ge(s_kept, NTP)
            sp.dma_start(new_state[0, 0].rearrange("h k v -> k h v"), S[:]).then_inc(final_stored, 16)
            store(NTP, 0)
            for h in range(HB):
                sp.wait_ge(ss_kept, 2 * (h + 1))
                sp.dma_start(new_state_s[0, :, h].rearrange("b k v -> k b v"), S_new[:, h % 2]).then_inc(
                    new_stored[h % 2], 16)
            sp.wait_ge(final_stored, 16)
            for q in range(2):
                sp.wait_ge(new_stored[q], 32)
                sp.wait_ge(sm["out_stored"][q], 16 * ((NT + 1 - q) // 2))

        @block.tensor
        def _(pe):
            ident = const[:, IDENT, :]

            def front(n, q, decode):
                for p in range(2):
                    if not known(n, 1):
                        pe.wait_ge(lv["y_kept"][p], LP * n)
                        pe.wait_ge(sm["w_kept"][p], n)
                    pe.wait_ge(sm["qkv_in"][q], 8 * (n - q) + 16)
                    for i, at in enumerate((HB, 0, 2 * HB)):
                        for h in range(H2):
                            mm = nc.tensor.transpose(bank[p][i][:, h * P:(h + 1) * P], qkv[:, q, at + H2 * p + h, :], ident)
                    mm.then_inc(sm["turned"][p], 1)
                for p in range(2):
                    pe.wait_ge(sm["hats"][p], n + 1)
                    pe.wait_ge(sm["g_spread"][p], n + 1)
                    for h in range(H2):
                        cols = slice(h * P, (h + 1) * P)
                        nc.tensor.transpose(bank[p][0][:, cols], khat[:, p, h, :], ident)
                        nc.tensor.transpose(bank[p][1][:, cols], qhat[:, p, h, :], ident)
                        mm = nc.tensor.matmul(bank[p][2][:, cols], g_cols[:, p, h, :],
                                              const[:, UPTO_S if decode else UPTO, :], start=True, stop=True)
                    mm.then_inc(sm["hats_turned"][p], 1)
                for p in range(2):
                    pe.wait_ge(sm["rows_kept"][p], n + 1)
                    for h in range(H2):
                        cols = slice(h * P, (h + 1) * P)
                        nc.tensor.matmul(bank[p][0][:, cols], kT[:, p, h, :], kT[:, p, h, :], start=True, stop=True)
                        mm = nc.tensor.matmul(bank[p][1][:, cols], kT[:, p, h, :], qT[:, p, h, :], start=True, stop=True)
                    mm.then_inc(sm["grams"][p], 1)
                for p in range(2):
                    pe.wait_ge(sm["b_first"][p], n + 1)
                    pe.wait_ge(sm["e_done"][p], n + 1)
                    for h in range(H2):
                        mm = nc.tensor.transpose(bank[p][2][:, h * P:(h + 1) * P], below[:, 0, p, h, :], ident)
                    mm.then_inc(sm["b0_turned"][p], 1)

            def level(n, q, i, last, between=None):
                for p in range(2):
                    pe.wait_ge(lv["y_kept"][p], LP * n + i)
                    if i == 1:
                        pe.wait_ge(sm["b_all"][p], n + 1)
                        pe.wait_ge(sm["low_ready"][p], n + 1)
                    for h in range(H2):
                        mm = nc.tensor.matmul(bank[p][0][:, h * P:(h + 1) * P], below[:, i, p, h, :], Y[:, q, p, h, :],
                                              start=True, stop=True)
                    mm.then_inc(lv["z_done"][p], 1)
                if between is not None:
                    between()
                for p in range(2):
                    pe.wait_ge(lv["z_kept"][p], (LP - 1) * n + i)
                    if i == 1:
                        pe.wait_ge(sm["x0"][p], n + 1)
                        pe.wait_ge(sm["attn_ready"][p], n + 1)
                    else:
                        pe.wait_ge(lv["x_kept"][p], (LP - 2) * n + i - 1)
                    for h in range(H2):
                        mm = nc.tensor.matmul(bank[p][1][:, h * P:(h + 1) * P], X[:, p, h, :], Z[:, p, h, :],
                                              start=True, stop=True)
                    mm.then_inc(lv["y_done"][p], 1)
                    if not last:
                        for h in range(H2):
                            mm = nc.tensor.matmul(bank[p][2][:, h * P:(h + 1) * P], Z[:, p, h, :], X[:, p, h, :],
                                                  start=True, stop=True)
                        mm.then_inc(lv["x_done"][p], 1)

            def weights(n, q, levels):
                for p in range(2):
                    pe.wait_ge(lv["y_kept"][p], LP * n + levels)
                    pe.wait_ge(sm["scaled"][p], n + 1)
                    for h in range(H2):
                        mm = nc.tensor.matmul(bank[p][0][:, h * P:(h + 1) * P], kbg[:, q, p, h, :], Y[:, q, p, h, :],
                                              start=True, stop=True)
                    mm.then_inc(sm["w_done"][p], 1)

            def new_values(n, q):
                for p in range(2):
                    pe.wait_ge(sm["w_kept"][p], n + 1)
                if known(n, 1):
                    pe.wait_ge(cleared, 1)
                else:
                    pe.wait_ge(s_kept, n)
                for h in range(HB):
                    out = p_v[:, h * P:(h + 1) * P]
                    nc.tensor.matmul(out, Y[:, q, h // 2, h % 2, :], vb[:, q, h // 2, h % 2, :], start=True, stop=False)
                    mm = nc.tensor.matmul(out, wT[:, q, h // 2, h % 2, :], S[:, h, :], start=False, stop=True)
                mm.then_inc(v_done, 1)

            def outputs_and_state(n, q):
                pe.wait_ge(v_kept, n + 1)
                if not known(n, 1):
                    pe.wait_ge(o_kept, n)
                for p in range(2):
                    pe.wait_ge(sm["q_scaled"][p], n + 1)
                    pe.wait_ge(sm["attn_masked"][p], n + 1)
                for h in range(HB):
                    out = p_o[:, h * P:(h + 1) * P]
                    nc.tensor.matmul(out, S[:, h, :], qTe[:, q, h // 2, h % 2, :], start=True, stop=False)
                    mm = nc.tensor.matmul(out, V[:, h, :], attn[:, q, h // 2, h % 2, :], start=False, stop=True)
                mm.then_inc(o_done, 1)
                for h in range(HB):
                    mm = nc.tensor.matmul(p_v[:, h * P:(h + 1) * P], kdec[:, q, h // 2, h % 2, :], V[:, h, :],
                                          start=True, stop=True)
                mm.then_inc(s_done, 1)

            def step(n, q, decode=False):
                levels = LS if decode else LP
                front(n, q, decode)
                level(n, q, 1, False, None if known(n, 1) else lambda: new_values(n - 1, 1 - q))
                level(n, q, 2, False, None if known(n, 1) else lambda: outputs_and_state(n - 1, 1 - q))
                for i in range(3, levels):
                    level(n, q, i, i == levels - 1)
                weights(n, q, levels)

            in_steps(pe, step, 0, NTP)
            step(NTP, 0, True)
            for p in range(2):
                pe.wait_ge(sm["w_kept"][p], NT)
                pe.wait_ge(sm["q_scaled"][p], NT)
                pe.wait_ge(sm["attn_masked"][p], NT)
            pe.wait_ge(s_kept, NTP)
            pe.wait_ge(state_in, 16)
            for h in range(HB):
                nc.tensor.matmul(p_v[:, h * P:(h + 1) * P], vb[:, 0, h // 2, h % 2, :], Y[:, 0, h // 2, h % 2, :],
                                 start=True, stop=False)
                for b in range(BATCH_S):
                    mine = slice(b * SEQ_S, (b + 1) * SEQ_S)
                    mm = nc.tensor.matmul(p_v[:, h * P + b * SEQ_S:h * P + (b + 1) * SEQ_S], S_s[:, b, h, :],
                                          wT[:, 0, h // 2, h % 2, mine], start=False, stop=(b == BATCH_S - 1))
            mm.then_inc(vt_done, 1)
            pe.wait_ge(vt_kept, 1)
            for h in range(HB):
                mm = nc.tensor.transpose(p_v[:, h * P:(h + 1) * P], VT[:, h, :], ident)
            mm.then_inc(v_done, 1)
            pe.wait_ge(v_kept, NT)
            pe.wait_ge(o_kept, NTP)
            for h in range(HB):
                nc.tensor.matmul(p_o[:, h * P:(h + 1) * P], V[:, h, :], attn[:, 0, h // 2, h % 2, :], start=True, stop=False)
                for b in range(BATCH_S):
                    mine = slice(b * SEQ_S, (b + 1) * SEQ_S)
                    mm = nc.tensor.matmul(p_o[:, h * P + b * SEQ_S:h * P + (b + 1) * SEQ_S], S_s[:, b, h, :],
                                          qTe[:, 0, h // 2, h % 2, mine], start=False, stop=(b == BATCH_S - 1))
            mm.then_inc(o_done, 1)
            for h in range(HB):
                pe.wait_ge(v_spread, h + 1)
                for c in range(2):
                    if h >= 1:
                        pe.wait_ge(ss_kept, 2 * (h - 1) + c + 1)
                    nc.tensor.matmul(bank[c][1][:], kdec[:, 0, h // 2, h % 2, :],
                                     V_of[:, h % 2, 4 * c:4 * c + 4, :].rearrange("p b v -> p (b v)"),
                                     start=True, stop=True).then_inc(ss_done, 1)

        @block.vector
        def _(dve):
            def heads(p, at=0):
                return slice(at + H2 * p, at + H2 * p + H2)

            def front(n, q, decode):
                for p in range(2):
                    dve.wait_ge(sm["turned"][p], n + 1)
                    if not known(n, 2):
                        dve.wait_ge(s_done, n - 1)
                    if not known(n, 1):
                        dve.wait_ge(sm["scaled"][p], n)
                    nc.vector.tensor_tensor(khat[:, p], view(bank[p][0]), over_heads(inv_norm[:, n, heads(p, HB)]), ALU.mult)
                    nc.vector.tensor_tensor(qhat[:, p], view(bank[p][1]), over_heads(inv_norm[:, n, heads(p)]), ALU.mult)
                    nc.vector.tensor_tensor(vb[:, q, p], view(bank[p][2]), over_heads(beta[:, n, heads(p)]),
                                            ALU.mult).then_inc(sm["hats"][p], 1)
                for p in range(2):
                    dve.wait_ge(sm["hats_turned"][p], n + 1)
                    nc.vector.tensor_tensor(gap[:, p], view(bank[p][2]), over_heads(cum[:, n, heads(p)]),
                                            ALU.subtract).then_inc(sm["gap_ready"][p], 1)
                    dve.wait_ge(sm["gap_ready"][p], n + 1)
                    if not known(n, 1):
                        dve.wait_ge(sm["low_ready"][p], n)
                    nc.vector.tensor_scalar(E_up[:, p], gap[:, p], 0.0, None, ALU.min)
                    nc.vector.tensor_scalar(E_low[:, p], gap[:, p], -1.0, 0.0, ALU.mult, ALU.min).then_inc(
                        sm["clamped"][p], 1)
                for p in range(2):
                    dve.wait_ge(sm["grams"][p], n + 1)
                    dve.wait_ge(sm["e_done"][p], n + 1)
                    if not known(n, 1):
                        dve.wait_ge(sm["b_all"][p], n)
                    nc.vector.tensor_tensor(low[:, p], view(bank[p][0]), E_low[:, p], ALU.mult).then_inc(
                        sm["low_ready"][p], 1)
                    nc.vector.tensor_tensor(attn[:, q, p], view(bank[p][1]), E_up[:, p], ALU.mult).then_inc(
                        sm["attn_ready"][p], 1)
                for p in range(2):
                    dve.wait_ge(sm["b0_turned"][p], n + 1)
                    nc.vector.tensor_tensor(Y[:, q, p], for_heads(const[:, IDENT, :], H2), view(bank[p][2]),
                                            ALU.subtract).then_inc(lv["y_kept"][p], 1)

            def level(n, q, i, last):
                for p in range(2):
                    dve.wait_ge(lv["y_done"][p], (LP - 1) * n + i)
                    dve.wait_ge(lv["y_kept"][p], LP * n + i)
                    nc.vector.tensor_tensor(Y[:, q, p], Y[:, q, p], view(bank[p][1]), ALU.subtract).then_inc(
                        lv["y_kept"][p], 1)
                    if not last:
                        dve.wait_ge(lv["x_done"][p], (LP - 2) * n + i)
                        if i > 1:
                            dve.wait_ge(lv["x_kept"][p], (LP - 2) * n + i - 1)
                        nc.vector.tensor_tensor(X[:, p], X[:, p], view(bank[p][2]), ALU.subtract).then_inc(
                            lv["x_kept"][p], 1)

            def next_state(n):
                dve.wait_ge(s_done, n + 1)
                if known(n, 1):
                    dve.wait_ge(cleared, 1)
                else:
                    dve.wait_ge(s_kept, n)
                for h in range(HB):
                    ins = nc.vector.scalar_tensor_tensor(out=S[:, h, :], in0=S[:, h, :], scalar=last_p[:, n, h:h + 1],
                                                         in1=p_v[:, h * P:(h + 1) * P], op0=ALU.mult, op1=ALU.add)
                ins.then_inc(s_kept, 1)

            def step(n, q, decode=False):
                levels = LS if decode else LP
                front(n, q, decode)
                for i in range(1, levels):
                    level(n, q, i, i == levels - 1)
                    if i == 2 and not known(n, 1):
                        next_state(n - 1)

            in_steps(dve, step, 0, NTP)
            step(NTP, 0, True)
            for h in range(HB):
                if h == 0:
                    dve.wait_ge(v_kept, NT)
                if h >= 2:
                    dve.wait_ge(ss_done, 2 * (h - 1))
                nc.vector.tensor_tensor(V_of[:, h % 2], for_heads(V[:, h, :], BATCH_S),
                                        over_heads(const[:, BATCH_OF, 0:BATCH_S]), ALU.mult).then_inc(v_spread, 1)
                if h >= 1:
                    decode_state(nc, dve, h - 1, S_new, S_s, last_s, bank, ss_done, ss_kept, new_stored)
            decode_state(nc, dve, HB - 1, S_new, S_s, last_s, bank, ss_done, ss_kept, new_stored)

        @block.scalar
        def _(act):
            def front(n, q, decode):
                for p in range(2):
                    act.wait_ge(sm["hats_turned"][p], n + 1)
                    nc.scalar.copy(kT[:, p], view(bank[p][0]))
                    nc.scalar.copy(qT[:, p], view(bank[p][1])).then_inc(sm["rows_kept"][p], 1)
                    act.wait_ge(sm["gap_ready"][p], n + 1)
                    if not known(n, 1):
                        act.wait_ge(sm["q_scaled"][p], n)
                    nc.scalar.activation(e_row[:, p], view(bank[p][2]), ACT.Exp)
                    act.wait_ge(sm["clamped"][p], n + 1)
                    nc.scalar.activation(E_up[:, p], E_up[:, p], ACT.Exp)
                    nc.scalar.activation(E_low[:, p], E_low[:, p], ACT.Exp).then_inc(sm["e_done"][p], 1)

            def level(n, q, i):
                for p in range(2):
                    act.wait_ge(lv["z_done"][p], (LP - 1) * n + i)
                    nc.scalar.copy(Z[:, p], view(bank[p][0])).then_inc(lv["z_kept"][p], 1)

            def keep_values(n):
                act.wait_ge(v_done, n + 1)
                nc.scalar.copy(V[:], p_v[:].rearrange("p (h c) -> p h c", h=HB)).then_inc(v_kept, 1)

            def keep_outputs(n, q):
                act.wait_ge(o_done, n + 1)
                if not known(n, 2):
                    act.wait_ge(sm["out_stored"][q], 8 * (n - q))
                nc.scalar.copy(outT[:, q], p_o[:].rearrange("p (h c) -> p h c", h=HB)).then_inc(o_kept, 1)

            def step(n, q, decode=False):
                levels = LS if decode else LP
                front(n, q, decode)
                for i in range(1, levels):
                    level(n, q, i)
                    if i == 1 and not known(n, 1):
                        keep_values(n - 1)
                    if i == 2 and not known(n, 1):
                        keep_outputs(n - 1, 1 - q)
                for p in range(2):
                    act.wait_ge(sm["w_done"][p], n + 1)
                    nc.scalar.copy(wT[:, q, p], view(bank[p][0])).then_inc(sm["w_kept"][p], 1)

            in_steps(act, step, 0, NTP)
            step(NTP, 0, True)
            act.wait_ge(vt_done, 1)
            nc.scalar.copy(VT[:], p_v[:].rearrange("p (h c) -> p h c", h=HB)).then_inc(vt_kept, 1)
            keep_values(NTP)
            keep_outputs(NTP, 0)

        @block.gpsimd
        def _(pool):
            nc.gpsimd.memset(S[:], 0.0).then_inc(cleared, 1)

            def heads(p):
                return slice(H2 * p, H2 * p + H2)

            def step(n, q, decode=False):
                levels = LS if decode else LP
                for p in range(2):
                    if not known(n, 1):
                        pool.wait_ge(sm["hats_turned"][p], n)
                    nc.gpsimd.tensor_tensor(g_cols[:, p], over_heads(g[:, n, heads(p)]),
                                            for_heads(const[:, ONES, :], H2), ALU.mult).then_inc(sm["g_spread"][p], 1)
                for p in range(2):
                    pool.wait_ge(sm["hats"][p], n + 1)
                    nc.gpsimd.tensor_tensor(kbg[:, q, p], khat[:, p], over_heads(c_key[:, n, heads(p)]), ALU.mult)
                    nc.gpsimd.tensor_tensor(kdec[:, q, p], khat[:, p], over_heads(c_last[:, n, heads(p)]),
                                            ALU.mult).then_inc(sm["scaled"][p], 1)
                for p in range(2):
                    pool.wait_ge(sm["low_ready"][p], n + 1)
                    if not known(n, 1):
                        pool.wait_ge(lv["y_done"][p], (LP - 1) * n)
                    nc.gpsimd.tensor_tensor(low[:, p], low[:, p], over_heads(beta[:, n, heads(p)]), ALU.mult).then_inc(
                        sm["low_scaled"][p], 1)
                    pool.wait_ge(sm["low_scaled"][p], n + 1)
                    nc.gpsimd.tensor_tensor(below[:, 0, p], low[:, p], for_heads(const[:, LEVEL, :], H2),
                                            ALU.mult).then_inc(sm["b_first"][p], 1)
                    pool.wait_ge(sm["b_first"][p], n + 1)
                    nc.gpsimd.tensor_tensor(X[:, p], for_heads(const[:, IDENT, :], H2), below[:, 0, p],
                                            ALU.subtract).then_inc(sm["x0"][p], 1)
                for p in range(2):
                    for i in range(1, levels):
                        ins = nc.gpsimd.tensor_tensor(below[:, i, p], low[:, p], for_heads(const[:, LEVEL + i, :], H2),
                                                      ALU.mult)
                    ins.then_inc(sm["b_all"][p], 1)
                for p in range(2):
                    pool.wait_ge(sm["e_done"][p], n + 1)
                    nc.gpsimd.tensor_tensor(qTe[:, q, p], qT[:, p], e_row[:, p], ALU.mult).then_inc(sm["q_scaled"][p], 1)
                    pool.wait_ge(sm["attn_ready"][p], n + 1)
                    nc.gpsimd.tensor_tensor(attn[:, q, p], attn[:, q, p],
                                            for_heads(const[:, UPTO_S if decode else UPTO, :], H2),
                                            ALU.mult).then_inc(sm["attn_masked"][p], 1)

            in_steps(pool, step, 0, NTP)
            step(NTP, 0, True)


def decode_state(nc, dve, h, S_new, S_s, last_s, bank, ss_done, ss_kept, new_stored):
    for c in range(2):
        dve.wait_ge(ss_done, 2 * h + c + 1)
        if h >= 2:
            dve.wait_ge(new_stored[h % 2], 16)
        for b in range(4 * c, 4 * c + 4):
            ins = nc.vector.scalar_tensor_tensor(out=S_new[:, h % 2, b, :], in0=S_s[:, b, h, :],
                                                 scalar=last_s[:, h, b:b + 1],
                                                 in1=bank[c][1][:, (b % 4) * P:(b % 4 + 1) * P], op0=ALU.mult,
                                                 op1=ALU.add)
        ins.then_inc(ss_kept, 1)


def split_branches(nc, const, delta_norm, attended_d, out_d, projected_d, a_hi, a_lo, b_hi, b_lo):
    with Scope(nc, "sb_") as s:
        att, o, z = s.sbuf("att", [P, 2, TOK]), s.sbuf("o", [P, 2, TOK]), s.sbuf("z", [P, 2, TOK])
        square, mean, root, normed = (s.sbuf(n, [P, TOK]) for n in ("square", "mean", "root", "normed"))
        gain = s.sbuf("gain", [P, 1])
        p_sum = [s.psum(f"p_sum{i}") for i in range(NG)]
        gain_in = s.sem("gain_in")
        a_in, o_in, z_in = ((s.sem(f"{n}0"), s.sem(f"{n}1")) for n in ("a_in", "o_in", "z_in"))
        (a_hi_done, a_lo_done, squared, summed, averaged, rooted, inverted, scaled, gated, hi_done, lo_done) = (
            s.sem(n) for n in ("a_hi_done", "a_lo_done", "squared", "summed", "averaged", "rooted", "inverted", "scaled",
                               "gated", "hi_done", "lo_done"))
        block = s.block()

        @block.sync
        def _(sp):
            sp.dma_start(gain[:], delta_norm.rearrange("(p a) -> p a", a=1)).then_inc(gain_in, 16)
            for h in range(HB):
                if h >= 2:
                    sp.wait_ge(lo_done, h - 1)
                    sp.wait_ge(a_lo_done, h - 1)
                sp.dma_start(o[:, h % 2], out_d[h]).then_inc(o_in[h % 2], 16)
                sp.dma_start(z[:, h % 2], projected_d[NC + h]).then_inc(z_in[h % 2], 16)
                sp.dma_start(att[:, h % 2], attended_d[h]).then_inc(a_in[h % 2], 16)

        @block.scalar
        def _(act):
            for h in range(HB):
                turn = 16 * (h // 2 + 1)
                act.wait_ge(o_in[h % 2], turn)
                if h >= 1:
                    act.wait_ge(summed, NG * h)
                nc.scalar.activation(square[:], o[:, h % 2], ACT.Square).then_inc(squared, 1)
                act.wait_ge(a_in[h % 2], turn)
                nc.scalar.copy(a_hi[:, h], att[:, h % 2]).then_inc(a_hi_done, 1)
                act.wait_ge(averaged, NG * (h + 1))
                nc.scalar.activation(root[:], mean[:], ACT.Sqrt).then_inc(rooted, 1)
                act.wait_ge(gated, h + 1)
                nc.scalar.copy(b_hi[:, h], normed[:]).then_inc(hi_done, 1)

        @block.tensor
        def _(pe):
            for h in range(HB):
                pe.wait_ge(squared, h + 1)
                for g in range(NG):
                    if h >= 1:
                        pe.wait_ge(averaged, NG * (h - 1) + g + 1)
                    nc.tensor.matmul(p_sum[g][:, 0:TG], const[:, ONES, :], square[:, g * TG:(g + 1) * TG], start=True,
                                     stop=True).then_inc(summed, 1)

        @block.vector
        def _(dve):
            dve.wait_ge(gain_in, 16)
            for h in range(HB):
                for g in range(NG):
                    dve.wait_ge(summed, NG * h + g + 1)
                    nc.vector.tensor_scalar(mean[:, g * TG:(g + 1) * TG], p_sum[g][:, 0:TG], 1.0 / P, EPS, ALU.mult,
                                            ALU.add).then_inc(averaged, 1)
                dve.wait_ge(a_hi_done, h + 1)
                nc.vector.tensor_tensor(a_lo[:, h], att[:, h % 2], a_hi[:, h].bitcast(F32), ALU.subtract).then_inc(
                    a_lo_done, 1)
                dve.wait_ge(rooted, h + 1)
                nc.vector.reciprocal(root[:], root[:]).then_inc(inverted, 1)
                dve.wait_ge(inverted, h + 1)
                if h >= 1:
                    dve.wait_ge(lo_done, h)
                nc.vector.tensor_tensor(normed[:], o[:, h % 2], root[:], ALU.mult).then_inc(scaled, 1)
                dve.wait_ge(scaled, h + 1)
                dve.wait_ge(z_in[h % 2], 16 * (h // 2 + 1))
                nc.vector.scalar_tensor_tensor(out=normed[:], in0=normed[:], scalar=gain[:], in1=z[:, h % 2],
                                               op0=ALU.mult, op1=ALU.mult).then_inc(gated, 1)
                dve.wait_ge(hi_done, h + 1)
                nc.vector.tensor_tensor(b_lo[:, h], normed[:], b_hi[:, h].bitcast(F32), ALU.subtract).then_inc(lo_done, 1)


def merge(nc, x, a_hi, a_lo, b_hi, b_lo, w_branch_a, w_branch_b, w_out, projected_d):
    KB = HB
    FIRST_GATE = NC + HB
    with Scope(nc, "mg_") as s:
        raw_a, raw_b, raw_o = s.sbuf("raw_a", [P, KB, P]), s.sbuf("raw_b", [P, KB, P]), s.sbuf("raw_o", [P, D])
        wa_hi, wa_lo, wb_hi, wb_lo = (s.sbuf(n, [P, 2, KB, P], F32R) for n in ("wa_hi", "wa_lo", "wb_hi", "wb_lo"))
        wo_hi, wo_lo = (s.sbuf(n, [P, 2, D], F32R) for n in ("wo_hi", "wo_lo"))
        gate_a, gate_b = s.sbuf("gate_a", [P, 2, TOK]), s.sbuf("gate_b", [P, 2, TOK])
        part_a, part_b = s.sbuf("part_a", [P, 2, TG]), s.sbuf("part_b", [P, 2, TG])
        m_hi, m_lo = (s.sbuf(n, [P, 2, TOK], F32R) for n in ("m_hi", "m_lo"))
        p_a = [s.psum(f"p_a{i}") for i in range(2)]
        p_b = [s.psum(f"p_b{i}") for i in range(2)]
        p_out = [s.psum(f"p_out{i}") for i in range(4)]
        a_in, b_in, o_in, ab_hi, ab_lo, o_hi, o_lo = (s.sem(n) for n in (
            "a_in", "b_in", "o_in", "ab_hi", "ab_lo", "o_hi", "o_lo"))
        gates_in = s.sem("gates_in0"), s.sem("gates_in1")
        branches, gated_a, gated_b, summed, mhi_done, mlo_done, projected, added = (s.sem(n) for n in (
            "branches", "gated_a", "gated_b", "summed", "mhi_done", "mlo_done", "projected", "added"))
        NO = 2 * NT
        wa, wb = (w.rearrange("(k p) d -> p k d", p=P) for w in (w_branch_a, w_branch_b))
        block = s.block()

        @block.sync
        def _(sp):
            for n in range(KD):
                cols = slice(n * P, (n + 1) * P)
                if n:
                    sp.wait_ge(ab_lo, 2 * n)
                sp.dma_start(raw_a[:], wa[:, :, cols]).then_inc(a_in, 16)
                sp.dma_start(raw_b[:], wb[:, :, cols]).then_inc(b_in, 16)
                if n:
                    sp.wait_ge(o_lo, n)
                sp.dma_start(raw_o[:], w_out[cols, :]).then_inc(o_in, 16)

        @block.gpsimd
        def _(pool):
            for n in range(KD):
                if n >= 2:
                    pool.wait_ge(gated_b, NG * (n - 1))
                pool.dma_start(gate_a[:, n % 2], projected_d[FIRST_GATE + n]).then_inc(gates_in[n % 2], 16)
                pool.dma_start(gate_b[:, n % 2], projected_d[FIRST_GATE + KD + n]).then_inc(gates_in[n % 2], 16)

        @block.scalar
        def _(act):
            def split_branch(n):
                if n >= 2:
                    act.wait_ge(branches, NG * (n - 1))
                act.wait_ge(a_in, 16 * n + 16)
                nc.scalar.copy(wa_hi[:, n % 2], raw_a[:]).then_inc(ab_hi, 1)
                act.wait_ge(b_in, 16 * n + 16)
                nc.scalar.copy(wb_hi[:, n % 2], raw_b[:]).then_inc(ab_hi, 1)

            def split_out(n):
                if n >= 2:
                    act.wait_ge(projected, NO * (n - 1))
                act.wait_ge(o_in, 16 * n + 16)
                nc.scalar.copy(wo_hi[:, n % 2], raw_o[:]).then_inc(o_hi, 1)

            split_branch(0)
            split_branch(1)
            split_out(0)
            for n in range(KD):
                for g in range(NG):
                    act.wait_ge(summed, NG * n + g + 1)
                    if g == 0 and n >= 2:
                        act.wait_ge(projected, NO * (n - 1))
                    nc.scalar.copy(m_hi[:, n % 2, g * TG:(g + 1) * TG], part_a[:, (NG * n + g) % 2]).then_inc(mhi_done, 1)
                if n + 2 < KD:
                    split_branch(n + 2)
                if n + 1 < KD:
                    split_out(n + 1)

        @block.vector
        def _(dve):
            def lo_branch(n):
                dve.wait_ge(ab_hi, 2 * n + 1)
                nc.vector.tensor_tensor(wa_lo[:, n % 2], raw_a[:], wa_hi[:, n % 2].bitcast(F32), ALU.subtract).then_inc(ab_lo, 1)
                dve.wait_ge(ab_hi, 2 * n + 2)
                nc.vector.tensor_tensor(wb_lo[:, n % 2], raw_b[:], wb_hi[:, n % 2].bitcast(F32), ALU.subtract).then_inc(ab_lo, 1)

            def lo_out(n):
                dve.wait_ge(o_hi, n + 1)
                nc.vector.tensor_tensor(wo_lo[:, n % 2], raw_o[:], wo_hi[:, n % 2].bitcast(F32), ALU.subtract).then_inc(o_lo, 1)

            def add_out(n):
                for o in range(NO):
                    dve.wait_ge(projected, NO * n + o + 1)
                    if n:
                        dve.wait_ge(added, NO * (n - 1) + o + 1)
                    xs = x[:, o // 2, o % 2 * 512:o % 2 * 512 + 512]
                    nc.vector.tensor_tensor(xs, p_out[(NO * n + o) % 4][:], xs, ALU.add).then_inc(added, 1)

            lo_branch(0)
            lo_branch(1)
            lo_out(0)
            for n in range(KD):
                dve.wait_ge(gates_in[n % 2], 32 * (n // 2 + 1))
                for g in range(NG):
                    u, mine = NG * n + g, slice(g * TG, (g + 1) * TG)
                    dve.wait_ge(branches, u + 1)
                    if u >= 2:
                        dve.wait_ge(mlo_done, u - 1)
                        dve.wait_ge(summed, u - 1)
                    nc.vector.tensor_tensor(part_a[:, u % 2], p_a[u % 2][:, 0:TG], gate_a[:, n % 2, mine],
                                            ALU.mult).then_inc(gated_a, 1)
                    nc.vector.tensor_tensor(part_b[:, u % 2], p_b[u % 2][:, 0:TG], gate_b[:, n % 2, mine],
                                            ALU.mult).then_inc(gated_b, 1)
                    dve.wait_ge(gated_b, u + 1)
                    nc.vector.tensor_tensor(part_a[:, u % 2], part_a[:, u % 2], part_b[:, u % 2], ALU.add).then_inc(summed, 1)
                    dve.wait_ge(mhi_done, u + 1)
                    nc.vector.tensor_tensor(m_lo[:, n % 2, mine], part_a[:, u % 2], m_hi[:, n % 2, mine].bitcast(F32),
                                            ALU.subtract).then_inc(mlo_done, 1)
                if n:
                    add_out(n - 1)
                if n + 2 < KD:
                    lo_branch(n + 2)
                if n + 1 < KD:
                    lo_out(n + 1)
            add_out(KD - 1)

        @block.tensor
        def _(pe):
            def branch(n):
                for g in range(NG):
                    u, mine = NG * n + g, slice(g * TG, (g + 1) * TG)
                    pe.wait_ge(ab_lo, 2 * n + 2)
                    if u >= 2:
                        pe.wait_ge(gated_b, u - 1)
                    three_passes(nc, p_a[u % 2][:, 0:TG], lambda k: (wa_hi[:, n % 2, k, :], wa_lo[:, n % 2, k, :]),
                                 lambda k: (a_hi[:, k, mine], a_lo[:, k, mine]), range(KB))
                    three_passes(nc, p_b[u % 2][:, 0:TG], lambda k: (wb_hi[:, n % 2, k, :], wb_lo[:, n % 2, k, :]),
                                 lambda k: (b_hi[:, k, mine], b_lo[:, k, mine]), range(KB)).then_inc(branches, 1)

            def out(n):
                pe.wait_ge(o_lo, n + 1)
                for o in range(NO):
                    tokens, cols = slice(o // 2 * P, (o // 2 + 1) * P), slice(o % 2 * 512, o % 2 * 512 + 512)
                    if o % 6 == 0:
                        pe.wait_ge(mlo_done, NG * n + o // 6 + 1)
                    if NO * n + o >= 4:
                        pe.wait_ge(added, NO * n + o - 3)
                    three_passes(nc, p_out[(NO * n + o) % 4][:], lambda k: (m_hi[:, n % 2, tokens], m_lo[:, n % 2, tokens]),
                                 lambda k: (wo_hi[:, n % 2, cols], wo_lo[:, n % 2, cols]), [0]).then_inc(projected, 1)

            for n in range(KD):
                branch(n)
                if n:
                    out(n - 1)
            out(KD - 1)


def finish(nc, x, gain, y_prompt, y_sample):
    with Scope(nc, "fn_") as s:
        gain_b = s.sbuf("gain_b", [P, D])
        square, y = s.sbuf("square", [P, 2, D]), s.sbuf("y", [P, NT, D])
        sumsq, mean, root, rstd = (s.sbuf(n, [P, NT]) for n in ("sumsq", "mean", "root", "rstd"))
        gain_in, squared, averaged, rooted, inverted, normed, stored = (s.sem(n) for n in (
            "gain_in", "squared", "averaged", "rooted", "inverted", "normed", "stored"))
        block = s.block()

        @block.sync
        def _(sp):
            sp.dma_start(gain_b[:], gain.rearrange("(a d) -> a d", a=1).to_broadcast([P, D])).then_inc(gain_in, 16)
            for t in range(NT):
                sp.wait_ge(normed, t + 1)
                dst = y_prompt[0, t * P:(t + 1) * P, :] if t < NTP else y_sample.rearrange("b s d -> (b s) d")
                sp.dma_start(dst, y[:, t]).then_inc(stored, 16)
            sp.wait_ge(stored, 16 * NT)

        @block.scalar
        def _(act):
            for t in range(NT):
                if t >= 2:
                    act.wait_ge(squared, t - 1)
                nc.scalar.activation(square[:, t % 2], x[:, t, :], ACT.Square, accum_out=sumsq[:, t:t + 1]).then_inc(
                    squared, 1)
            act.wait_ge(averaged, 1)
            nc.scalar.activation(root[:], mean[:], ACT.Sqrt).then_inc(rooted, 1)

        @block.vector
        def _(dve):
            dve.wait_ge(squared, NT)
            nc.vector.tensor_scalar(mean[:], sumsq[:], 1.0 / D, EPS, ALU.mult, ALU.add).then_inc(averaged, 1)
            dve.wait_ge(rooted, 1)
            nc.vector.reciprocal(rstd[:], root[:]).then_inc(inverted, 1)
            dve.wait_ge(inverted, 1)
            dve.wait_ge(gain_in, 16)
            for t in range(NT):
                nc.vector.scalar_tensor_tensor(out=y[:, t], in0=x[:, t, :], scalar=rstd[:, t:t + 1], in1=gain_b[:],
                                               op0=ALU.mult, op1=ALU.mult).then_inc(normed, 1)


INPUTS = ["x_prompt", "x_sample", "cache_attn_k", "cache_attn_v", "cache_idx_k", "state_conv", "state_delta",
          "ffn1_norm", "ffn1_w_gate", "ffn1_w_up", "ffn1_w_down", "mix_norm", "w_in", "conv_w", "a_log", "dt_bias",
          "delta_norm", "w_branch_a", "w_branch_b", "w_out", "ffn2_norm", "ffn2_w_gate", "ffn2_w_up", "ffn2_w_down",
          "final_norm"]
OUTPUTS = [("y_prompt", (1, SEQ, D)), ("y_sample", (BATCH_S, SEQ_S, D)),
           ("new_k", (1, 1, SEQ, KV, HD)), ("new_v", (1, 1, SEQ, KV, HD)), ("new_idx_k", (1, 1, SEQ, HD)),
           ("new_conv", (1, 1, CONV_W - 1, CONV_CH)), ("new_delta", (1, 1, HB, DK, DK)),
           ("new_k_s", (1, BATCH_S, SEQ_S, KV, HD)), ("new_v_s", (1, BATCH_S, SEQ_S, KV, HD)),
           ("new_idx_k_s", (1, BATCH_S, SEQ_S, HD)), ("new_conv_s", (1, BATCH_S, CONV_W - 1, CONV_CH)),
           ("new_delta_s", (1, BATCH_S, HB, DK, DK))]


def encoder_step(nc, i, o, const_in):
    projected_d = nc.dram_tensor("projected_d", (NC + HB + 2 * KD, P, TOK), F32, kind="Internal").ap()
    conv_d = nc.dram_tensor("conv_d", (NC, P, TOK), F32, kind="Internal").ap()
    delta_d = nc.dram_tensor("delta_d", (HB, P, TOK), F32, kind="Internal").ap()
    attended_d = nc.dram_tensor("attended_d", (HB, P, TOK), F32, kind="Internal").ap()
    w_in = i["w_in"][0]
    with Scope(nc, "") as top:
        x, const = top.sbuf("x", [P, NT, D]), top.sbuf("const", [P, CONSTS, P])
        load_start(nc, x, const, i["x_prompt"], i["x_sample"], const_in)

        with Scope(nc, "f1_") as s:
            hT_hi, hT_lo = s.sbuf("hT_hi", [P, KD, TOK], F32R), s.sbuf("hT_lo", [P, KD, TOK], F32R)
            norm_turn(nc, x, const, hT_hi, hT_lo, i["ffn1_norm"][0], "n1_")
            ffn(nc, x, hT_hi, hT_lo, i["ffn1_w_gate"][0], i["ffn1_w_up"][0], i["ffn1_w_down"][0], "ffn1_")

        with Scope(nc, "mx_") as mix:
            small = mix.sbuf("small", [P, NT, 12])
            with Scope(nc, "sa_") as sparse:
                qkT, va = sparse.sbuf("qkT", [P, 5, TOK]), sparse.sbuf("va", [P, NT, P])
                scores = sparse.sbuf("scores", [P, SCORES])
                with Scope(nc, "h_") as s:
                    hT_hi, hT_lo = s.sbuf("hT_hi", [P, KD, TOK], F32R), s.sbuf("hT_lo", [P, KD, TOK], F32R)
                    norm_turn(nc, x, const, hT_hi, hT_lo, i["mix_norm"][0], "n2_")
                    project_small(nc, hT_hi, hT_lo, w_in, va, small, o["new_k"], o["new_v"], o["new_idx_k"],
                                  o["new_k_s"], o["new_v_s"], o["new_idx_k_s"])
                    with Scope(nc, "ix_") as index:
                        qiT = index.sbuf("qiT", [P, 4, TOK])
                        project_turned(nc, hT_hi, hT_lo, w_in, qkT, qiT)
                        score(nc, const, qiT, small, i["cache_idx_k"], scores)
                    select_and_project(nc, hT_hi, hT_lo, w_in, scores, projected_d)
                attend(nc, const, qkT, va, scores, i["cache_attn_k"], i["cache_attn_v"], attended_d)
            with Scope(nc, "dn_") as s:
                inv_norm = s.sbuf("inv_norm", [P, NT, 2 * HB])
                convolve(nc, const, i["conv_w"][0], i["state_conv"], projected_d, conv_d, inv_norm, o["new_conv"],
                         o["new_conv_s"])
                beta, g, cum, c_key, c_last = (s.sbuf(n, [P, NT, HB]) for n in ("beta", "g", "cum", "c_key", "c_last"))
                last_p, last_s = s.sbuf("last_p", [P, NTP, HB]), s.sbuf("last_s", [P, HB, BATCH_S])
                decays(nc, const, small, i["a_log"], i["dt_bias"], beta, g, cum, c_key, c_last, last_p, last_s)
                delta(nc, const, beta, g, cum, c_key, c_last, last_p, last_s, inv_norm, conv_d, i["state_delta"],
                      delta_d, o["new_delta"], o["new_delta_s"])
            with Scope(nc, "br_") as s:
                a_hi, a_lo, b_hi, b_lo = (s.sbuf(n, [P, HB, TOK], F32R) for n in ("a_hi", "a_lo", "b_hi", "b_lo"))
                split_branches(nc, const, i["delta_norm"][0], attended_d, delta_d, projected_d, a_hi, a_lo, b_hi, b_lo)
                merge(nc, x, a_hi, a_lo, b_hi, b_lo, i["w_branch_a"][0], i["w_branch_b"][0], i["w_out"][0], projected_d)

        with Scope(nc, "f2_") as s:
            hT_hi, hT_lo = s.sbuf("hT_hi", [P, KD, TOK], F32R), s.sbuf("hT_lo", [P, KD, TOK], F32R)
            norm_turn(nc, x, const, hT_hi, hT_lo, i["ffn2_norm"][0], "n3_")
            ffn(nc, x, hT_hi, hT_lo, i["ffn2_w_gate"][0], i["ffn2_w_up"][0], i["ffn2_w_down"][0], "ffn2_")
        finish(nc, x, i["final_norm"], o["y_prompt"], o["y_sample"])


def kernel(**inputs):
    import concourse.bacc as bacc
    from concourse.bass_utils import run_bass_kernel_spmd

    nc = bacc.Bacc("TRN2", target_bir_lowering=False, num_devices=1)
    arrays, ins, outs = {}, {}, {}
    for name in INPUTS:
        a = np.ascontiguousarray(inputs[name])
        arrays[f"in_{name}"] = a
        ins[name] = nc.dram_tensor(f"in_{name}", a.shape, mybir.dt.from_np(a.dtype), kind="ExternalInput").ap()
    arrays["in_constants"] = constants()
    const_in = nc.dram_tensor("in_constants", (P, CONSTS, P), F32, kind="ExternalInput").ap()
    for name, shape in OUTPUTS:
        outs[name] = nc.dram_tensor(f"out_{name}", shape, F32, kind="ExternalOutput").ap()
    encoder_step(nc, ins, outs, const_in)
    got = run_bass_kernel_spmd(nc, [arrays], core_ids=[0]).results[0]
    return tuple(got[f"out_{name}"] for name, _ in OUTPUTS)
```

```python
from contextlib import ExitStack

import numpy as np

import concourse.bass as bass
from concourse import mybir

F32 = mybir.dt.float32
F32R = mybir.dt.float32r
ALU = mybir.AluOpType
ACT = mybir.ActivationFunctionType
AX = mybir.AxisListType

P = 128
D = 1024
KD = D // P
DFF = 2816
NF = DFF // P
SEQ = 1024
BATCH_S, SEQ_S, PAST = 8, 16, 256
TOK = SEQ + BATCH_S * SEQ_S
NT = TOK // P
NTP = SEQ // P
TG = 384
NG = TOK // TG
EPS = 1e-6

HEADS, KV, HD = 8, 2, 64
IH = 4
CHUNK = 64
TOPK_P, TOPK_S = 256, 68
KEYS_S = PAST + SEQ_S
HB, DK = 4, 128
CONV_CH, CONV_W = 1536, 4
NC = CONV_CH // P
C_Q, C_K, C_V, C_QI, C_KI, C_WI = 0, 512, 640, 768, 1024, 1088
C_CONV, C_Z, C_BB, C_GATE = 1092, 2628, 3140, 3148
D_IN = 5196
SMALL = 256 + 68 + 8
S_V, S_KI, S_WI, S_BB = 128, 256, 320, 324

TAKEN, INADMISSIBLE, FILL, UNSELECTED = -3.0e38, -2.0e38, -1.0e38, -1.0e30
WIDTH = [P * (t + 1) for t in range(NTP)] + [KEYS_S]
PAD_S = 8
AT = [sum(WIDTH[:t]) for t in range(NT)]
SCORES = sum(WIDTH) + PAD_S

ONES, IDENT, UPTO, UPTO_S, SAME_S, BATCH_OF, LEVEL = range(7)
LEVELS_P, LEVELS_S = 7, 4
CONSTS = LEVEL + LEVELS_P


def constants():
    i, j = np.arange(P)[:, None], np.arange(P)[None, :]
    same = i // SEQ_S == j // SEQ_S
    planes = [np.ones((P, P)), i == j, i <= j, (i <= j) & same, same, (i // SEQ_S == j)]
    for level in range(LEVELS_P):
        m = 1 << level
        planes.append((i // (2 * m) == j // (2 * m)) & (i % (2 * m) >= m) & (j % (2 * m) < m))
    return np.ascontiguousarray(np.stack([np.asarray(p, np.float32) for p in planes], 1))


def known(n, below):
    return isinstance(n, int) and n < below


def in_steps(eng, step, first, last, lead=1):
    n = first
    while n < min(first + lead, last):
        step(n, n % 2)
        n += 1
    pairs = (last - n) // 2
    if pairs > 1:
        with eng.Fori(0, pairs) as j:
            step(2 * j + n, n % 2)
            step(2 * j + n + 1, (n + 1) % 2)
        n += 2 * pairs
    while n < last:
        step(n, n % 2)
        n += 1


class Scope:

    def __init__(self, nc, name):
        self.nc, self.name, self.stack, self.sems = nc, name, ExitStack(), []

    def __enter__(self):
        return self

    def __exit__(self, *what):
        left = self.stack.__exit__(*what)
        if self.sems:
            self.nc.clear_and_free_semaphores(self.sems)
            self.nc.all_engine_barrier()
        return left

    def sbuf(self, name, shape, dt=F32):
        return self.stack.enter_context(self.nc.sbuf_tensor(self.name + name, shape, dt))

    def psum(self, name, shape=(P, 512)):
        return self.stack.enter_context(self.nc.psum_tensor(self.name + name, list(shape), F32))

    def sem(self, name):
        self.sems.append(self.nc.alloc_semaphore(self.name + name))
        return self.sems[-1]

    def block(self):
        return self.stack.enter_context(self.nc.Block())


def three_passes(nc, out, stationary, moving, ks):
    n, mm = 3 * len(ks), None
    for at, k in enumerate(ks):
        for i, (a, b) in enumerate(((0, 0), (0, 1), (1, 0))):
            mm = nc.tensor.matmul(out, stationary(k)[a], moving(k)[b], start=(at == 0 and i == 0),
                                  stop=(3 * at + i == n - 1))
    return mm


def load_start(nc, x, const, x_prompt, x_sample, const_in):
    with Scope(nc, "in_") as s:
        x_in, const_ready = s.sem("x_in"), s.sem("const_in")
        block = s.block()

        @block.sync
        def _(sp):
            sp.dma_start(x[:, 0:NTP, :], x_prompt[0].rearrange("(t p) d -> p t d", p=P)).then_inc(x_in, 16)
            sp.wait_ge(x_in, 16)

        @block.scalar
        def _(act):
            act.dma_start(x[:, NTP, :], x_sample.rearrange("b s d -> (b s) d")).then_inc(const_ready, 16)
            act.dma_start(const[:], const_in).then_inc(const_ready, 16)
            act.wait_ge(const_ready, 32)


def norm_turn(nc, x, const, hT_hi, hT_lo, gain, name):
    with Scope(nc, name) as s:
        gain_b = s.sbuf("gain_b", [P, D])
        sumsq, mean, root, rstd = (s.sbuf(n, [P, NT]) for n in ("sumsq", "mean", "root", "rstd"))
        h = s.sbuf("h", [P, 2, D])
        pT = [s.psum(f"pT{i}", (P, 4, P)) for i in range(4)]
        gain_in, squared, mean_ready, rooted, rstd_ready = (
            s.sem(n) for n in ("gain_in", "squared", "mean_ready", "rooted", "rstd_ready"))
        h_ready, turned, hi_ready, lo_ready = (s.sem(n) for n in ("h_ready", "turned", "hi_ready", "lo_ready"))
        block = s.block()

        def part(i):
            return slice(None), slice(4 * (i % 2), 4 * (i % 2) + 4), slice((i // 2) * P, (i // 2 + 1) * P)

        @block.sync
        def _(sp):
            sp.dma_start(gain_b[:], gain.rearrange("(a d) -> a d", a=1).to_broadcast([P, D])).then_inc(gain_in, 16)

        @block.scalar
        def _(act):
            for t in range(NT):
                if t >= 2:
                    act.wait_ge(squared, t - 1)
                nc.scalar.activation(h[:, t % 2, :], x[:, t, :], ACT.Square,
                                     accum_out=sumsq[:, t:t + 1]).then_inc(squared, 1)
            act.wait_ge(mean_ready, 1)
            nc.scalar.activation(root[:], mean[:], ACT.Sqrt).then_inc(rooted, 1)
            for i in range(2 * NT):
                act.wait_ge(turned, i + 1)
                nc.scalar.copy(hT_hi[part(i)], pT[i % 4][:]).then_inc(hi_ready, 1)

        @block.vector
        def _(dve):
            dve.wait_ge(squared, NT)
            nc.vector.tensor_scalar(mean[:], sumsq[:], 1.0 / D, EPS, ALU.mult, ALU.add).then_inc(mean_ready, 1)
            dve.wait_ge(rooted, 1)
            nc.vector.reciprocal(rstd[:], root[:]).then_inc(rstd_ready, 1)
            dve.wait_ge(rstd_ready, 1)
            dve.wait_ge(gain_in, 16)
            for t in range(NT + 1):
                if t < NT:
                    if t >= 2:
                        dve.wait_ge(turned, 2 * (t - 1))
                    nc.vector.scalar_tensor_tensor(out=h[:, t % 2, :], in0=x[:, t, :], scalar=rstd[:, t:t + 1],
                                                   in1=gain_b[:], op0=ALU.mult, op1=ALU.mult).then_inc(h_ready, 1)
                if t >= 1:
                    for i in (2 * t - 2, 2 * t - 1):
                        dve.wait_ge(hi_ready, i + 1)
                        nc.vector.tensor_tensor(hT_lo[part(i)], pT[i % 4][:], hT_hi[part(i)].bitcast(F32),
                                                ALU.subtract).then_inc(lo_ready, 1)

        @block.tensor
        def _(pe):
            for i in range(2 * NT):
                pe.wait_ge(h_ready, i // 2 + 1)
                if i >= 4:
                    pe.wait_ge(lo_ready, i - 3)
                for k in range(4):
                    kk = 4 * (i % 2) + k
                    mm = nc.tensor.transpose(pT[i % 4][:, k, :], h[:, (i // 2) % 2, kk * P:(kk + 1) * P],
                                             const[:, IDENT, :])
                mm.then_inc(turned, 1)


def ffn(nc, x, hT_hi, hT_lo, w_gate, w_up, w_down, name):
    with Scope(nc, name) as s:
        raw_g, raw_u, raw_d = s.sbuf("raw_g", [P, KD, P]), s.sbuf("raw_u", [P, KD, P]), s.sbuf("raw_d", [P, D])
        g_hi, g_lo, u_hi, u_lo = (s.sbuf(n, [P, 2, KD, P], F32R) for n in ("g_hi", "g_lo", "u_hi", "u_lo"))
        d_hi, d_lo = (s.sbuf(n, [P, 2, D], F32R) for n in ("d_hi", "d_lo"))
        a_hi, a_lo = (s.sbuf(n, [P, 2, TOK], F32R) for n in ("a_hi", "a_lo"))
        silu, prod = s.sbuf("silu", [P, 2, TG]), s.sbuf("prod", [P, 2, TG])
        p_gate = [s.psum(f"p_gate{i}") for i in range(2)]
        p_up = [s.psum(f"p_up{i}") for i in range(2)]
        p_down = [s.psum(f"p_down{i}") for i in range(4)]
        g_in, u_in, d_in = s.sem("g_in"), s.sem("u_in"), s.sem("d_in")
        gu_hi, gu_lo = s.sem("gu_hi"), s.sem("gu_lo")
        dn_hi, dn_lo = s.sem("dn_hi"), s.sem("dn_lo")
        gate_up, silu_done, prod_done, act_hi, act_lo = (
            s.sem(n) for n in ("gate_up", "silu_done", "prod_done", "act_hi", "act_lo"))
        down, added = s.sem("down"), s.sem("added")
        wg, wu = (w.rearrange("(k p) f -> p k f", p=P) for w in (w_gate, w_up))
        NO = 2 * NT
        block = s.block()

        @block.sync
        def _(sp):
            def load(n, q):
                if not known(n, 1):
                    sp.wait_ge(gu_lo, 2 * n - 1)
                sp.dma_start(raw_g[:], wg[:, :, bass.ts(n, P)]).then_inc(g_in, 16)
                if not known(n, 1):
                    sp.wait_ge(gu_lo, 2 * n)
                sp.dma_start(raw_u[:], wu[:, :, bass.ts(n, P)]).then_inc(u_in, 16)
                if not known(n, 1):
                    sp.wait_ge(dn_lo, n)
                sp.dma_start(raw_d[:], w_down[bass.ts(n, P), :]).then_inc(d_in, 16)

            in_steps(sp, load, 0, NF)

        @block.scalar
        def _(act):
            def split_gate_up(n, q):
                if not known(n, 2):
                    act.wait_ge(gate_up, NG * (n - 1))
                act.wait_ge(g_in, 16 * n + 16)
                nc.scalar.copy(g_hi[:, q], raw_g[:]).then_inc(gu_hi, 1)
                act.wait_ge(u_in, 16 * n + 16)
                nc.scalar.copy(u_hi[:, q], raw_u[:]).then_inc(gu_hi, 1)

            def split_down(n, q):
                if not known(n, 2):
                    act.wait_ge(down, NO * (n - 1))
                act.wait_ge(d_in, 16 * n + 16)
                nc.scalar.copy(d_hi[:, q], raw_d[:]).then_inc(dn_hi, 1)

            def step(n, q):
                for g in range(NG):
                    slot = (NG * q + g) % 2
                    act.wait_ge(gate_up, NG * n + g + 1)
                    if not (known(n, 1) and g < 2):
                        act.wait_ge(prod_done, NG * n + g - 1)
                    nc.scalar.activation(silu[:, slot], p_gate[slot][:, 0:TG], ACT.Silu).then_inc(silu_done, 1)
                    act.wait_ge(prod_done, NG * n + g + 1)
                    if g == 0 and not known(n, 2):
                        act.wait_ge(down, NO * (n - 1))
                    nc.scalar.copy(a_hi[:, q, g * TG:(g + 1) * TG], prod[:, slot]).then_inc(act_hi, 1)
                if not known(n, NF) or n + 2 < NF:
                    split_gate_up(n + 2, q)
                if not known(n, NF) or n + 1 < NF:
                    split_down(n + 1, 1 - q)

            split_gate_up(0, 0)
            split_gate_up(1, 1)
            split_down(0, 0)
            in_steps(act, step, 0, NF - 2, lead=2)
            in_steps(act, step, NF - 2, NF)

        @block.vector
        def _(dve):
            def split_gate_up(n, q):
                dve.wait_ge(gu_hi, 2 * n + 1)
                nc.vector.tensor_tensor(g_lo[:, q], raw_g[:], g_hi[:, q].bitcast(F32), ALU.subtract).then_inc(gu_lo, 1)
                dve.wait_ge(gu_hi, 2 * n + 2)
                nc.vector.tensor_tensor(u_lo[:, q], raw_u[:], u_hi[:, q].bitcast(F32), ALU.subtract).then_inc(gu_lo, 1)

            def split_down(n, q):
                dve.wait_ge(dn_hi, n + 1)
                nc.vector.tensor_tensor(d_lo[:, q], raw_d[:], d_hi[:, q].bitcast(F32), ALU.subtract).then_inc(dn_lo, 1)

            def add_down(n, q):
                for o in range(NO):
                    dve.wait_ge(down, NO * n + o + 1)
                    if not known(n, 1):
                        dve.wait_ge(added, NO * (n - 1) + o + 1)
                    xs = x[:, o // 2, (o % 2) * 512:(o % 2) * 512 + 512]
                    nc.vector.scalar_tensor_tensor(out=xs, in0=p_down[(NO * q + o) % 4][:], scalar=0.5, in1=xs,
                                                   op0=ALU.mult, op1=ALU.add).then_inc(added, 1)

            def step(n, q):
                for g in range(NG):
                    slot = (NG * q + g) % 2
                    dve.wait_ge(silu_done, NG * n + g + 1)
                    if not (known(n, 1) and g < 2):
                        dve.wait_ge(act_lo, NG * n + g - 1)
                    nc.vector.tensor_tensor(prod[:, slot], silu[:, slot], p_up[slot][:, 0:TG],
                                            ALU.mult).then_inc(prod_done, 1)
                    dve.wait_ge(act_hi, NG * n + g + 1)
                    mine = slice(g * TG, (g + 1) * TG)
                    nc.vector.tensor_tensor(a_lo[:, q, mine], prod[:, slot], a_hi[:, q, mine].bitcast(F32),
                                            ALU.subtract).then_inc(act_lo, 1)
                if not known(n, 1):
                    add_down(n - 1, 1 - q)
                if not known(n, NF) or n + 2 < NF:
                    split_gate_up(n + 2, q)
                if not known(n, NF) or n + 1 < NF:
                    split_down(n + 1, 1 - q)

            split_gate_up(0, 0)
            split_gate_up(1, 1)
            split_down(0, 0)
            in_steps(dve, step, 0, NF - 2, lead=2)
            in_steps(dve, step, NF - 2, NF)
            add_down(NF - 1, (NF - 1) % 2)

        @block.tensor
        def _(pe):
            def gate_and_up(n, q):
                for g in range(NG):
                    slot, mine = (NG * q + g) % 2, slice(g * TG, (g + 1) * TG)
                    if g == 0:
                        pe.wait_ge(gu_lo, 2 * n + 1)
                    if not (known(n, 1) and g < 2):
                        pe.wait_ge(silu_done, NG * n + g - 1)
                    three_passes(nc, p_gate[slot][:, 0:TG], lambda k: (g_hi[:, q, k, :], g_lo[:, q, k, :]),
                                 lambda k: (hT_hi[:, k, mine], hT_lo[:, k, mine]), range(KD))
                    if g == 0:
                        pe.wait_ge(gu_lo, 2 * n + 2)
                    if not (known(n, 1) and g < 2):
                        pe.wait_ge(prod_done, NG * n + g - 1)
                    three_passes(nc, p_up[slot][:, 0:TG], lambda k: (u_hi[:, q, k, :], u_lo[:, q, k, :]),
                                 lambda k: (hT_hi[:, k, mine], hT_lo[:, k, mine]), range(KD)).then_inc(gate_up, 1)

            def down_proj(n, q):
                pe.wait_ge(dn_lo, n + 1)
                for o in range(NO):
                    tokens, cols = slice(o // 2 * P, (o // 2 + 1) * P), slice(o % 2 * 512, o % 2 * 512 + 512)
                    if o % 6 == 0:
                        pe.wait_ge(act_lo, NG * n + o // 6 + 1)
                    if not (known(n, 1) and o < 4):
                        pe.wait_ge(added, NO * n + o - 3)
                    three_passes(nc, p_down[(NO * q + o) % 4][:], lambda k: (a_hi[:, q, tokens], a_lo[:, q, tokens]),
                                 lambda k: (d_hi[:, q, cols], d_lo[:, q, cols]), [0]).then_inc(down, 1)

            def step(n, q):
                gate_and_up(n, q)
                if not known(n, 1):
                    down_proj(n - 1, 1 - q)

            in_steps(pe, step, 0, NF, lead=2)
            down_proj(NF - 1, (NF - 1) % 2)


def diagonal(flat):
    return flat.rearrange("p (b c) -> p b c", b=BATCH_S)[:, :, 0:SEQ_S]


def project_small(nc, hT_hi, hT_lo, w_in, va, small, new_k, new_v, new_ki, new_ks, new_vs, new_kis):
    with Scope(nc, "ps_") as s:
        raw = s.sbuf("raw", [P, KD, SMALL])
        w_hi, w_lo = s.sbuf("w_hi", [P, KD, SMALL], F32R), s.sbuf("w_lo", [P, KD, SMALL], F32R)
        out = s.sbuf("out", [P, 2, SMALL])
        p_out = [s.psum(f"p_out{i}") for i in range(2)]
        w_raw, w_split_hi, w_split_lo, projected, kept, copied = (
            s.sem(n) for n in ("w_raw", "w_split_hi", "w_split_lo", "projected", "kept", "copied"))
        stored = s.sem("stored0"), s.sem("stored1")
        w = w_in.rearrange("(k p) c -> p k c", p=P)
        block = s.block()
        spans = ((0, C_K, S_KI), (S_KI, C_KI, S_BB - S_KI), (S_BB, C_BB, SMALL - S_BB))

        @block.sync
        def _(sp):
            for at, column, n in spans:
                sp.dma_start(raw[:, :, at:at + n], w[:, :, column:column + n]).then_inc(w_raw, 16)
            for t in range(NT):
                sp.wait_ge(copied, t + 1)
                if t < NTP:
                    rows = slice(t * P, (t + 1) * P)
                    outs = (new_k[0, 0, rows, :, :].rearrange("s n d -> s (n d)"),
                            new_v[0, 0, rows, :, :].rearrange("s n d -> s (n d)"), new_ki[0, 0, rows, :])
                else:
                    outs = (new_ks[0].rearrange("b s n d -> (b s) (n d)"), new_vs[0].rearrange("b s n d -> (b s) (n d)"),
                            new_kis[0].rearrange("b s d -> (b s) d"))
                for dst, cols in zip(outs, (slice(0, S_V), slice(S_V, S_KI), slice(S_KI, S_WI))):
                    sp.dma_start(dst, out[:, t % 2, cols]).then_inc(stored[t % 2], 16)
            for q in range(2):
                sp.wait_ge(stored[q], 48 * ((NT + 1 - q) // 2))

        @block.scalar
        def _(act):
            act.wait_ge(w_raw, 16 * len(spans))
            nc.scalar.copy(w_hi[:], raw[:]).then_inc(w_split_hi, 1)
            for t in range(NT):
                act.wait_ge(projected, t + 1)
                if t >= 2:
                    act.wait_ge(stored[t % 2], 48 * (t // 2))
                    act.wait_ge(kept, t - 1)
                nc.scalar.copy(out[:, t % 2, :], p_out[t % 2][:, 0:SMALL]).then_inc(copied, 1)

        @block.vector
        def _(dve):
            dve.wait_ge(w_split_hi, 1)
            nc.vector.tensor_tensor(w_lo[:], raw[:], w_hi[:].bitcast(F32), ALU.subtract).then_inc(w_split_lo, 1)
            for t in range(NT):
                dve.wait_ge(copied, t + 1)
                nc.vector.tensor_copy(va[:, t, :], out[:, t % 2, S_V:S_KI])
                nc.vector.tensor_copy(small[:, t, :], out[:, t % 2, S_WI:SMALL]).then_inc(kept, 1)

        @block.tensor
        def _(pe):
            pe.wait_ge(w_split_lo, 1)
            for t in range(NT):
                if t >= 2:
                    pe.wait_ge(copied, t - 1)
                tokens = slice(t * P, (t + 1) * P)
                three_passes(nc, p_out[t % 2][:, 0:SMALL], lambda k: (hT_hi[:, k, tokens], hT_lo[:, k, tokens]),
                             lambda k: (w_hi[:, k, :], w_lo[:, k, :]), range(KD)).then_inc(projected, 1)


def project_turned(nc, hT_hi, hT_lo, w_in, qkT, qiT):
    with Scope(nc, "pt_") as s:
        raw = s.sbuf("raw", [P, KD, P])
        w_hi, w_lo = s.sbuf("w_hi", [P, 2, KD, P], F32R), s.sbuf("w_lo", [P, 2, KD, P], F32R)
        p_out = [s.psum(f"p_out{i}") for i in range(2 * NG)]
        w_raw, w_split_hi, w_split_lo, projected, copied, upper_zero = (
            s.sem(n) for n in ("w_raw", "w_split_hi", "w_split_lo", "projected", "copied", "upper_zero"))
        w = w_in.rearrange("(k p) c -> p k c", p=P)
        block = s.block()

        @block.gpsimd
        def _(pool):
            nc.gpsimd.memset(qiT[HD:P, 2, :], 0.0).then_inc(upper_zero, 1)
            pool.wait_ge(upper_zero, 1)
            nc.gpsimd.memset(qiT[0:HD, 3, :], 0.0)

        starts = [(C_Q + HD * j, C_Q + HD * (4 + j)) for j in range(4)]
        starts += [(C_K, C_K + HD), (C_QI, C_QI + HD), (C_QI + 2 * HD, C_QI + 3 * HD), (C_KI, C_KI)]
        NB = len(starts)

        @block.sync
        def _(sp):
            for n, pair in enumerate(starts):
                if n:
                    sp.wait_ge(w_split_lo, n)
                for i, c in enumerate(pair):
                    sp.dma_start(raw[:, :, i * HD:(i + 1) * HD], w[:, :, c:c + HD]).then_inc(w_raw, 16)

        @block.scalar
        def _(act):
            def split(n):
                act.wait_ge(w_raw, 32 * (n + 1))
                if n >= 2:
                    act.wait_ge(projected, NG * (n - 1))
                nc.scalar.copy(w_hi[:, n % 2], raw[:]).then_inc(w_split_hi, 1)

            split(0)
            split(1)
            for n in range(NB):
                for g in range(NG):
                    act.wait_ge(projected, NG * n + g + 1)
                    mine, bank = slice(g * TG, (g + 1) * TG), p_out[NG * (n % 2) + g]
                    if n < NB - 1:
                        dst = qkT[:, n, mine] if n < 5 else qiT[:, n - 5, mine]
                        nc.scalar.copy(dst, bank[:, 0:TG]).then_inc(copied, 1)
                    else:
                        nc.scalar.copy(qiT[0:HD, 2, mine], bank[0:HD, 0:TG])
                        nc.scalar.copy(qiT[HD:P, 3, mine], bank[HD:P, 0:TG]).then_inc(copied, 1)
                if n + 2 < NB:
                    split(n + 2)

        @block.vector
        def _(dve):
            for n in range(NB):
                dve.wait_ge(w_split_hi, n + 1)
                nc.vector.tensor_tensor(w_lo[:, n % 2], raw[:], w_hi[:, n % 2].bitcast(F32),
                                        ALU.subtract).then_inc(w_split_lo, 1)

        @block.tensor
        def _(pe):
            for n in range(NB):
                pe.wait_ge(w_split_lo, n + 1)
                for g in range(NG):
                    if n >= 2:
                        pe.wait_ge(copied, NG * (n - 2) + g + 1)
                    mine = slice(g * TG, (g + 1) * TG)
                    three_passes(nc, p_out[NG * (n % 2) + g][:, 0:TG],
                                 lambda k: (w_hi[:, n % 2, k, :], w_lo[:, n % 2, k, :]),
                                 lambda k: (hT_hi[:, k, mine], hT_lo[:, k, mine]), range(KD)).then_inc(projected, 1)


def score(nc, const, qiT, small, cache_idx_k, scores):
    with Scope(nc, "sc_") as s:
        weight = s.sbuf("weight", [P, NT, IH])
        cache = s.sbuf("cache", [P, 2, 2, P])
        keysT = s.sbuf("keysT", [P, BATCH_S, KEYS_S])
        spread = s.sbuf("spread", [P, 2, BATCH_S * (P + SEQ_S)])
        relu = s.sbuf("relu", [P, 2, 512])
        p_logit = [s.psum(f"p_logit{i}") for i in range(4)]
        p_keys = [s.psum(f"p_keys{i}", (P, 2, PAST)) for i in range(2)]
        names = ("cache_in0", "cache_in1", "weighted", "cleared", "spread_ready", "keys_turned", "keys_ready",
                 "new_keys", "logits", "rectified", "summed", "masked")
        (cache_in0, cache_in1, weighted, cleared, spread_ready, keys_turned, keys_ready, new_keys, logits, rectified,
         summed, masked) = (
            s.sem(n) for n in names)
        cache_in = (cache_in0, cache_in1)
        units = [(t, c, min(512, WIDTH[t] - c), h) for t in range(2, NTP) for c in range(0, WIDTH[t], 512)
                 for h in range(IH)] + [(NTP, 0, KEYS_S, h) for h in range(IH)]
        block = s.block()

        @block.sync
        def _(sp):
            for b in range(BATCH_S):
                if b >= 2:
                    sp.wait_ge(keys_turned, b - 1)
                for i in range(2):
                    sp.dma_start(cache[:, b % 2, :, i * HD:(i + 1) * HD],
                                 cache_idx_k[0, b].rearrange("(c p) d -> p c d", p=P)).then_inc(cache_in[b % 2], 16)

        @block.gpsimd
        def _(pool):
            nc.gpsimd.tensor_scalar(weight[:], small[:, :, 0:IH], 1.0 / 16.0, None, ALU.mult).then_inc(weighted, 1)
            nc.gpsimd.memset(spread[:], 0.0).then_inc(cleared, 1)
            pool.wait_ge(weighted, 1)
            pool.wait_ge(cleared, 1)
            for i in range(2):
                rows = slice(HD * i, HD * i + HD)
                if i:
                    pool.wait_ge(new_keys, i)
                nc.gpsimd.tensor_copy(keysT[rows, :, PAST:KEYS_S], qiT[rows, 2 + i, SEQ:TOK].rearrange(
                    "p (b j) -> p b j", b=BATCH_S)).then_inc(new_keys, 1)
            pool.wait_ge(new_keys, 2)
            for h in range(IH):
                if h:
                    pool.wait_ge(spread_ready, h)
                if h >= 2:
                    pool.wait_ge(logits, len(units) - IH + h - 1)
                rows = slice(HD * (h % 2), HD * (h % 2) + HD)
                nc.gpsimd.tensor_copy(diagonal(spread[rows, h % 2, :]), qiT[rows, h // 2, SEQ:TOK].rearrange(
                    "p (b j) -> p b j", b=BATCH_S)).then_inc(spread_ready, 1)

        @block.scalar
        def _(act):
            for i in range(BATCH_S // 2):
                act.wait_ge(keys_turned, 2 * i + 2)
                nc.scalar.copy(keysT[:, 2 * i:2 * i + 2, 0:PAST], p_keys[i % 2][:]).then_inc(keys_ready, 1)
            for u, (t, c, n, h) in enumerate(units):
                act.wait_ge(logits, u + 1)
                if u >= 2:
                    act.wait_ge(summed, u - 1)
                nc.scalar.activation(relu[:, u % 2, 0:n], p_logit[u % 4][:, 0:n], ACT.Relu).then_inc(rectified, 1)

        @block.vector
        def _(dve):
            nc.vector.memset(scores[:, AT[0]:AT[2]], 0.0).then_inc(masked, 1)
            nc.vector.memset(scores[:, AT[NTP] + KEYS_S:SCORES], FILL)
            dve.wait_ge(masked, 1)
            for t in range(2):
                nc.vector.memset(scores[0:CHUNK, AT[t] + WIDTH[t] - CHUNK:AT[t] + WIDTH[t]], UNSELECTED)
            dve.wait_ge(weighted, 1)
            for u, (t, c, n, h) in enumerate(units):
                dve.wait_ge(rectified, u + 1)
                dst, w = scores[:, AT[t] + c:AT[t] + c + n], weight[:, t, h:h + 1]
                if h == 0:
                    nc.vector.tensor_scalar(dst, relu[:, u % 2, 0:n], w, None, ALU.mult).then_inc(summed, 1)
                else:
                    dve.wait_ge(summed, u)
                    nc.vector.scalar_tensor_tensor(out=dst, in0=relu[:, u % 2, 0:n], scalar=w, in1=dst,
                                                   op0=ALU.mult, op1=ALU.add).then_inc(summed, 1)
            dve.wait_ge(summed, len(units))
            for t in range(2, NTP):
                nc.vector.memset(scores[0:CHUNK, AT[t] + WIDTH[t] - CHUNK:AT[t] + WIDTH[t]], INADMISSIBLE)

        @block.tensor
        def _(pe):
            for b in range(BATCH_S):
                pe.wait_ge(cache_in[b % 2], 32 * (b // 2 + 1))
                if b % 2 == 0 and b >= 4:
                    pe.wait_ge(keys_ready, b // 2 - 1)
                for c in range(2):
                    mm = nc.tensor.transpose(p_keys[(b // 2) % 2][:, b % 2, c * P:(c + 1) * P], cache[:, b % 2, c, :],
                                             const[:, IDENT, :])
                mm.then_inc(keys_turned, 1)
            for u, (t, c, n, h) in enumerate(units):
                if u >= 4:
                    pe.wait_ge(rectified, u - 3)
                if t < NTP:
                    nc.tensor.matmul(p_logit[u % 4][:, 0:n], qiT[:, h // 2, t * P:(t + 1) * P],
                                     qiT[:, 2 + h % 2, c:c + n], start=True, stop=True).then_inc(logits, 1)
                else:
                    pe.wait_ge(spread_ready, h + 1)
                    pe.wait_ge(keys_ready, BATCH_S // 2)
                    pe.wait_ge(new_keys, 2)
                    for b in range(BATCH_S):
                        mm = nc.tensor.matmul(p_logit[u % 4][:, 0:n], spread[:, h % 2, b * P:(b + 1) * P],
                                              keysT[:, b, :], start=(b == 0), stop=(b == BATCH_S - 1))
                    mm.then_inc(logits, 1)


def select_and_project(nc, hT_hi, hT_lo, w_in, scores, projected_d):
    NB = NC + HB + 2 * KD
    with Scope(nc, "sp_") as s:
        raw = s.sbuf("raw", [P, KD, P])
        w_hi, w_lo = s.sbuf("w_hi", [P, 2, KD, P], F32R), s.sbuf("w_lo", [P, 2, KD, P], F32R)
        stage = s.sbuf("stage", [P, 2, TOK])
        best = s.sbuf("best", [P, NT, 8])
        p_out = [s.psum(f"p_out{i}") for i in range(2 * NG)]
        names = ("w_raw", "w_split_hi", "w_split_lo", "projected", "copied", "stored0", "stored1")
        w_raw, w_split_hi, w_split_lo, projected, copied, stored0, stored1 = (
            s.sem(n) for n in names)
        stored = (stored0, stored1)
        w = w_in.rearrange("(k p) c -> p k c", p=P)
        block = s.block()
        first_gate = NC + HB

        @block.sync
        def _(sp):
            def load(n, column):
                if not known(n, 1):
                    sp.wait_ge(w_split_lo, n)
                sp.dma_start(raw[:], w[:, :, bass.ds(column, P)]).then_inc(w_raw, 16)

            in_steps(sp, lambda n, q: load(n, n * P + C_CONV), 0, first_gate)
            in_steps(sp, lambda n, q: load(n, (n - first_gate) * P + C_GATE), first_gate, NB)
            for q in range(2):
                sp.wait_ge(stored[q], 16 * (NB // 2))

        @block.scalar
        def _(act):
            def split(n, q):
                act.wait_ge(w_raw, 16 * n + 16)
                if not known(n, 2):
                    act.wait_ge(projected, NG * (n - 1))
                nc.scalar.copy(w_hi[:, q], raw[:]).then_inc(w_split_hi, 1)

            def step(n, q, func):
                if not known(n, 2):
                    act.wait_ge(stored[q], 8 * (n - q))
                for g in range(NG):
                    act.wait_ge(projected, NG * n + g + 1)
                    nc.scalar.activation(stage[:, q, g * TG:(g + 1) * TG], p_out[NG * q + g][:, 0:TG],
                                         func).then_inc(copied, 1)
                act.wait_ge(copied, NG * n + NG)
                act.dma_start(projected_d[bass.ds(n, 1)].rearrange("a p t -> p (a t)"), stage[:, q]).then_inc(stored[q], 16)
                if not known(n, NB) or n + 2 < NB:
                    split(n + 2, q)

            split(0, 0)
            split(1, 1)
            in_steps(act, lambda n, q: step(n, q, ACT.Copy), 0, NC, lead=2)
            in_steps(act, lambda n, q: step(n, q, ACT.Silu), NC, first_gate, lead=0)
            in_steps(act, lambda n, q: step(n, q, ACT.Sigmoid), first_gate, NB - 2, lead=0)
            in_steps(act, lambda n, q: step(n, q, ACT.Sigmoid), NB - 2, NB)

        @block.gpsimd
        def _(pool):
            def split(n, q):
                pool.wait_ge(w_split_hi, n + 1)
                nc.gpsimd.tensor_tensor(w_lo[:, q], raw[:], w_hi[:, q].bitcast(F32), ALU.subtract).then_inc(w_split_lo, 1)

            in_steps(pool, split, 0, NB)

        @block.vector
        def _(dve):
            def row(t):
                return scores[:, AT[t]:AT[t] + WIDTH[t] + (PAD_S if t == NTP else 0)]

            def find(tiles):
                for t in tiles:
                    nc.vector.max(best[:, t, :], row(t))
                dve.drain()

            def take(tiles):
                for t in tiles:
                    nc.vector.match_replace(row(t), best[:, t, :], row(t), TAKEN)
                dve.drain()

            for tiles in ((2, 3), (4, 5), (6, 7)):
                with dve.Fori(0, TOPK_P // 8):
                    find(tiles)
                    take(tiles)
            with dve.Fori(0, TOPK_S // 8):
                find([NTP])
                take([NTP])
            find([NTP])
            nc.vector.memset(best[:, NTP, TOPK_S % 8:8], FILL)
            dve.drain()
            take([NTP])
            todo = scores[:, AT[2]:SCORES]
            nc.vector.tensor_scalar(todo, todo, TAKEN, UNSELECTED, ALU.not_equal, ALU.mult)

        @block.tensor
        def _(pe):
            def step(n, q):
                pe.wait_ge(w_split_lo, n + 1)
                for g in range(NG):
                    if not known(n, 2):
                        pe.wait_ge(copied, NG * (n - 2) + g + 1)
                    mine = slice(g * TG, (g + 1) * TG)
                    three_passes(nc, p_out[NG * q + g][:, 0:TG], lambda k: (w_hi[:, q, k, :], w_lo[:, q, k, :]),
                                 lambda k: (hT_hi[:, k, mine], hT_lo[:, k, mine]), range(KD)).then_inc(projected, 1)

            in_steps(pe, step, 0, NB, lead=2)


def attend(nc, const, qkT, va, scores, cache_k, cache_v, attended_d):
    with Scope(nc, "at_") as s:
        parts, swapped = s.sbuf("parts", [P, KV, 5, SEQ], F32R), s.sbuf("swapped", [P, KV, SEQ], F32R)
        cache, keysT = s.sbuf("cache", [P, 2, 2, 2, P]), s.sbuf("keysT", [P, BATCH_S, KEYS_S])
        values, own_values = s.sbuf("values", [P, BATCH_S, 2, P]), s.sbuf("own_values", [SEQ_S, BATCH_S, P])
        spread = s.sbuf("spread", [P, BATCH_S, P])
        pick = s.sbuf("pick", [P, BATCH_S, P])
        masked, prob, probT = (s.sbuf(n, [P, 2 * SEQ]) for n in ("masked", "prob", "probT"))
        o_tok, oT = s.sbuf("o_tok", [P, 2, 512]), s.sbuf("oT", [P, 2, 4, P])
        o_dec, oT_dec = s.sbuf("o_dec", [P, 2, HD]), s.sbuf("oT_dec", [HD, HEADS, P])
        top, shift, total, rtotal = (s.sbuf(n, [P, 4]) for n in ("top", "shift", "total", "rtotal"))
        p_s = s.psum("p_s", (P, 2 * SEQ))
        p_pT = [s.psum(f"p_pT{i}", (P, 4, P)) for i in range(2)]
        p_o, p_oT = s.psum("p_o"), s.psum("p_oT", (P, 4, P))
        names = ("cache_in0", "cache_in1", "values_in", "own_in", "cleared", "spread_ready", "picks_ready", "keys_turned",
                 "keys_ready", "new_keys", "split_hi", "split_lo", "scored", "topped", "shifted", "exped", "prob_turned",
                 "probT_ready", "weighed", "inverted", "normed", "o_turned", "oT_ready", "stored0", "stored1", "stored_dec")
        (cache_in0, cache_in1, values_in, own_in, cleared, spread_ready, picks_ready, keys_turned, keys_ready, new_keys, split_hi,
         split_lo, scored, topped, shifted, exped, prob_turned, probT_ready, weighed, inverted, normed, o_turned,
         oT_ready, stored0, stored1, stored_dec) = (s.sem(n) for n in names)
        cache_in, stored = (cache_in0, cache_in1), (stored0, stored1)
        units = [(t, j, kv) for t in range(NTP) for j in range(4) for kv in range(KV)] + [
            (NTP, b, 0) for b in range(BATCH_S)]
        U, DEC = len(units), HEADS * NTP

        def cols(u):
            width = WIDTH[units[u][0]]
            at = (u % 2) * SEQ if width > 512 else (u % 4) * 512
            return at, width

        def same_place(u):
            def place(v):
                at, width = cols(v)
                return set(range(at // 512, (at + width + 511) // 512))
            return max([v + 1 for v in range(u) if place(v) & place(u)], default=0)

        def coming(slot):
            return [v for v in range(U) if max(v - (1 if cols(v)[1] > 512 else 2), -1) == slot]

        groups = [(1 if t == NTP else (WIDTH[t] // P + 3) // 4) for t, _, _ in units]
        before = [sum(groups[:u]) for u in range(U + 1)]
        own, other = (slice(0, HD), slice(HD, P)), (slice(HD, P), slice(0, HD))
        block = s.block()

        @block.sync
        def _(sp):
            for i in range(BATCH_S // 2):
                if i >= 2:
                    sp.wait_ge(keys_turned, i - 1)
                sp.dma_start(cache[:, i % 2], cache_k[0, 2 * i:2 * i + 2].rearrange(
                    "b (c p) n d -> p b c (n d)", p=P)).then_inc(cache_in[i % 2], 16)
            sp.dma_start(values[:], cache_v[0].rearrange("b (c p) n d -> p b c (n d)", p=P)).then_inc(values_in, 16)
            for b in range(BATCH_S):
                sp.dma_start(own_values[:, b, :], va[b * SEQ_S:(b + 1) * SEQ_S, NTP, :]).then_inc(own_in, 16)
            for t in range(NTP):
                sp.wait_ge(oT_ready, t + 1)
                sp.dma_start(attended_d[:, :, t * P:(t + 1) * P].rearrange("j p t -> p j t"), oT[:, t % 2]).then_inc(
                    stored[t % 2], 16)
            sp.wait_ge(oT_ready, NTP + 2)
            for i in range(HEADS):
                sp.dma_start(attended_d[i // 2, (i % 2) * HD:(i % 2 + 1) * HD, SEQ:TOK], oT_dec[:, i, :]).then_inc(
                    stored_dec, 16)
            for q in range(2):
                sp.wait_ge(stored[q], 16 * (NTP // 2))
            sp.wait_ge(stored_dec, 16 * HEADS)

        @block.gpsimd
        def _(pool):
            def split(t):
                mine = slice(t * P, (t + 1) * P)
                for kv in range(KV):
                    pool.wait_ge(split_hi, 2 * t + kv + 1)
                    if t or kv:
                        pool.wait_ge(split_lo, 4 * t + 2 * kv)
                    hi = parts[own[kv], kv, :, mine].bitcast(F32)
                    nc.gpsimd.tensor_tensor(parts[other[kv], kv, :, mine], qkT[own[kv], :, mine], hi,
                                            ALU.subtract).then_inc(split_lo, 1)
                    pool.wait_ge(split_lo, 4 * t + 2 * kv + 1)
                    nc.gpsimd.tensor_tensor(swapped[own[kv], kv, mine], qkT[own[kv], 4, mine],
                                            parts[own[kv], kv, 4, mine].bitcast(F32), ALU.subtract).then_inc(split_lo, 1)

            split(0)
            split(1)
            pool.wait_ge(split_lo, 8)
            nc.gpsimd.memset(spread[:], 0.0).then_inc(cleared, 1)
            pool.wait_ge(cleared, 1)
            for kv in range(KV):
                if kv:
                    pool.wait_ge(spread_ready, kv)
                nc.gpsimd.tensor_copy(
                    spread[own[kv], :, own[kv]].rearrange("p b (j c) -> p b j c", j=4),
                    qkT[own[kv], 0:4, SEQ:TOK].rearrange("p j (b c) -> p b j c", b=BATCH_S)).then_inc(spread_ready, 1)
            pool.wait_ge(spread_ready, KV)
            nc.gpsimd.tensor_copy(keysT[:, :, PAST:KEYS_S], qkT[:, 4, SEQ:TOK].rearrange(
                "p (b c) -> p b c", b=BATCH_S)).then_inc(new_keys, 1)
            nc.gpsimd.tensor_copy(pick[:].rearrange("p b (h c) -> p b h c", h=HEADS), const[:, IDENT, :].rearrange(
                "p (b a c) -> p b a c", b=BATCH_S, a=1).to_broadcast([P, BATCH_S, HEADS, SEQ_S])).then_inc(picks_ready, 1)
            pool.wait_ge(new_keys, 1)
            pool.wait_ge(picks_ready, 1)
            for t in range(2, NTP):
                split(t)

        @block.tensor
        def _(pe):
            def turn_cache(i):
                pe.wait_ge(cache_in[i % 2], 16 * (i // 2 + 1))
                if i:
                    pe.wait_ge(keys_ready, i)
                for k in range(4):
                    mm = nc.tensor.transpose(p_oT[:, k, :], cache[:, i % 2, k // 2, k % 2, :], const[:, IDENT, :])
                mm.then_inc(keys_turned, 1)

            def query_keys(u):
                t, j, kv = units[u]
                at, width = cols(u)
                if same_place(u):
                    pe.wait_ge(topped, same_place(u))
                    if same_place(u) > DEC:
                        pe.wait_ge(exped, same_place(u))
                if t < NTP:
                    pe.wait_ge(split_lo, 4 * t + 4)
                    queries = parts[:, kv, j, t * P:(t + 1) * P]
                    for c in range(0, width, 512):
                        keys = slice(c, min(c + 512, width))
                        out = p_s[:, at + keys.start:at + keys.stop]
                        nc.tensor.matmul(out, queries, parts[:, kv, 4, keys], start=True, stop=False)
                        mm = nc.tensor.matmul(out, queries, swapped[:, kv, keys], start=False, stop=True)
                else:
                    pe.wait_ge(spread_ready, KV)
                    pe.wait_ge(new_keys, 1)
                    pe.wait_ge(keys_ready, BATCH_S // 2)
                    out = p_s[:, at:at + KEYS_S]
                    nc.tensor.matmul(out, spread[:, j, :], keysT[:, j, :], start=True, stop=False)
                    pe.wait_ge(picks_ready, 1)
                    mm = nc.tensor.matmul(out, pick[:, j, :],
                        scores[:, AT[NTP]:AT[NTP] + KEYS_S], start=False, stop=True)
                mm.then_inc(scored, 1)

            def turn(u):
                at, width = cols(u)
                pe.wait_ge(exped, u + 1)
                n = (width + P - 1) // P
                for g in range(groups[u]):
                    if before[u] + g >= 2:
                        pe.wait_ge(probT_ready, before[u] + g - 1)
                    for k in range(4 * g, min(4 * g + 4, n)):
                        rows = min(P, width - k * P)
                        mm = nc.tensor.transpose(p_pT[(before[u] + g) % 2][0:rows, k - 4 * g, :],
                                                 prob[:, at + k * P:at + k * P + rows], const[:, IDENT, :])
                    mm.then_inc(prob_turned, 1)

            def weigh(u):
                t, j, kv = units[u]
                at, width = cols(u)
                pe.wait_ge(probT_ready, before[u + 1])
                if u >= 1:
                    pe.wait_ge(normed, u)
                if t == NTP:
                    pe.wait_ge(values_in, 16)
                    pe.wait_ge(own_in, 16 * BATCH_S)
                n = (width + P - 1) // P
                for k in range(n):
                    rows = min(P, width - k * P)
                    v = va[:, k, :] if t < NTP else values[:, j, k, :] if k < 2 else own_values[:, j, :]
                    mm = nc.tensor.matmul(p_o[:, 0:P], probT[0:rows, at + k * P:at + (k + 1) * P], v, start=(k == 0),
                                          stop=(k == n - 1))
                mm.then_inc(weighed, 1)

            def turn_out(t):
                pe.wait_ge(normed, HEADS * (t + 1))
                if t == 0:
                    pe.wait_ge(keys_ready, BATCH_S // 2)
                else:
                    pe.wait_ge(oT_ready, t)
                for j in range(4):
                    mm = nc.tensor.transpose(p_oT[:, j, :], o_tok[:, t % 2, j * P:(j + 1) * P], const[:, IDENT, :])
                mm.then_inc(o_turned, 1)

            def turn_out_dec(b):
                pe.wait_ge(normed, DEC + b + 1)
                if b % 4 == 0:
                    pe.wait_ge(oT_ready, NTP + b // 4)
                nc.tensor.transpose(p_oT[0:HD, b % 4, :], o_dec[:, b % 2, :], const[:, IDENT, :]).then_inc(o_turned, 1)

            for v in coming(-1):
                query_keys(v)
            for u in range(U):
                for v in coming(u):
                    query_keys(v)
                turn(u)
                if u >= 1:
                    weigh(u - 1)
                if 1 <= u <= BATCH_S // 2:
                    turn_cache(u - 1)
                if u % HEADS == 2 and HEADS < u <= DEC + 2:
                    turn_out(u // HEADS - 1)
                if u >= DEC + 3:
                    turn_out_dec(u - DEC - 3)
            weigh(U - 1)
            for b in range(BATCH_S - 3, BATCH_S):
                turn_out_dec(b)

        @block.vector
        def _(dve):
            def mask_and_top(u):
                t = units[u][0]
                at, width = cols(u)
                q = slice(u % 4, u % 4 + 1)
                dve.wait_ge(scored, u + 1)
                if max(same_place(u), u - 3) > 0:
                    dve.wait_ge(exped, max(same_place(u), u - 3))
                if t < NTP:
                    nc.vector.tensor_tensor_reduce(masked[:, at:at + width], p_s[:, at:at + width],
                                                   scores[:, AT[t]:AT[t] + width], 1.0, -3.4e38, ALU.add, ALU.max,
                                                   top[:, q]).then_inc(topped, 1)
                else:
                    nc.vector.tensor_reduce(top[:, q], p_s[:, at:at + width], AX.X, ALU.max).then_inc(topped, 1)
                dve.wait_ge(topped, u + 1)
                nc.vector.tensor_scalar(shift[:, q], top[:, q], -HD ** -0.5, None, ALU.mult).then_inc(shifted, 1)

            def norm(u):
                t, j, kv = units[u]
                q = slice(u % 4, u % 4 + 1)
                dve.wait_ge(exped, u + 1)
                nc.vector.reciprocal(rtotal[:, q], total[:, q]).then_inc(inverted, 1)
                dve.wait_ge(inverted, u + 1)
                dve.wait_ge(weighed, u + 1)
                if t < NTP:
                    head = j + 4 * kv
                    if u % HEADS == 0 and t >= 2:
                        dve.wait_ge(o_turned, t - 1)
                    nc.vector.tensor_scalar(o_tok[:, t % 2, head * HD:(head + 1) * HD], p_o[:, own[kv]], rtotal[:, q],
                                            None, ALU.mult).then_inc(normed, 1)
                else:
                    if j >= 2:
                        dve.wait_ge(o_turned, NTP + j - 1)
                    for half in own:
                        mul = nc.vector.tensor_scalar(o_dec[half, j % 2, :], p_o[half, half], rtotal[half, q], None,
                                                      ALU.mult)
                    mul.then_inc(normed, 1)

            for v in coming(-1):
                mask_and_top(v)
            for u in range(U):
                for v in coming(u):
                    mask_and_top(v)
                if u >= 1:
                    norm(u - 1)
            norm(U - 1)

        @block.scalar
        def _(act):
            def split(t):
                mine = slice(t * P, (t + 1) * P)
                for kv in range(KV):
                    nc.scalar.copy(swapped[other[kv], kv, mine], qkT[own[kv], 4, mine])
                    nc.scalar.copy(parts[own[kv], kv, :, mine], qkT[own[kv], :, mine]).then_inc(split_hi, 1)

            def exp(u):
                at, width = cols(u)
                q = slice(u % 4, u % 4 + 1)
                act.wait_ge(shifted, u + 1)
                if same_place(u):
                    act.wait_ge(prob_turned, before[same_place(u)])
                if u >= 4:
                    act.wait_ge(inverted, u - 3)
                src = masked if units[u][0] < NTP else p_s
                nc.scalar.activation(prob[:, at:at + width], src[:, at:at + width], ACT.Exp, bias=shift[:, q],
                                     scale=HD ** -0.5, accum_out=total[:, q]).then_inc(exped, 1)

            def keep_turned(u):
                at, width = cols(u)
                if same_place(u):
                    act.wait_ge(weighed, same_place(u))
                for g in range(groups[u]):
                    act.wait_ge(prob_turned, before[u] + g + 1)
                    bank = p_pT[(before[u] + g) % 2]
                    full = min(4, width // P - 4 * g)
                    first = at + 4 * g * P
                    if units[u][0] < NTP:
                        nc.scalar.copy(probT[:, first:first + full * P].rearrange("p (k q) -> p k q", k=full),
                                       bank[:, 0:full, :]).then_inc(probT_ready, 1)
                    else:
                        nc.scalar.copy(probT[:, first:first + full * P].rearrange("p (k q) -> p k q", k=full),
                                       bank[:, 0:full, :])
                        nc.scalar.copy(probT[0:SEQ_S, first + full * P:first + (full + 1) * P],
                                       bank[0:SEQ_S, full, :]).then_inc(probT_ready, 1)

            def keep_out(t):
                act.wait_ge(o_turned, t + 1)
                if t >= 2:
                    act.wait_ge(stored[t % 2], 16 * (t // 2))
                nc.scalar.copy(oT[:, t % 2], p_oT[:]).then_inc(oT_ready, 1)

            def keep_out_dec(i):
                act.wait_ge(o_turned, NTP + 4 * i + 4)
                nc.scalar.copy(oT_dec[:, :, 4 * i * SEQ_S:4 * (i + 1) * SEQ_S].rearrange("p h (b c) -> p b h c", b=4),
                               p_oT[0:HD].rearrange("p b (h c) -> p b h c", h=HEADS)).then_inc(oT_ready, 1)

            split(0)
            split(1)
            exp(0)
            for u in range(U):
                if u + 1 < U:
                    exp(u + 1)
                keep_turned(u)
                if 1 <= u <= BATCH_S // 2:
                    act.wait_ge(keys_turned, u)
                    nc.scalar.copy(keysT[:, 2 * u - 2:2 * u, 0:PAST].rearrange("p b (c s) -> p b c s", c=2),
                                   p_oT[:].rearrange("p (b c) s -> p b c s", b=2)).then_inc(keys_ready, 1)
                if u % HEADS == 0 and 2 <= u // HEADS + 2 < NTP:
                    split(u // HEADS + 2)
                if u % HEADS == 3 and HEADS < u <= DEC + 3:
                    keep_out(u // HEADS - 1)
                if u == DEC + 7:
                    keep_out_dec(0)
            keep_out_dec(1)


def convolve(nc, const, conv_w, state_conv, projected_d, conv_d, inv_norm, new_conv, new_conv_s):
    HIST = CONV_W - 1
    RUN_S = HIST + SEQ_S
    PAD = HIST + SEQ
    with Scope(nc, "cv_") as s:
        padded = s.sbuf("padded", [P, 2, PAD + BATCH_S * RUN_S])
        decode = s.sbuf("decode", [P, 2, P])
        acc, out, square = s.sbuf("acc", [P, 2, TOK]), s.sbuf("out", [P, 2, TOK]), s.sbuf("square", [P, 2, TOK])
        taps_in, state_in = s.sbuf("taps_in", [CONV_W * NC, P]), s.sbuf("state_in", [BATCH_S * HIST, CONV_CH])
        taps, state = s.sbuf("taps", [P, CONV_W, NC]), s.sbuf("state", [P, NC, BATCH_S * HIST])
        tail = s.sbuf("tail", [P, NC, HIST * (1 + BATCH_S)])
        tail_tok = s.sbuf("tail_tok", [HIST * (1 + BATCH_S), CONV_CH])
        mean, root = s.sbuf("mean", [P, NT, 2 * HB]), s.sbuf("root", [P, NT, 2 * HB])
        p_taps, p_state, p_sum = s.psum("p_taps"), s.psum("p_state"), s.psum("p_sum")
        p_tail = [s.psum(f"p_tail{i}") for i in range(3)]
        names = ("small_in", "small_turned", "small_ready", "raw_in0", "raw_in1", "cleared", "filled", "tailed", "conv_done",
                 "silu_done", "squared", "summed", "mean_ready", "rooted", "stored0", "stored1", "tail_turned", "tail_ready",
                 "tail_stored", "scaled")
        (small_in, small_turned, small_ready, raw_in0, raw_in1, cleared, filled, tailed, conv_done, silu_done, squared,
         summed, mean_ready, rooted, stored0, stored1, tail_turned, tail_ready, tail_stored, scaled) = (
            s.sem(n) for n in names)
        raw_in, stored = (raw_in0, raw_in1), (stored0, stored1)
        TAPS = CONV_W * 2
        block = s.block()

        def decode_part(n):
            return padded[:, n % 2, PAD:].rearrange("p (b c) -> p b c", b=BATCH_S)

        @block.sync
        def _(sp):
            sp.dma_start(taps_in[:], conv_w.rearrange("j (n p) -> (j n) p", p=P)).then_inc(small_in, 16)
            sp.dma_start(state_in[:], state_conv[0].rearrange("b j c -> (b j) c")).then_inc(small_in, 16)
            for n in range(NC):
                if n >= 2:
                    sp.wait_ge(conv_done, TAPS * (n - 1))
                    sp.wait_ge(tailed, n - 1)
                sp.dma_start(padded[:, n % 2, HIST:PAD], projected_d[n, :, 0:SEQ]).then_inc(raw_in[n % 2], 16)
                sp.dma_start(decode[:, n % 2], projected_d[n, :, SEQ:TOK]).then_inc(raw_in[n % 2], 16)
            sp.wait_ge(tail_ready, 3)
            sp.dma_start(new_conv[0, 0], tail_tok[0:HIST, :]).then_inc(tail_stored, 16)
            sp.dma_start(new_conv_s[0].rearrange("b j c -> (b j) c"), tail_tok[HIST:, :]).then_inc(tail_stored, 16)
            sp.wait_ge(tail_stored, 32)

        @block.gpsimd
        def _(pool):
            nc.gpsimd.memset(padded[:, :, 0:HIST], 0.0).then_inc(cleared, 1)
            pool.wait_ge(small_ready, 2)
            for n in range(NC):
                pool.wait_ge(raw_in[n % 2], 32 * (n // 2 + 1))
                dst = decode_part(n)
                nc.gpsimd.tensor_copy(dst[:, :, 0:HIST], state[:, n, :].rearrange("p (b j) -> p b j", b=BATCH_S))
                nc.gpsimd.tensor_copy(dst[:, :, HIST:RUN_S], decode[:, n % 2].rearrange(
                    "p (b c) -> p b c", b=BATCH_S)).then_inc(filled, 1)
                pool.wait_ge(filled, n + 1)
                nc.gpsimd.tensor_copy(tail[:, n, 0:HIST], padded[:, n % 2, PAD - HIST:PAD])
                nc.gpsimd.tensor_copy(tail[:, n, HIST:].rearrange("p (b j) -> p b j", b=BATCH_S),
                                      dst[:, :, SEQ_S:RUN_S]).then_inc(tailed, 1)

        @block.vector
        def _(dve):
            dve.wait_ge(small_turned, 2)
            nc.vector.tensor_copy(taps[:], p_taps[:, 0:CONV_W * NC].rearrange("p (j n) -> p j n", n=NC)).then_inc(
                small_ready, 1)
            nc.vector.tensor_copy(state[:], p_state[:, 0:NC * BATCH_S * HIST].rearrange(
                "p (n c) -> p n c", n=NC)).then_inc(small_ready, 1)
            dve.wait_ge(small_ready, 2)
            dve.wait_ge(cleared, 1)
            done = 0
            for n in range(NC):
                dve.wait_ge(filled, n + 1)
                if n >= 2:
                    dve.wait_ge(silu_done, n - 1)
                for j in range(CONV_W):
                    w = taps[:, j, n:n + 1]
                    pairs = ((acc[:, n % 2, 0:SEQ], padded[:, n % 2, j:j + SEQ]),
                             (acc[:, n % 2, SEQ:TOK].rearrange("p (b c) -> p b c", b=BATCH_S),
                              decode_part(n)[:, :, j:j + SEQ_S]))
                    for dst, src in pairs:
                        if j == 0:
                            nc.vector.tensor_scalar(dst, src, w, None, ALU.mult).then_inc(conv_done, 1)
                        else:
                            dve.wait_ge(conv_done, done - 1)
                            nc.vector.scalar_tensor_tensor(out=dst, in0=src, scalar=w, in1=dst, op0=ALU.mult,
                                                           op1=ALU.add).then_inc(conv_done, 1)
                        done += 1
            for i in range(3):
                dve.wait_ge(tail_turned, i + 1)
                nc.vector.tensor_copy(tail_tok[:, i * 512:(i + 1) * 512], p_tail[i][0:HIST * (1 + BATCH_S), :]).then_inc(
                    tail_ready, 1)
            dve.wait_ge(summed, 2 * HB)
            nc.vector.tensor_scalar(mean[:], p_sum[:, 0:NT * 2 * HB].rearrange("p (n t) -> p t n", t=NT), EPS, None,
                                    ALU.add).then_inc(mean_ready, 1)
            dve.wait_ge(rooted, 1)
            nc.vector.reciprocal(inv_norm[:], root[:]).then_inc(scaled, 1)
            dve.wait_ge(scaled, 1)
            nc.vector.tensor_scalar(inv_norm[:, :, 0:HB], inv_norm[:, :, 0:HB], DK ** -0.5, None, ALU.mult)

        @block.scalar
        def _(act):
            for n in range(NC):
                act.wait_ge(conv_done, TAPS * (n + 1))
                if n >= 2:
                    act.wait_ge(stored[n % 2], 16 * (n // 2))
                nc.scalar.activation(out[:, n % 2], acc[:, n % 2], ACT.Silu).then_inc(silu_done, 1)
                act.wait_ge(silu_done, n + 1)
                if n < 2 * HB:
                    if n >= 2:
                        act.wait_ge(summed, n - 1)
                    nc.scalar.activation(square[:, n % 2], out[:, n % 2], ACT.Square).then_inc(squared, 1)
                act.dma_start(conv_d[n], out[:, n % 2]).then_inc(stored[n % 2], 16)
            act.wait_ge(mean_ready, 1)
            nc.scalar.activation(root[:], mean[:], ACT.Sqrt).then_inc(rooted, 1)
            for q in range(2):
                act.wait_ge(stored[q], 16 * (NC // 2))

        @block.tensor
        def _(pe):
            pe.wait_ge(small_in, 32)
            nc.tensor.transpose(p_taps[:, 0:CONV_W * NC], taps_in[:], const[0:CONV_W * NC, IDENT, 0:CONV_W * NC]).then_inc(
                small_turned, 1)
            H = BATCH_S * HIST
            for n in range(NC):
                mm = nc.tensor.transpose(p_state[:, n * H:(n + 1) * H], state_in[:, n * P:(n + 1) * P],
                                         const[0:H, IDENT, 0:H])
            mm.then_inc(small_turned, 1)
            for n in range(2 * HB):
                pe.wait_ge(squared, n + 1)
                for t in range(NT):
                    mm = nc.tensor.matmul(p_sum[:, n * NT + t:n * NT + t + 1], square[:, n % 2, t * P:(t + 1) * P],
                                          const[:, ONES, 0:1], start=True, stop=True)
                mm.then_inc(summed, 1)
            pe.wait_ge(tailed, NC)
            for i in range(3):
                for n in range(4):
                    mm = nc.tensor.transpose(p_tail[i][0:HIST * (1 + BATCH_S), n * P:(n + 1) * P], tail[:, 4 * i + n, :],
                                             const[:, IDENT, :])
                mm.then_inc(tail_turned, 1)


def decays(nc, const, small, a_log, dt_bias, beta, g, cum, c_key, c_last, last_p, last_s):
    with Scope(nc, "dc_") as s:
        bias, rate = s.sbuf("bias", [P, HB]), s.sbuf("rate", [P, HB])
        a, absa, e, ln = (s.sbuf(n, [P, NT, HB]) for n in ("a", "absa", "e", "ln"))
        g_of = s.sbuf("g_of", [P, HB, BATCH_S])
        e_cum, diff = s.sbuf("e_cum", [P, NT, HB]), s.sbuf("diff", [P, NT, HB])
        p_cum, p_last, p_last_s = s.psum("p_cum"), s.psum("p_last"), s.psum("p_last_s")
        param_in, done_v, done_a, done_p = (s.sem(n) for n in ("param_in", "done_v", "done_a", "done_p"))
        NP = NTP * HB
        block = s.block()

        @block.sync
        def _(sp):
            sp.dma_start(bias[:], dt_bias.to_broadcast([P, HB])).then_inc(param_in, 16)
            sp.dma_start(rate[:], a_log.to_broadcast([P, HB])).then_inc(param_in, 16)

        @block.vector
        def _(dve):
            count = [0]

            def then(ins):
                count[0] += 1
                ins.then_inc(done_v, 1)
                dve.wait_ge(done_v, count[0])

            dve.wait_ge(param_in, 32)
            then(nc.vector.tensor_tensor(a[:], small[:, :, 8:12], bias[:].rearrange("p (a h) -> p a h", a=1).to_broadcast(
                [P, NT, HB]), ALU.add))
            then(nc.vector.scalar_tensor_tensor(out=absa[:], in0=a[:], scalar=-1.0, in1=a[:], op0=ALU.mult, op1=ALU.max))
            dve.wait_ge(done_a, 2)
            then(nc.vector.tensor_scalar(e[:], e[:], 1.0, None, ALU.add))
            then(nc.vector.tensor_scalar(a[:], a[:], 0.0, None, ALU.max))
            dve.wait_ge(done_a, 3)
            then(nc.vector.tensor_tensor(a[:], a[:], ln[:], ALU.add))
            then(nc.vector.tensor_scalar(rate[:], rate[:], -1.0, None, ALU.mult))
            then(nc.vector.tensor_tensor(g[:], a[:], rate[:].rearrange("p (a h) -> p a h", a=1).to_broadcast(
                [P, NT, HB]), ALU.mult))
            then(nc.vector.tensor_tensor(g_of[:], g[:, NTP, :].rearrange("p (h a) -> p h a", a=1).to_broadcast(
                [P, HB, BATCH_S]), const[:, BATCH_OF, 0:BATCH_S].rearrange("p (a b) -> p a b", a=1).to_broadcast(
                [P, HB, BATCH_S]), ALU.mult))
            dve.wait_ge(done_p, 1)
            then(nc.vector.tensor_copy(cum[:], p_cum[:, 0:NT * HB].rearrange("p (t h) -> p t h", h=HB)))
            then(nc.vector.tensor_tensor(diff[:], p_last[:, 0:NT * HB].rearrange("p (t h) -> p t h", h=HB), cum[:],
                                         ALU.subtract))
            dve.wait_ge(done_a, 5)
            nc.vector.scalar_tensor_tensor(out=c_key[:], in0=beta[:], scalar=-1.0, in1=e_cum[:], op0=ALU.mult,
                                           op1=ALU.mult)

        @block.scalar
        def _(act):
            act.wait_ge(param_in, 32)
            act.wait_ge(done_v, 2)
            nc.scalar.activation(e[:], absa[:], ACT.Exp, scale=-1.0).then_inc(done_a, 1)
            nc.scalar.activation(rate[:], rate[:], ACT.Exp).then_inc(done_a, 1)
            act.wait_ge(done_v, 3)
            nc.scalar.activation(ln[:], e[:], ACT.Ln).then_inc(done_a, 1)
            act.wait_ge(done_v, 9)
            nc.scalar.activation(e_cum[:], cum[:], ACT.Exp).then_inc(done_a, 1)
            act.wait_ge(done_v, 10)
            nc.scalar.activation(c_last[:], diff[:], ACT.Exp)
            nc.scalar.activation(last_p[:], p_last[:, 0:NP].rearrange("p (t h) -> p t h", h=HB), ACT.Exp)
            nc.scalar.activation(last_s[:], p_last_s[:, 0:HB * BATCH_S].rearrange("p (h b) -> p h b", h=HB), ACT.Exp)
            nc.scalar.activation(beta[:], small[:, :, 4:8], ACT.Sigmoid).then_inc(done_a, 1)

        @block.tensor
        def _(pe):
            pe.wait_ge(done_v, 8)
            prompt, own = g[:, 0:NTP, :].rearrange("p t h -> p (t h)"), g[:, NTP, :]
            nc.tensor.matmul(p_cum[:, 0:NP], const[:, UPTO, :], prompt, start=True, stop=True)
            nc.tensor.matmul(p_cum[:, NP:NP + HB], const[:, UPTO_S, :], own, start=True, stop=True)
            nc.tensor.matmul(p_last[:, 0:NP], const[:, ONES, :], prompt, start=True, stop=True)
            nc.tensor.matmul(p_last[:, NP:NP + HB], const[:, SAME_S, :], own, start=True, stop=True)
            nc.tensor.matmul(p_last_s[:, 0:HB * BATCH_S], const[:, ONES, :], g_of[:].rearrange("p h b -> p (h b)"),
                             start=True, stop=True).then_inc(done_p, 1)


def over_heads(ap, n=P):
    return ap.rearrange("p (h a) -> p h a", a=1).to_broadcast([P, ap.shape[-1], n])


def for_heads(ap, n):
    return ap.rearrange("p (a c) -> p a c", a=1).to_broadcast([P, n, ap.shape[-1]])


def delta(nc, const, beta, g, cum, c_key, c_last, last_p, last_s, inv_norm, conv_d, state_delta, out_d,
          new_state, new_state_s):
    with Scope(nc, "dl_") as s:
        H2 = HB // 2
        qkv = s.sbuf("qkv", [P, 2, NC, P])
        khat, qhat, kT, qT, e_row, gap, E_up, E_low, low, g_cols = (s.sbuf(n, [P, HB, P]) for n in (
            "khat", "qhat", "kT", "qT", "e_row", "gap", "E_up", "E_low", "low", "g_cols"))
        Z = s.sbuf("Z", [P, HB, P])
        below = s.sbuf("below", [P, 2, LEVELS_P, HB, P])
        X, vb, kbg, kdec, qTe, attn, Y, wT = (s.sbuf(n, [P, 2, HB, P]) for n in (
            "X", "vb", "kbg", "kdec", "qTe", "attn", "Y", "wT"))
        V, S = s.sbuf("V", [P, HB, P]), s.sbuf("S", [P, HB, P])
        outT = s.sbuf("outT", [P, 2, HB, P])
        S_s = s.sbuf("S_s", [P, BATCH_S, HB, P])
        VT, V_of = s.sbuf("VT", [P, HB, P]), s.sbuf("V_of", [P, 2, BATCH_S, P])
        S_new = s.sbuf("S_new", [P, 2, BATCH_S, P])
        p_z, p_yx = ([s.psum(f"p_{n}{p}", (P, 4, P)) for p in range(2)] for n in ("z", "yx"))
        front_0, front_1, p_v, p_o = (s.psum(n, (P, HB, P)) for n in ("front_0", "front_1", "p_v", "p_o"))

        (k_turned, q_turned, v_turned, khat_turned, qhat_turned, rows_done, gram_k, gram_q, b0_turned, khat_ready,
         qhat_ready, vb_ready, kT_kept, qT_kept, gap_ready, clamped, e_row_done, e_done, low_ready, attn_ready,
         y_first, x_first, k_scaled, k_faded, q_scaled, attn_masked, g_spread) = (s.sem(n) for n in (
             "k_turned", "q_turned", "v_turned", "khat_turned", "qhat_turned", "rows_done", "gram_k", "gram_q",
             "b0_turned", "khat_ready", "qhat_ready", "vb_ready", "kT_kept", "qT_kept", "gap_ready", "clamped",
             "e_row_done", "e_done", "low_ready", "attn_ready", "y_first", "x_first", "k_scaled", "k_faded",
             "q_scaled", "attn_masked", "g_spread"))
        b_made = s.sem("b_made")
        z_done, z_kept, y_done, y_kept, x_done, x_kept, w_done, w_kept = ([s.sem(f"{n}{p}") for p in range(2)] for n in (
            "z_done", "z_kept", "y_done", "y_kept", "x_done", "x_kept", "w_done", "w_kept"))
        v_done, v_kept, o_done, o_kept, s_done, s_kept, cleared, final_stored = (s.sem(n) for n in (
            "v_done", "v_kept", "o_done", "o_kept", "s_done", "s_kept", "cleared", "final_stored"))
        state_in, vt_done, vt_kept, v_spread, ss_done, ss_kept = (s.sem(n) for n in (
            "state_in", "vt_done", "vt_kept", "v_spread", "ss_done", "ss_kept"))
        qkv_in, out_stored, new_stored = ([s.sem(f"{n}{q}") for q in range(2)] for n in (
            "qkv_in", "out_stored", "new_stored"))
        LP, LS = LEVELS_P, LEVELS_S
        STATE_AT = 5
        pair = [slice(H2 * p, H2 * p + H2) for p in range(2)]
        block = s.block()

        @block.sync
        def _(sp):
            def load(m, q):
                if not known(m, 2):
                    sp.wait_ge(v_turned, m - 1)
                sp.dma_start(qkv[:, q], conv_d[:, :, bass.ts(m, P)].rearrange("n p t -> p n t")).then_inc(qkv_in[q], 16)

            def store(n, q):
                sp.wait_ge(o_kept, n + 1)
                sp.dma_start(out_d[:, :, bass.ts(n, P)].rearrange("n p t -> p n t"), outT[:, q]).then_inc(
                    out_stored[q], 16)

            load(0, 0)
            load(1, 1)
            sp.dma_start(S_s[:], state_delta[0].rearrange("b h k v -> k b h v")).then_inc(state_in, 16)

            def step(n, q):
                load(n + 1, 1 - q)
                store(n - 1, 1 - q)

            in_steps(sp, step, 1, NTP)
            store(NTP - 1, 1)
            sp.wait_ge(s_kept, NTP)
            sp.dma_start(new_state[0, 0].rearrange("h k v -> k h v"), S[:]).then_inc(final_stored, 16)
            store(NTP, 0)
            for h in range(HB):
                sp.wait_ge(ss_kept, 2 * (h + 1))
                sp.dma_start(new_state_s[0, :, h].rearrange("b k v -> k b v"), S_new[:, h % 2]).then_inc(
                    new_stored[h % 2], 16)
            sp.wait_ge(final_stored, 16)
            for q in range(2):
                sp.wait_ge(new_stored[q], 32)
                sp.wait_ge(out_stored[q], 16 * ((NT + 1 - q) // 2))

        @block.tensor
        def _(pe):
            ident = const[:, IDENT, :]

            def turn_in(m, q, bank, at, done):
                pe.wait_ge(qkv_in[q], 8 * (m - q) + 16)
                for h in range(HB):
                    mm = nc.tensor.transpose(bank[:, h, :], qkv[:, q, at + h, :], ident)
                mm.then_inc(done, 1)

            def rows_and_k(m, q, decode):
                pe.wait_ge(g_spread, m + 1)
                if not known(m, 1):
                    pe.wait_ge(attn_ready, m)
                    pe.wait_ge(y_first, m)
                for h in range(HB):
                    mm = nc.tensor.matmul(front_1[:, h, :], g_cols[:, h, :], const[:, UPTO_S if decode else UPTO, :],
                                          start=True, stop=True)
                mm.then_inc(rows_done, 1)
                turn_in(m, q, front_0, HB, k_turned)

            def q_and_v(m, q):
                pe.wait_ge(e_row_done, m + 1)
                turn_in(m, q, front_1, 0, q_turned)
                pe.wait_ge(khat_ready, m + 1)
                turn_in(m, q, front_0, 2 * HB, v_turned)

            def turn_hats(m):
                pe.wait_ge(khat_ready, m + 1)
                pe.wait_ge(qhat_ready, m + 1)
                for h in range(HB):
                    mm = nc.tensor.transpose(front_1[:, h, :], khat[:, h, :], ident)
                mm.then_inc(khat_turned, 1)
                pe.wait_ge(vb_ready, m + 1)
                for h in range(HB):
                    mm = nc.tensor.transpose(front_0[:, h, :], qhat[:, h, :], ident)
                mm.then_inc(qhat_turned, 1)

            def grams_k(m):
                pe.wait_ge(kT_kept, m + 1)
                pe.wait_ge(qT_kept, m + 1)
                for h in range(HB):
                    mm = nc.tensor.matmul(front_0[:, h, :], kT[:, h, :], kT[:, h, :], start=True, stop=True)
                mm.then_inc(gram_k, 1)

            def grams_q(m):
                for h in range(HB):
                    mm = nc.tensor.matmul(front_1[:, h, :], kT[:, h, :], qT[:, h, :], start=True, stop=True)
                mm.then_inc(gram_q, 1)

            def turn_first(m, q):
                pe.wait_ge(b_made, LP * m + 1)
                pe.wait_ge(low_ready, m + 1)
                for h in range(HB):
                    mm = nc.tensor.transpose(front_0[:, h, :], below[:, q, 0, h, :], ident)
                mm.then_inc(b0_turned, 1)

            def z(n, q, i, p):
                if i == 1:
                    pe.wait_ge(y_first, n + 1)
                    if not known(n, 1):
                        pe.wait_ge(w_kept[p], n)
                else:
                    pe.wait_ge(y_kept[p], (LP - 1) * n + i - 1)
                pe.wait_ge(b_made, LP * n + i + 1)
                for h in range(H2):
                    mm = nc.tensor.matmul(p_z[p][:, h, :], below[:, q, i, H2 * p + h, :], Y[:, q, H2 * p + h, :],
                                          start=True, stop=True)
                mm.then_inc(z_done[p], 1)

            def y(n, q, i, p):
                pe.wait_ge(z_kept[p], (LP - 1) * n + i)
                if i == 1:
                    pe.wait_ge(x_first, n + 1)
                else:
                    pe.wait_ge(x_kept[p], (LP - 2) * n + i - 1)
                for h in range(H2):
                    mm = nc.tensor.matmul(p_yx[p][:, h, :], X[:, q, H2 * p + h, :], Z[:, H2 * p + h, :], start=True,
                                          stop=True)
                mm.then_inc(y_done[p], 1)

            def x(n, q, i, p):
                pe.wait_ge(y_kept[p], (LP - 1) * n + i)
                for h in range(H2):
                    mm = nc.tensor.matmul(p_yx[p][:, H2 + h, :], Z[:, H2 * p + h, :], X[:, q, H2 * p + h, :], start=True,
                                          stop=True)
                mm.then_inc(x_done[p], 1)

            def weights(n, q, levels):
                pe.wait_ge(k_scaled, n + 1)
                for p in range(2):
                    pe.wait_ge(y_kept[p], (LP - 1) * n + levels - 1)
                    for h in range(H2):
                        mm = nc.tensor.matmul(p_z[p][:, h, :], kbg[:, q, H2 * p + h, :], Y[:, q, H2 * p + h, :],
                                              start=True, stop=True)
                    mm.then_inc(w_done[p], 1)

            def new_values(n, q):
                for p in range(2):
                    pe.wait_ge(w_kept[p], n + 1)
                if known(n, 1):
                    pe.wait_ge(cleared, 1)
                else:
                    pe.wait_ge(s_kept, n)
                for h in range(HB):
                    nc.tensor.matmul(p_v[:, h, :], Y[:, q, h, :], vb[:, q, h, :], start=True, stop=False)
                    mm = nc.tensor.matmul(p_v[:, h, :], wT[:, q, h, :], S[:, h, :], start=False, stop=True)
                mm.then_inc(v_done, 1)

            def outputs(n, q):
                pe.wait_ge(v_kept, n + 1)
                if not known(n, 1):
                    pe.wait_ge(o_kept, n)
                pe.wait_ge(q_scaled, n + 1)
                pe.wait_ge(attn_masked, n + 1)
                for h in range(HB):
                    nc.tensor.matmul(p_o[:, h, :], S[:, h, :], qTe[:, q, h, :], start=True, stop=False)
                    mm = nc.tensor.matmul(p_o[:, h, :], V[:, h, :], attn[:, q, h, :], start=False, stop=True)
                mm.then_inc(o_done, 1)

            def state(n, q):
                pe.wait_ge(k_faded, n + 1)
                pe.wait_ge(v_kept, n + 1)
                for h in range(HB):
                    mm = nc.tensor.matmul(p_v[:, h, :], kdec[:, q, h, :], V[:, h, :], start=True, stop=True)
                mm.then_inc(s_done, 1)

            def step(n, q, ahead="prompt"):
                levels = LP if ahead else LS
                for i in range(1, levels):
                    z(n, q, i, 0)
                    if i > 1:
                        x(n, q, i - 1, 1)
                    z(n, q, i, 1)
                    if ahead and i == 1:
                        rows_and_k(n + 1, 1 - q, ahead == "decode")
                    if ahead and i == 2:
                        q_and_v(n + 1, 1 - q)
                    if ahead and i == 3:
                        turn_hats(n + 1)
                    if ahead and i == 4:
                        grams_k(n + 1)
                    if ahead and i == 6:
                        turn_first(n + 1, 1 - q)
                    y(n, q, i, 0)
                    y(n, q, i, 1)
                    if not known(n, 1):
                        if i == 1:
                            new_values(n - 1, 1 - q)
                        if i == 2:
                            outputs(n - 1, 1 - q)
                        if i == min(STATE_AT, levels - 1):
                            state(n - 1, 1 - q)
                    if ahead and i == 4:
                        grams_q(n + 1)
                    if i < levels - 1:
                        x(n, q, i, 0)
                weights(n, q, levels)

            rows_and_k(0, 0, False)
            q_and_v(0, 0)
            turn_hats(0)
            grams_k(0)
            grams_q(0)
            turn_first(0, 0)
            in_steps(pe, step, 0, NTP - 1)
            step(NTP - 1, 1, "decode")
            step(NTP, 0, None)
            for p in range(2):
                pe.wait_ge(w_kept[p], NT)
            pe.wait_ge(q_scaled, NT)
            pe.wait_ge(attn_masked, NT)
            pe.wait_ge(k_faded, NT)
            pe.wait_ge(s_kept, NTP)
            pe.wait_ge(state_in, 16)
            for h in range(HB):
                nc.tensor.matmul(p_v[:, h, :], vb[:, 0, h, :], Y[:, 0, h, :], start=True, stop=False)
                for b in range(BATCH_S):
                    mine = slice(b * SEQ_S, (b + 1) * SEQ_S)
                    mm = nc.tensor.matmul(p_v[:, h, mine], S_s[:, b, h, :], wT[:, 0, h, mine], start=False,
                                          stop=(b == BATCH_S - 1))
            mm.then_inc(vt_done, 1)
            pe.wait_ge(vt_kept, 1)
            for h in range(HB):
                mm = nc.tensor.transpose(p_v[:, h, :], VT[:, h, :], ident)
            mm.then_inc(v_done, 1)
            pe.wait_ge(v_kept, NT)
            pe.wait_ge(o_kept, NTP)
            for h in range(HB):
                nc.tensor.matmul(p_o[:, h, :], V[:, h, :], attn[:, 0, h, :], start=True, stop=False)
                for b in range(BATCH_S):
                    mine = slice(b * SEQ_S, (b + 1) * SEQ_S)
                    mm = nc.tensor.matmul(p_o[:, h, mine], S_s[:, b, h, :], qTe[:, 0, h, mine], start=False,
                                          stop=(b == BATCH_S - 1))
            mm.then_inc(o_done, 1)
            for h in range(HB):
                pe.wait_ge(v_spread, h + 1)
                for c, bank in enumerate((front_0, front_1)):
                    if h >= 1:
                        pe.wait_ge(ss_kept, 2 * (h - 1) + c + 1)
                    nc.tensor.matmul(bank[:], kdec[:, 0, h, :], V_of[:, h % 2, 4 * c:4 * c + 4, :], start=True,
                                     stop=True).then_inc(ss_done, 1)

        @block.vector
        def _(dve):
            def gaps(m):
                dve.wait_ge(rows_done, m + 1)
                nc.vector.tensor_tensor(gap[:], front_1[:], over_heads(cum[:, m, :]), ALU.subtract).then_inc(gap_ready, 1)
                dve.wait_ge(gap_ready, m + 1)
                nc.vector.tensor_scalar(E_up[:], gap[:], 0.0, None, ALU.min)
                nc.vector.tensor_scalar(E_low[:], gap[:], -1.0, 0.0, ALU.mult, ALU.min).then_inc(clamped, 1)

            def hat_k(m):
                dve.wait_ge(k_turned, m + 1)
                if not known(m, 1):
                    dve.wait_ge(khat_turned, m)
                    dve.wait_ge(k_scaled, m)
                    dve.wait_ge(k_faded, m)
                nc.vector.tensor_tensor(khat[:], front_0[:], over_heads(inv_norm[:, m, HB:2 * HB]), ALU.mult).then_inc(
                    khat_ready, 1)

            def hat_q_and_v(m, q):
                dve.wait_ge(q_turned, m + 1)
                if not known(m, 1):
                    dve.wait_ge(qhat_turned, m)
                nc.vector.tensor_tensor(qhat[:], front_1[:], over_heads(inv_norm[:, m, 0:HB]), ALU.mult).then_inc(
                    qhat_ready, 1)
                dve.wait_ge(v_turned, m + 1)
                if not known(m, 2):
                    dve.wait_ge(v_done, m - 1)
                nc.vector.tensor_tensor(vb[:, q], front_0[:], over_heads(beta[:, m, :]), ALU.mult).then_inc(vb_ready, 1)

            def lower(m):
                dve.wait_ge(gram_k, m + 1)
                dve.wait_ge(e_done, m + 1)
                if not known(m, 1):
                    dve.wait_ge(b_made, LP * m)
                for h in range(HB):
                    ins = nc.vector.scalar_tensor_tensor(out=low[:, h, :], in0=front_0[:, h, :], scalar=beta[:, m, h:h + 1],
                                                         in1=E_low[:, h, :], op0=ALU.mult, op1=ALU.mult)
                ins.then_inc(low_ready, 1)

            def attend_in_tile(m, q):
                dve.wait_ge(gram_q, m + 1)
                if not known(m, 2):
                    dve.wait_ge(o_done, m - 1)
                nc.vector.tensor_tensor(attn[:, q], front_1[:], E_up[:], ALU.mult).then_inc(attn_ready, 1)

            def first_y(m, q):
                dve.wait_ge(b0_turned, m + 1)
                if not known(m, 2):
                    dve.wait_ge(v_done, m - 1)
                nc.vector.tensor_tensor(Y[:, q], for_heads(const[:, IDENT, :], HB), front_0[:], ALU.subtract).then_inc(
                    y_first, 1)

            def keep_y(n, q, i, p):
                dve.wait_ge(y_done[p], (LP - 1) * n + i)
                if i == 1:
                    dve.wait_ge(y_first, n + 1)
                else:
                    dve.wait_ge(y_kept[p], (LP - 1) * n + i - 1)
                nc.vector.tensor_tensor(Y[:, q, pair[p]], Y[:, q, pair[p]], p_yx[p][:, 0:H2], ALU.subtract).then_inc(
                    y_kept[p], 1)

            def keep_x(n, q, i, p):
                dve.wait_ge(x_done[p], (LP - 2) * n + i)
                if i == 1:
                    dve.wait_ge(x_first, n + 1)
                else:
                    dve.wait_ge(x_kept[p], (LP - 2) * n + i - 1)
                nc.vector.tensor_tensor(X[:, q, pair[p]], X[:, q, pair[p]], p_yx[p][:, H2:2 * H2], ALU.subtract).then_inc(
                    x_kept[p], 1)

            def next_state(n):
                dve.wait_ge(s_done, n + 1)
                dve.wait_ge(o_done, n + 1)
                if known(n, 1):
                    dve.wait_ge(cleared, 1)
                else:
                    dve.wait_ge(s_kept, n)
                for h in range(HB):
                    ins = nc.vector.scalar_tensor_tensor(out=S[:, h, :], in0=S[:, h, :], scalar=last_p[:, n, h:h + 1],
                                                         in1=p_v[:, h, :], op0=ALU.mult, op1=ALU.add)
                ins.then_inc(s_kept, 1)

            def step(n, q, ahead="prompt"):
                levels = LP if ahead else LS
                for i in range(1, levels):
                    if i > 1:
                        keep_x(n, q, i - 1, 1)
                    if ahead and i == 5:
                        attend_in_tile(n + 1, 1 - q)
                    if i == STATE_AT + 1 and not known(n, 1):
                        next_state(n - 1)
                    keep_y(n, q, i, 0)
                    keep_y(n, q, i, 1)
                    if i < levels - 1:
                        keep_x(n, q, i, 0)
                    if ahead and i == 1:
                        gaps(n + 1)
                        hat_k(n + 1)
                    if ahead and i == 2:
                        hat_q_and_v(n + 1, 1 - q)
                    if ahead and i == 4:
                        lower(n + 1)
                    if ahead and i == 6:
                        first_y(n + 1, 1 - q)
                if not ahead:
                    next_state(n - 1)

            gaps(0)
            hat_k(0)
            hat_q_and_v(0, 0)
            lower(0)
            attend_in_tile(0, 0)
            first_y(0, 0)
            in_steps(dve, step, 0, NTP - 1)
            step(NTP - 1, 1, "decode")
            step(NTP, 0, None)
            for h in range(HB):
                if h == 0:
                    dve.wait_ge(v_kept, NT)
                if h >= 2:
                    dve.wait_ge(ss_done, 2 * (h - 1))
                nc.vector.tensor_tensor(V_of[:, h % 2], for_heads(V[:, h, :], BATCH_S),
                                        over_heads(const[:, BATCH_OF, 0:BATCH_S]), ALU.mult).then_inc(v_spread, 1)
                if h >= 1:
                    decode_state(nc, dve, h - 1, S_new, S_s, last_s, (front_0, front_1), ss_done, ss_kept, new_stored)
            decode_state(nc, dve, HB - 1, S_new, S_s, last_s, (front_0, front_1), ss_done, ss_kept, new_stored)

        @block.scalar
        def _(act):
            def row_exp(m):
                act.wait_ge(gap_ready, m + 1)
                if not known(m, 1):
                    act.wait_ge(q_scaled, m)
                nc.scalar.activation(e_row[:], front_1[:], ACT.Exp).then_inc(e_row_done, 1)

            def exps(m):
                act.wait_ge(clamped, m + 1)
                nc.scalar.activation(E_up[:], E_up[:], ACT.Exp)
                nc.scalar.activation(E_low[:], E_low[:], ACT.Exp).then_inc(e_done, 1)

            def keep_hats(m):
                act.wait_ge(khat_turned, m + 1)
                if not known(m, 1):
                    act.wait_ge(gram_q, m)
                nc.scalar.copy(kT[:], front_1[:]).then_inc(kT_kept, 1)
                act.wait_ge(qhat_turned, m + 1)
                if not known(m, 1):
                    act.wait_ge(q_scaled, m)
                nc.scalar.copy(qT[:], front_0[:]).then_inc(qT_kept, 1)

            def keep_z(n, i, p):
                act.wait_ge(z_done[p], (LP - 1) * n + i)
                nc.scalar.copy(Z[:, pair[p]], p_z[p][:, 0:H2]).then_inc(z_kept[p], 1)

            def keep_values(n):
                act.wait_ge(v_done, n + 1)
                nc.scalar.copy(V[:], p_v[:]).then_inc(v_kept, 1)

            def keep_outputs(n, q):
                act.wait_ge(o_done, n + 1)
                if not known(n, 2):
                    act.wait_ge(out_stored[q], 8 * (n - q))
                nc.scalar.copy(outT[:, q], p_o[:]).then_inc(o_kept, 1)

            def step(n, q, ahead="prompt"):
                levels = LP if ahead else LS
                for i in range(1, levels):
                    if i == 2 and not known(n, 1):
                        keep_values(n - 1)
                    if i == 3 and not known(n, 1):
                        keep_outputs(n - 1, 1 - q)
                    keep_z(n, i, 0)
                    keep_z(n, i, 1)
                    if ahead and i == 1:
                        row_exp(n + 1)
                    if ahead and i == 2:
                        exps(n + 1)
                    if ahead and i == 3:
                        keep_hats(n + 1)
                for p in range(2):
                    act.wait_ge(w_done[p], n + 1)
                    nc.scalar.copy(wT[:, q, pair[p]], p_z[p][:, 0:H2]).then_inc(w_kept[p], 1)

            row_exp(0)
            exps(0)
            keep_hats(0)
            in_steps(act, step, 0, NTP - 1)
            step(NTP - 1, 1, "decode")
            step(NTP, 0, None)
            act.wait_ge(vt_done, 1)
            nc.scalar.copy(VT[:], p_v[:]).then_inc(vt_kept, 1)
            keep_values(NTP)
            keep_outputs(NTP, 0)

        @block.gpsimd
        def _(pool):
            nc.gpsimd.memset(S[:], 0.0).then_inc(cleared, 1)

            def spread_g(m):
                if not known(m, 1):
                    pool.wait_ge(rows_done, m)
                nc.gpsimd.tensor_tensor(g_cols[:], over_heads(g[:, m, :]), for_heads(const[:, ONES, :], HB),
                                        ALU.mult).then_inc(g_spread, 1)

            def front(m, q, decode=False):
                levels = LS if decode else LP
                pool.wait_ge(khat_ready, m + 1)
                if not known(m, 2):
                    for p in range(2):
                        pool.wait_ge(w_done[p], m - 1)
                nc.gpsimd.tensor_tensor(kbg[:, q], khat[:], over_heads(c_key[:, m, :]), ALU.mult).then_inc(k_scaled, 1)
                if not decode:
                    spread_g(m + 1)
                pool.wait_ge(low_ready, m + 1)
                if not known(m, 2):
                    for p in range(2):
                        pool.wait_ge(y_done[p], (LP - 1) * (m - 1))

                def blocks(i):
                    nc.gpsimd.tensor_tensor(below[:, q, i], low[:], for_heads(const[:, LEVEL + i, :], HB),
                                            ALU.mult).then_inc(b_made, 1)

                blocks(0)
                blocks(1)
                pool.wait_ge(b_made, LP * m + 1)
                nc.gpsimd.tensor_tensor(X[:, q], for_heads(const[:, IDENT, :], HB), below[:, q, 0],
                                        ALU.subtract).then_inc(x_first, 1)
                for i in range(2, levels):
                    blocks(i)
                pool.wait_ge(qT_kept, m + 1)
                pool.wait_ge(e_row_done, m + 1)
                if not known(m, 2):
                    pool.wait_ge(s_done, m - 1)
                nc.gpsimd.tensor_tensor(qTe[:, q], qT[:], e_row[:], ALU.mult).then_inc(q_scaled, 1)
                pool.wait_ge(attn_ready, m + 1)
                nc.gpsimd.tensor_tensor(attn[:, q], attn[:, q], for_heads(const[:, UPTO_S if decode else UPTO, :], HB),
                                        ALU.mult).then_inc(attn_masked, 1)
                nc.gpsimd.tensor_tensor(kdec[:, q], khat[:], over_heads(c_last[:, m, :]), ALU.mult).then_inc(k_faded, 1)

            spread_g(0)
            in_steps(pool, front, 0, NTP)
            front(NTP, 0, True)


def decode_state(nc, dve, h, S_new, S_s, last_s, bank, ss_done, ss_kept, new_stored):
    for c in range(2):
        dve.wait_ge(ss_done, 2 * h + c + 1)
        if h >= 2:
            dve.wait_ge(new_stored[h % 2], 16)
        for b in range(4 * c, 4 * c + 4):
            ins = nc.vector.scalar_tensor_tensor(out=S_new[:, h % 2, b, :], in0=S_s[:, b, h, :],
                                                 scalar=last_s[:, h, b:b + 1],
                                                 in1=bank[c][:, b % 4, :], op0=ALU.mult,
                                                 op1=ALU.add)
        ins.then_inc(ss_kept, 1)


def split_branches(nc, const, delta_norm, attended_d, out_d, projected_d, a_hi, a_lo, b_hi, b_lo):
    with Scope(nc, "sb_") as s:
        att, o, z = s.sbuf("att", [P, 2, TOK]), s.sbuf("o", [P, 2, TOK]), s.sbuf("z", [P, 2, TOK])
        square, mean, root, normed = (s.sbuf(n, [P, TOK]) for n in ("square", "mean", "root", "normed"))
        gain = s.sbuf("gain", [P, 1])
        p_sum = [s.psum(f"p_sum{i}") for i in range(NG)]
        gain_in = s.sem("gain_in")
        a_in, o_in, z_in = ((s.sem(f"{n}0"), s.sem(f"{n}1")) for n in ("a_in", "o_in", "z_in"))
        (a_hi_done, a_lo_done, squared, summed, averaged, rooted, inverted, scaled, gated, hi_done, lo_done) = (
            s.sem(n) for n in ("a_hi_done", "a_lo_done", "squared", "summed", "averaged", "rooted", "inverted", "scaled",
                               "gated", "hi_done", "lo_done"))
        block = s.block()

        @block.sync
        def _(sp):
            sp.dma_start(gain[:], delta_norm.rearrange("(p a) -> p a", a=1)).then_inc(gain_in, 16)
            for h in range(HB):
                if h >= 2:
                    sp.wait_ge(lo_done, h - 1)
                    sp.wait_ge(a_lo_done, h - 1)
                sp.dma_start(o[:, h % 2], out_d[h]).then_inc(o_in[h % 2], 16)
                sp.dma_start(z[:, h % 2], projected_d[NC + h]).then_inc(z_in[h % 2], 16)
                sp.dma_start(att[:, h % 2], attended_d[h]).then_inc(a_in[h % 2], 16)

        @block.scalar
        def _(act):
            for h in range(HB):
                turn = 16 * (h // 2 + 1)
                act.wait_ge(o_in[h % 2], turn)
                if h >= 1:
                    act.wait_ge(summed, NG * h)
                nc.scalar.activation(square[:], o[:, h % 2], ACT.Square).then_inc(squared, 1)
                act.wait_ge(a_in[h % 2], turn)
                nc.scalar.copy(a_hi[:, h], att[:, h % 2]).then_inc(a_hi_done, 1)
                act.wait_ge(averaged, NG * (h + 1))
                nc.scalar.activation(root[:], mean[:], ACT.Sqrt).then_inc(rooted, 1)
                act.wait_ge(gated, h + 1)
                nc.scalar.copy(b_hi[:, h], normed[:]).then_inc(hi_done, 1)

        @block.tensor
        def _(pe):
            for h in range(HB):
                pe.wait_ge(squared, h + 1)
                for g in range(NG):
                    if h >= 1:
                        pe.wait_ge(averaged, NG * (h - 1) + g + 1)
                    nc.tensor.matmul(p_sum[g][:, 0:TG], const[:, ONES, :], square[:, g * TG:(g + 1) * TG], start=True,
                                     stop=True).then_inc(summed, 1)

        @block.vector
        def _(dve):
            dve.wait_ge(gain_in, 16)
            for h in range(HB):
                for g in range(NG):
                    dve.wait_ge(summed, NG * h + g + 1)
                    nc.vector.tensor_scalar(mean[:, g * TG:(g + 1) * TG], p_sum[g][:, 0:TG], 1.0 / P, EPS, ALU.mult,
                                            ALU.add).then_inc(averaged, 1)
                dve.wait_ge(a_hi_done, h + 1)
                nc.vector.tensor_tensor(a_lo[:, h], att[:, h % 2], a_hi[:, h].bitcast(F32), ALU.subtract).then_inc(
                    a_lo_done, 1)
                dve.wait_ge(rooted, h + 1)
                nc.vector.reciprocal(root[:], root[:]).then_inc(inverted, 1)
                dve.wait_ge(inverted, h + 1)
                if h >= 1:
                    dve.wait_ge(lo_done, h)
                nc.vector.tensor_tensor(normed[:], o[:, h % 2], root[:], ALU.mult).then_inc(scaled, 1)
                dve.wait_ge(scaled, h + 1)
                dve.wait_ge(z_in[h % 2], 16 * (h // 2 + 1))
                nc.vector.scalar_tensor_tensor(out=normed[:], in0=normed[:], scalar=gain[:], in1=z[:, h % 2],
                                               op0=ALU.mult, op1=ALU.mult).then_inc(gated, 1)
                dve.wait_ge(hi_done, h + 1)
                nc.vector.tensor_tensor(b_lo[:, h], normed[:], b_hi[:, h].bitcast(F32), ALU.subtract).then_inc(lo_done, 1)


def merge(nc, x, a_hi, a_lo, b_hi, b_lo, w_branch_a, w_branch_b, w_out, projected_d):
    KB = HB
    FIRST_GATE = NC + HB
    with Scope(nc, "mg_") as s:
        raw_a, raw_b, raw_o = s.sbuf("raw_a", [P, KB, P]), s.sbuf("raw_b", [P, KB, P]), s.sbuf("raw_o", [P, D])
        wa_hi, wa_lo, wb_hi, wb_lo = (s.sbuf(n, [P, 2, KB, P], F32R) for n in ("wa_hi", "wa_lo", "wb_hi", "wb_lo"))
        wo_hi, wo_lo = (s.sbuf(n, [P, 2, D], F32R) for n in ("wo_hi", "wo_lo"))
        gate_a, gate_b = s.sbuf("gate_a", [P, 2, TOK]), s.sbuf("gate_b", [P, 2, TOK])
        part_a, part_b = s.sbuf("part_a", [P, 2, TG]), s.sbuf("part_b", [P, 2, TG])
        m_hi, m_lo = (s.sbuf(n, [P, 2, TOK], F32R) for n in ("m_hi", "m_lo"))
        p_a = [s.psum(f"p_a{i}") for i in range(2)]
        p_b = [s.psum(f"p_b{i}") for i in range(2)]
        p_out = [s.psum(f"p_out{i}") for i in range(4)]
        a_in, b_in, o_in, ab_hi, ab_lo, o_hi, o_lo = (s.sem(n) for n in (
            "a_in", "b_in", "o_in", "ab_hi", "ab_lo", "o_hi", "o_lo"))
        gates_in = s.sem("gates_in0"), s.sem("gates_in1")
        branches, gated_a, gated_b, summed, mhi_done, mlo_done, projected, added = (s.sem(n) for n in (
            "branches", "gated_a", "gated_b", "summed", "mhi_done", "mlo_done", "projected", "added"))
        NO = 2 * NT
        wa, wb = (w.rearrange("(k p) d -> p k d", p=P) for w in (w_branch_a, w_branch_b))
        block = s.block()

        @block.sync
        def _(sp):
            for n in range(KD):
                cols = slice(n * P, (n + 1) * P)
                if n:
                    sp.wait_ge(ab_lo, 2 * n)
                sp.dma_start(raw_a[:], wa[:, :, cols]).then_inc(a_in, 16)
                sp.dma_start(raw_b[:], wb[:, :, cols]).then_inc(b_in, 16)
                if n:
                    sp.wait_ge(o_lo, n)
                sp.dma_start(raw_o[:], w_out[cols, :]).then_inc(o_in, 16)

        @block.gpsimd
        def _(pool):
            for n in range(KD):
                if n >= 2:
                    pool.wait_ge(gated_b, NG * (n - 1))
                pool.dma_start(gate_a[:, n % 2], projected_d[FIRST_GATE + n]).then_inc(gates_in[n % 2], 16)
                pool.dma_start(gate_b[:, n % 2], projected_d[FIRST_GATE + KD + n]).then_inc(gates_in[n % 2], 16)

        @block.scalar
        def _(act):
            def split_branch(n):
                if n >= 2:
                    act.wait_ge(branches, NG * (n - 1))
                act.wait_ge(a_in, 16 * n + 16)
                nc.scalar.copy(wa_hi[:, n % 2], raw_a[:]).then_inc(ab_hi, 1)
                act.wait_ge(b_in, 16 * n + 16)
                nc.scalar.copy(wb_hi[:, n % 2], raw_b[:]).then_inc(ab_hi, 1)

            def split_out(n):
                if n >= 2:
                    act.wait_ge(projected, NO * (n - 1))
                act.wait_ge(o_in, 16 * n + 16)
                nc.scalar.copy(wo_hi[:, n % 2], raw_o[:]).then_inc(o_hi, 1)

            split_branch(0)
            split_branch(1)
            split_out(0)
            for n in range(KD):
                for g in range(NG):
                    act.wait_ge(summed, NG * n + g + 1)
                    if g == 0 and n >= 2:
                        act.wait_ge(projected, NO * (n - 1))
                    nc.scalar.copy(m_hi[:, n % 2, g * TG:(g + 1) * TG], part_a[:, (NG * n + g) % 2]).then_inc(mhi_done, 1)
                if n + 2 < KD:
                    split_branch(n + 2)
                if n + 1 < KD:
                    split_out(n + 1)

        @block.vector
        def _(dve):
            def lo_branch(n):
                dve.wait_ge(ab_hi, 2 * n + 1)
                nc.vector.tensor_tensor(wa_lo[:, n % 2], raw_a[:], wa_hi[:, n % 2].bitcast(F32), ALU.subtract).then_inc(ab_lo, 1)
                dve.wait_ge(ab_hi, 2 * n + 2)
                nc.vector.tensor_tensor(wb_lo[:, n % 2], raw_b[:], wb_hi[:, n % 2].bitcast(F32), ALU.subtract).then_inc(ab_lo, 1)

            def lo_out(n):
                dve.wait_ge(o_hi, n + 1)
                nc.vector.tensor_tensor(wo_lo[:, n % 2], raw_o[:], wo_hi[:, n % 2].bitcast(F32), ALU.subtract).then_inc(o_lo, 1)

            def add_out(n):
                for o in range(NO):
                    dve.wait_ge(projected, NO * n + o + 1)
                    if n:
                        dve.wait_ge(added, NO * (n - 1) + o + 1)
                    xs = x[:, o // 2, o % 2 * 512:o % 2 * 512 + 512]
                    nc.vector.tensor_tensor(xs, p_out[(NO * n + o) % 4][:], xs, ALU.add).then_inc(added, 1)

            lo_branch(0)
            lo_branch(1)
            lo_out(0)
            for n in range(KD):
                dve.wait_ge(gates_in[n % 2], 32 * (n // 2 + 1))
                for g in range(NG):
                    u, mine = NG * n + g, slice(g * TG, (g + 1) * TG)
                    dve.wait_ge(branches, u + 1)
                    if u >= 2:
                        dve.wait_ge(mlo_done, u - 1)
                        dve.wait_ge(summed, u - 1)
                    nc.vector.tensor_tensor(part_a[:, u % 2], p_a[u % 2][:, 0:TG], gate_a[:, n % 2, mine],
                                            ALU.mult).then_inc(gated_a, 1)
                    nc.vector.tensor_tensor(part_b[:, u % 2], p_b[u % 2][:, 0:TG], gate_b[:, n % 2, mine],
                                            ALU.mult).then_inc(gated_b, 1)
                    dve.wait_ge(gated_b, u + 1)
                    nc.vector.tensor_tensor(part_a[:, u % 2], part_a[:, u % 2], part_b[:, u % 2], ALU.add).then_inc(summed, 1)
                    dve.wait_ge(mhi_done, u + 1)
                    nc.vector.tensor_tensor(m_lo[:, n % 2, mine], part_a[:, u % 2], m_hi[:, n % 2, mine].bitcast(F32),
                                            ALU.subtract).then_inc(mlo_done, 1)
                if n:
                    add_out(n - 1)
                if n + 2 < KD:
                    lo_branch(n + 2)
                if n + 1 < KD:
                    lo_out(n + 1)
            add_out(KD - 1)

        @block.tensor
        def _(pe):
            def branch(n):
                for g in range(NG):
                    u, mine = NG * n + g, slice(g * TG, (g + 1) * TG)
                    pe.wait_ge(ab_lo, 2 * n + 2)
                    if u >= 2:
                        pe.wait_ge(gated_b, u - 1)
                    three_passes(nc, p_a[u % 2][:, 0:TG], lambda k: (wa_hi[:, n % 2, k, :], wa_lo[:, n % 2, k, :]),
                                 lambda k: (a_hi[:, k, mine], a_lo[:, k, mine]), range(KB))
                    three_passes(nc, p_b[u % 2][:, 0:TG], lambda k: (wb_hi[:, n % 2, k, :], wb_lo[:, n % 2, k, :]),
                                 lambda k: (b_hi[:, k, mine], b_lo[:, k, mine]), range(KB)).then_inc(branches, 1)

            def out(n):
                pe.wait_ge(o_lo, n + 1)
                for o in range(NO):
                    tokens, cols = slice(o // 2 * P, (o // 2 + 1) * P), slice(o % 2 * 512, o % 2 * 512 + 512)
                    if o % 6 == 0:
                        pe.wait_ge(mlo_done, NG * n + o // 6 + 1)
                    if NO * n + o >= 4:
                        pe.wait_ge(added, NO * n + o - 3)
                    three_passes(nc, p_out[(NO * n + o) % 4][:], lambda k: (m_hi[:, n % 2, tokens], m_lo[:, n % 2, tokens]),
                                 lambda k: (wo_hi[:, n % 2, cols], wo_lo[:, n % 2, cols]), [0]).then_inc(projected, 1)

            for n in range(KD):
                branch(n)
                if n:
                    out(n - 1)
            out(KD - 1)


def finish(nc, x, gain, y_prompt, y_sample):
    with Scope(nc, "fn_") as s:
        gain_b = s.sbuf("gain_b", [P, D])
        square, y = s.sbuf("square", [P, 2, D]), s.sbuf("y", [P, NT, D])
        sumsq, mean, root, rstd = (s.sbuf(n, [P, NT]) for n in ("sumsq", "mean", "root", "rstd"))
        gain_in, squared, averaged, rooted, inverted, normed, stored = (s.sem(n) for n in (
            "gain_in", "squared", "averaged", "rooted", "inverted", "normed", "stored"))
        block = s.block()

        @block.sync
        def _(sp):
            sp.dma_start(gain_b[:], gain.rearrange("(a d) -> a d", a=1).to_broadcast([P, D])).then_inc(gain_in, 16)
            for t in range(NT):
                sp.wait_ge(normed, t + 1)
                dst = y_prompt[0, t * P:(t + 1) * P, :] if t < NTP else y_sample.rearrange("b s d -> (b s) d")
                sp.dma_start(dst, y[:, t]).then_inc(stored, 16)
            sp.wait_ge(stored, 16 * NT)

        @block.scalar
        def _(act):
            for t in range(NT):
                if t >= 2:
                    act.wait_ge(squared, t - 1)
                nc.scalar.activation(square[:, t % 2], x[:, t, :], ACT.Square, accum_out=sumsq[:, t:t + 1]).then_inc(
                    squared, 1)
            act.wait_ge(averaged, 1)
            nc.scalar.activation(root[:], mean[:], ACT.Sqrt).then_inc(rooted, 1)

        @block.vector
        def _(dve):
            dve.wait_ge(squared, NT)
            nc.vector.tensor_scalar(mean[:], sumsq[:], 1.0 / D, EPS, ALU.mult, ALU.add).then_inc(averaged, 1)
            dve.wait_ge(rooted, 1)
            nc.vector.reciprocal(rstd[:], root[:]).then_inc(inverted, 1)
            dve.wait_ge(inverted, 1)
            dve.wait_ge(gain_in, 16)
            for t in range(NT):
                nc.vector.scalar_tensor_tensor(out=y[:, t], in0=x[:, t, :], scalar=rstd[:, t:t + 1], in1=gain_b[:],
                                               op0=ALU.mult, op1=ALU.mult).then_inc(normed, 1)


INPUTS = ["x_prompt", "x_sample", "cache_attn_k", "cache_attn_v", "cache_idx_k", "state_conv", "state_delta",
          "ffn1_norm", "ffn1_w_gate", "ffn1_w_up", "ffn1_w_down", "mix_norm", "w_in", "conv_w", "a_log", "dt_bias",
          "delta_norm", "w_branch_a", "w_branch_b", "w_out", "ffn2_norm", "ffn2_w_gate", "ffn2_w_up", "ffn2_w_down",
          "final_norm"]
OUTPUTS = [("y_prompt", (1, SEQ, D)), ("y_sample", (BATCH_S, SEQ_S, D)),
           ("new_k", (1, 1, SEQ, KV, HD)), ("new_v", (1, 1, SEQ, KV, HD)), ("new_idx_k", (1, 1, SEQ, HD)),
           ("new_conv", (1, 1, CONV_W - 1, CONV_CH)), ("new_delta", (1, 1, HB, DK, DK)),
           ("new_k_s", (1, BATCH_S, SEQ_S, KV, HD)), ("new_v_s", (1, BATCH_S, SEQ_S, KV, HD)),
           ("new_idx_k_s", (1, BATCH_S, SEQ_S, HD)), ("new_conv_s", (1, BATCH_S, CONV_W - 1, CONV_CH)),
           ("new_delta_s", (1, BATCH_S, HB, DK, DK))]


def encoder_step(nc, i, o, const_in):
    projected_d = nc.dram_tensor("projected_d", (NC + HB + 2 * KD, P, TOK), F32, kind="Internal").ap()
    conv_d = nc.dram_tensor("conv_d", (NC, P, TOK), F32, kind="Internal").ap()
    delta_d = nc.dram_tensor("delta_d", (HB, P, TOK), F32, kind="Internal").ap()
    attended_d = nc.dram_tensor("attended_d", (HB, P, TOK), F32, kind="Internal").ap()
    w_in = i["w_in"][0]
    with Scope(nc, "") as top:
        x, const = top.sbuf("x", [P, NT, D]), top.sbuf("const", [P, CONSTS, P])
        load_start(nc, x, const, i["x_prompt"], i["x_sample"], const_in)

        with Scope(nc, "f1_") as s:
            hT_hi, hT_lo = s.sbuf("hT_hi", [P, KD, TOK], F32R), s.sbuf("hT_lo", [P, KD, TOK], F32R)
            norm_turn(nc, x, const, hT_hi, hT_lo, i["ffn1_norm"][0], "n1_")
            ffn(nc, x, hT_hi, hT_lo, i["ffn1_w_gate"][0], i["ffn1_w_up"][0], i["ffn1_w_down"][0], "ffn1_")

        with Scope(nc, "mx_") as mix:
            small = mix.sbuf("small", [P, NT, 12])
            with Scope(nc, "sa_") as sparse:
                qkT, va = sparse.sbuf("qkT", [P, 5, TOK]), sparse.sbuf("va", [P, NT, P])
                scores = sparse.sbuf("scores", [P, SCORES])
                with Scope(nc, "h_") as s:
                    hT_hi, hT_lo = s.sbuf("hT_hi", [P, KD, TOK], F32R), s.sbuf("hT_lo", [P, KD, TOK], F32R)
                    norm_turn(nc, x, const, hT_hi, hT_lo, i["mix_norm"][0], "n2_")
                    project_small(nc, hT_hi, hT_lo, w_in, va, small, o["new_k"], o["new_v"], o["new_idx_k"],
                                  o["new_k_s"], o["new_v_s"], o["new_idx_k_s"])
                    with Scope(nc, "ix_") as index:
                        qiT = index.sbuf("qiT", [P, 4, TOK])
                        project_turned(nc, hT_hi, hT_lo, w_in, qkT, qiT)
                        score(nc, const, qiT, small, i["cache_idx_k"], scores)
                    select_and_project(nc, hT_hi, hT_lo, w_in, scores, projected_d)
                attend(nc, const, qkT, va, scores, i["cache_attn_k"], i["cache_attn_v"], attended_d)
            with Scope(nc, "dn_") as s:
                inv_norm = s.sbuf("inv_norm", [P, NT, 2 * HB])
                convolve(nc, const, i["conv_w"][0], i["state_conv"], projected_d, conv_d, inv_norm, o["new_conv"],
                         o["new_conv_s"])
                beta, g, cum, c_key, c_last = (s.sbuf(n, [P, NT, HB]) for n in ("beta", "g", "cum", "c_key", "c_last"))
                last_p, last_s = s.sbuf("last_p", [P, NTP, HB]), s.sbuf("last_s", [P, HB, BATCH_S])
                decays(nc, const, small, i["a_log"], i["dt_bias"], beta, g, cum, c_key, c_last, last_p, last_s)
                delta(nc, const, beta, g, cum, c_key, c_last, last_p, last_s, inv_norm, conv_d, i["state_delta"],
                      delta_d, o["new_delta"], o["new_delta_s"])
            with Scope(nc, "br_") as s:
                a_hi, a_lo, b_hi, b_lo = (s.sbuf(n, [P, HB, TOK], F32R) for n in ("a_hi", "a_lo", "b_hi", "b_lo"))
                split_branches(nc, const, i["delta_norm"][0], attended_d, delta_d, projected_d, a_hi, a_lo, b_hi, b_lo)
                merge(nc, x, a_hi, a_lo, b_hi, b_lo, i["w_branch_a"][0], i["w_branch_b"][0], i["w_out"][0], projected_d)

        with Scope(nc, "f2_") as s:
            hT_hi, hT_lo = s.sbuf("hT_hi", [P, KD, TOK], F32R), s.sbuf("hT_lo", [P, KD, TOK], F32R)
            norm_turn(nc, x, const, hT_hi, hT_lo, i["ffn2_norm"][0], "n3_")
            ffn(nc, x, hT_hi, hT_lo, i["ffn2_w_gate"][0], i["ffn2_w_up"][0], i["ffn2_w_down"][0], "ffn2_")
        finish(nc, x, i["final_norm"], o["y_prompt"], o["y_sample"])


def kernel(**inputs):
    import concourse.bacc as bacc
    from concourse.bass_utils import run_bass_kernel_spmd

    nc = bacc.Bacc("TRN2", target_bir_lowering=False, num_devices=1)
    arrays, ins, outs = {}, {}, {}
    for name in INPUTS:
        a = np.ascontiguousarray(inputs[name])
        arrays[f"in_{name}"] = a
        ins[name] = nc.dram_tensor(f"in_{name}", a.shape, mybir.dt.from_np(a.dtype), kind="ExternalInput").ap()
    arrays["in_constants"] = constants()
    const_in = nc.dram_tensor("in_constants", (P, CONSTS, P), F32, kind="ExternalInput").ap()
    for name, shape in OUTPUTS:
        outs[name] = nc.dram_tensor(f"out_{name}", shape, F32, kind="ExternalOutput").ap()
    encoder_step(nc, ins, outs, const_in)
    got = run_bass_kernel_spmd(nc, [arrays], core_ids=[0]).results[0]
    return tuple(got[f"out_{name}"] for name, _ in OUTPUTS)
```

```python
from contextlib import ExitStack

import numpy as np

import concourse.bass as bass
from concourse import mybir

F32 = mybir.dt.float32
F32R = mybir.dt.float32r
ALU = mybir.AluOpType
ACT = mybir.ActivationFunctionType
AX = mybir.AxisListType

P = 128
D = 1024
KD = D // P
DFF = 2816
NF = DFF // P
SEQ = 1024
BATCH_S, SEQ_S, PAST = 8, 16, 256
TOK = SEQ + BATCH_S * SEQ_S
NT = TOK // P
NTP = SEQ // P
TG = 384
NG = TOK // TG
EPS = 1e-6

HEADS, KV, HD = 8, 2, 64
IH = 4
CHUNK = 64
TOPK_P, TOPK_S = 256, 68
KEYS_S = PAST + SEQ_S
HB, DK = 4, 128
CONV_CH, CONV_W = 1536, 4
NC = CONV_CH // P
C_Q, C_K, C_V, C_QI, C_KI, C_WI = 0, 512, 640, 768, 1024, 1088
C_CONV, C_Z, C_BB, C_GATE = 1092, 2628, 3140, 3148
D_IN = 5196
SMALL = 256 + 68 + 8
S_V, S_KI, S_WI, S_BB = 128, 256, 320, 324

TAKEN, INADMISSIBLE, FILL, UNSELECTED = -3.0e38, -2.0e38, -1.0e38, -1.0e30
WIDTH = [P * (t + 1) for t in range(NTP)] + [KEYS_S]
PAD_S = 8
AT = [sum(WIDTH[:t]) for t in range(NT)]
SCORES = sum(WIDTH) + PAD_S

ONES, IDENT, UPTO, UPTO_S, SAME_S, BATCH_OF, LEVEL = range(7)
LEVELS_P, LEVELS_S = 7, 4
CONSTS = LEVEL + LEVELS_P


def constants():
    i, j = np.arange(P)[:, None], np.arange(P)[None, :]
    same = i // SEQ_S == j // SEQ_S
    planes = [np.ones((P, P)), i == j, i <= j, (i <= j) & same, same, (i // SEQ_S == j)]
    for level in range(LEVELS_P):
        m = 1 << level
        planes.append((i // (2 * m) == j // (2 * m)) & (i % (2 * m) >= m) & (j % (2 * m) < m))
    return np.ascontiguousarray(np.stack([np.asarray(p, np.float32) for p in planes], 1))


def known(n, below):
    return isinstance(n, int) and n < below


def in_steps(eng, step, first, last, lead=1):
    n = first
    while n < min(first + lead, last):
        step(n, n % 2)
        n += 1
    pairs = (last - n) // 2
    if pairs > 1:
        with eng.Fori(0, pairs) as j:
            step(2 * j + n, n % 2)
            step(2 * j + n + 1, (n + 1) % 2)
        n += 2 * pairs
    while n < last:
        step(n, n % 2)
        n += 1


class Scope:

    def __init__(self, nc, name):
        self.nc, self.name, self.stack, self.sems = nc, name, ExitStack(), []

    def __enter__(self):
        return self

    def __exit__(self, *what):
        left = self.stack.__exit__(*what)
        if self.sems:
            self.nc.clear_and_free_semaphores(self.sems)
            self.nc.all_engine_barrier()
        return left

    def sbuf(self, name, shape, dt=F32):
        return self.stack.enter_context(self.nc.sbuf_tensor(self.name + name, shape, dt))

    def psum(self, name, shape=(P, 512)):
        return self.stack.enter_context(self.nc.psum_tensor(self.name + name, list(shape), F32))

    def sem(self, name):
        self.sems.append(self.nc.alloc_semaphore(self.name + name))
        return self.sems[-1]

    def block(self):
        return self.stack.enter_context(self.nc.Block())


def three_passes(nc, out, stationary, moving, ks, start=True, stop=True):
    n, mm = 3 * len(ks), None
    for at, k in enumerate(ks):
        for i, (a, b) in enumerate(((0, 0), (0, 1), (1, 0))):
            mm = nc.tensor.matmul(out, stationary(k)[a], moving(k)[b], start=(start and at == 0 and i == 0),
                                  stop=(stop and 3 * at + i == n - 1))
    return mm


class NormTurn:
    TILES, UNITS = TG // P, 2 * TG // P

    def __init__(self, nc, s, x, const, hT_hi, hT_lo, gain, banks):
        self.nc, self.x, self.const, self.hT_hi, self.hT_lo, self.gain, self.pT = nc, x, const, hT_hi, hT_lo, gain, banks
        self.gain_b = s.sbuf("gain_b", [P, D])
        self.sumsq, self.mean, self.root, self.rstd = (s.sbuf(n, [P, NT]) for n in ("sumsq", "mean", "root", "rstd"))
        self.h = s.sbuf("h", [P, 2, 512])
        self.gain_in, self.squared, self.mean_ready, self.rooted, self.rstd_ready = (
            s.sem(n) for n in ("gain_in", "squared", "mean_ready", "rooted", "rstd_ready"))
        self.h_ready, self.turned, self.hi_ready, self.lo_ready = (
            s.sem(n) for n in ("h_ready", "turned", "hi_ready", "lo_ready"))

    def part(self, i):
        return slice(None), slice(4 * (i % 2), 4 * (i % 2) + 4), slice((i // 2) * P, (i // 2 + 1) * P)

    def load_gain(self, eng):
        eng.dma_start(self.gain_b[:], self.gain.rearrange("(a d) -> a d", a=1).to_broadcast([P, D])).then_inc(
            self.gain_in, 16)

    def square(self, t):
        self.nc.scalar.activation(self.hT_hi[:, :, t * P:(t + 1) * P], self.x[:, t, :].rearrange("p (k c) -> p k c", c=P),
                                  ACT.Square, accum_out=self.sumsq[:, t:t + 1]).then_inc(self.squared, 1)

    def roots(self, act, g):
        tiles = slice(g % NG * self.TILES, (g % NG + 1) * self.TILES)
        act.wait_ge(self.mean_ready, g + 1)
        self.nc.scalar.activation(self.root[:, tiles], self.mean[:, tiles], ACT.Sqrt).then_inc(self.rooted, 1)

    def keep_hi(self, act, t):
        for i in (2 * t, 2 * t + 1):
            act.wait_ge(self.turned, i + 1)
            self.nc.scalar.copy(self.hT_hi[self.part(i)], self.pT[i % 4][:]).then_inc(self.hi_ready, 1)

    def scalar(self, act, tile_loaded):
        for t in range(self.TILES):
            tile_loaded(t)
            self.square(t)
        for g in range(NG):
            self.roots(act, g)
            for t in range(g * self.TILES, (g + 1) * self.TILES):
                self.keep_hi(act, t)
                if g + 1 < NG:
                    tile_loaded(t + self.TILES)
                    self.square(t + self.TILES)

    def scales(self, dve, g):
        tiles = slice(g % NG * self.TILES, (g % NG + 1) * self.TILES)
        dve.wait_ge(self.squared, self.TILES * (g + 1))
        self.nc.vector.tensor_scalar(self.mean[:, tiles], self.sumsq[:, tiles], 1.0 / D, EPS, ALU.mult,
                                     ALU.add).then_inc(self.mean_ready, 1)
        dve.wait_ge(self.rooted, g + 1)
        self.nc.vector.reciprocal(self.rstd[:, tiles], self.root[:, tiles]).then_inc(self.rstd_ready, 1)
        dve.wait_ge(self.rstd_ready, g + 1)

    def keep_lo(self, dve, i):
        dve.wait_ge(self.hi_ready, i + 1)
        self.nc.vector.tensor_tensor(self.hT_lo[self.part(i)], self.pT[i % 4][:], self.hT_hi[self.part(i)].bitcast(F32),
                                     ALU.subtract).then_inc(self.lo_ready, 1)

    def vector(self, dve, g, after_tile=None):
        self.scales(dve, g)
        if g == 0:
            dve.wait_ge(self.gain_in, 16)
        for i in range(g * self.UNITS, (g + 1) * self.UNITS):
            if i >= 2:
                dve.wait_ge(self.turned, i - 1)
            t, cols = i // 2, slice(i % 2 * 512, i % 2 * 512 + 512)
            self.nc.vector.scalar_tensor_tensor(out=self.h[:, i % 2, :], in0=self.x[:, t, cols],
                                                scalar=self.rstd[:, t:t + 1], in1=self.gain_b[:, cols], op0=ALU.mult,
                                                op1=ALU.mult).then_inc(self.h_ready, 1)
            if i > g * self.UNITS:
                self.keep_lo(dve, i - 1)
            if i % 2 and after_tile:
                after_tile(t)
        self.keep_lo(dve, (g + 1) * self.UNITS - 1)

    def turn(self, pe, i):
        pe.wait_ge(self.h_ready, i + 1)
        if i >= 4:
            pe.wait_ge(self.lo_ready, i - 3)
        for k in range(4):
            mm = self.nc.tensor.transpose(self.pT[i % 4][:, k, :], self.h[:, i % 2, k * P:(k + 1) * P],
                                          self.const[:, IDENT, :])
        mm.then_inc(self.turned, 1)


def ffn(nc, x, const, gain, w_gate, w_up, w_down, name, start=None, finish=None):
    with Scope(nc, name) as s:
        hT_hi, hT_lo = s.sbuf("hT_hi", [P, KD, TOK], F32R), s.sbuf("hT_lo", [P, KD, TOK], F32R)
        raw_g, raw_u, raw_d = s.sbuf("raw_g", [P, KD, P]), s.sbuf("raw_u", [P, KD, P]), s.sbuf("raw_d", [P, D])
        g_hi, g_lo, u_hi, u_lo = (s.sbuf(n, [P, 2, KD, P], F32R) for n in ("g_hi", "g_lo", "u_hi", "u_lo"))
        d_hi, d_lo = (s.sbuf(n, [P, 2, D], F32R) for n in ("d_hi", "d_lo"))
        a_hi, a_lo = (s.sbuf(n, [P, 2, TOK], F32R) for n in ("a_hi", "a_lo"))
        silu, prod = s.sbuf("silu", [P, 2, TG]), s.sbuf("prod", [P, 2, TG])
        p_gate = [s.psum(f"p_gate{i}") for i in range(2)]
        p_up = [s.psum(f"p_up{i}") for i in range(2)]
        p_down = [s.psum(f"p_down{i}") for i in range(4)]
        norm = NormTurn(nc, s, x, const, hT_hi, hT_lo, gain, [b[:].rearrange("p (k c) -> p k c", c=P) for b in p_down])
        x_in = [s.sem(f"x_in{g}") for g in range(NG)]
        const_ready, last_gain_in, y_ready, stored = (s.sem(n) for n in ("const_ready", "last_gain_in", "y_ready", "stored"))
        g_in, u_in, d_in = s.sem("g_in"), s.sem("u_in"), s.sem("d_in")
        gu_hi, gu_lo = s.sem("gu_hi"), s.sem("gu_lo")
        dn_hi, dn_lo = s.sem("dn_hi"), s.sem("dn_lo")
        gate_up, silu_done, prod_done, act_hi, act_lo = (
            s.sem(n) for n in ("gate_up", "silu_done", "prod_done", "act_hi", "act_lo"))
        down, added = s.sem("down"), s.sem("added")
        wg, wu = (w.rearrange("(k p) f -> p k f", p=P) for w in (w_gate, w_up))
        NO = 2 * NT
        block = s.block()

        @block.sync
        def _(sp):
            def load(n, q):
                if not known(n, 1):
                    sp.wait_ge(gu_lo, 2 * n - 1)
                sp.dma_start(raw_g[:], wg[:, :, bass.ts(n, P)]).then_inc(g_in, 16)
                if not known(n, 1):
                    sp.wait_ge(gu_lo, 2 * n)
                sp.dma_start(raw_u[:], wu[:, :, bass.ts(n, P)]).then_inc(u_in, 16)
                if not known(n, 1):
                    sp.wait_ge(dn_lo, n)
                sp.dma_start(raw_d[:], w_down[bass.ts(n, P), :]).then_inc(d_in, 16)

            GT = norm.TILES
            if start:
                x_prompt, x_sample, const_in = start
                sp.dma_start(x[:, 0:GT, :], x_prompt[0, 0:TG].rearrange("(t p) d -> p t d", p=P)).then_inc(x_in[0], 16)
            norm.load_gain(sp)
            load(0, 0)
            if start:
                sp.dma_start(x[:, GT:2 * GT, :], x_prompt[0, TG:2 * TG].rearrange("(t p) d -> p t d", p=P)).then_inc(
                    x_in[1], 16)
                sp.dma_start(x[:, 2 * GT:NTP, :], x_prompt[0, 2 * TG:SEQ].rearrange("(t p) d -> p t d", p=P)).then_inc(
                    x_in[2], 16)
                sp.dma_start(x[:, NTP, :], x_sample.rearrange("b s d -> (b s) d")).then_inc(x_in[2], 16)
            in_steps(sp, load, 1, NF)
            if finish:
                last_gain, y_prompt, y_sample = finish
                sp.wait_ge(norm.h_ready, 2 * NT)
                sp.dma_start(norm.gain_b[:], last_gain.rearrange("(a d) -> a d", a=1).to_broadcast([P, D])).then_inc(
                    last_gain_in, 16)
                for t in range(NT):
                    sp.wait_ge(y_ready, t + 1)
                    dst = y_prompt[0, t * P:(t + 1) * P, :] if t < NTP else y_sample.rearrange("b s d -> (b s) d")
                    sp.dma_start(dst, x[:, t, :]).then_inc(stored, 16)
                sp.wait_ge(stored, 16 * NT)

        @block.scalar
        def _(act):
            def split_gate_up(n, q):
                if not known(n, 2):
                    act.wait_ge(gate_up, NG * (n - 1))
                act.wait_ge(g_in, 16 * n + 16)
                nc.scalar.copy(g_hi[:, q], raw_g[:]).then_inc(gu_hi, 1)
                act.wait_ge(u_in, 16 * n + 16)
                nc.scalar.copy(u_hi[:, q], raw_u[:]).then_inc(gu_hi, 1)

            def split_down(n, q):
                if not known(n, 2):
                    act.wait_ge(down, NO * (n - 1))
                act.wait_ge(d_in, 16 * n + 16)
                nc.scalar.copy(d_hi[:, q], raw_d[:]).then_inc(dn_hi, 1)

            def step(n, q):
                for g in range(NG):
                    slot = (NG * q + g) % 2
                    act.wait_ge(gate_up, NG * n + g + 1)
                    if not (known(n, 1) and g < 2):
                        act.wait_ge(prod_done, NG * n + g - 1)
                    nc.scalar.activation(silu[:, slot], p_gate[slot][:, 0:TG], ACT.Silu).then_inc(silu_done, 1)
                    act.wait_ge(prod_done, NG * n + g + 1)
                    if g == 0 and not known(n, 2):
                        act.wait_ge(down, NO * (n - 1))
                    nc.scalar.copy(a_hi[:, q, g * TG:(g + 1) * TG], prod[:, slot]).then_inc(act_hi, 1)
                if not known(n, NF) or n + 2 < NF:
                    split_gate_up(n + 2, q)
                if not known(n, NF) or n + 1 < NF:
                    split_down(n + 1, 1 - q)

            if start:
                act.dma_start(const[:], start[2]).then_inc(const_ready, 16)

            def tile_loaded(t):
                g = t // norm.TILES
                if start:
                    act.wait_ge(x_in[g], 32 if g == NG - 1 else 16)

            split_gate_up(0, 0)
            norm.scalar(act, tile_loaded)
            split_gate_up(1, 1)
            split_down(0, 0)
            in_steps(act, step, 0, NF - 2, lead=2)
            in_steps(act, step, NF - 2, NF)
            if finish:
                for g in range(NG):
                    for t in range(g * norm.TILES, (g + 1) * norm.TILES):
                        act.wait_ge(added, NO * (NF - 1) + 2 * t + 2)
                        if g == 0:
                            act.wait_ge(norm.rstd_ready, NG)
                        norm.square(t)
                    norm.roots(act, NG + g)

        @block.vector
        def _(dve):
            def split_gate_up(n, q):
                dve.wait_ge(gu_hi, 2 * n + 1)
                nc.vector.tensor_tensor(g_lo[:, q], raw_g[:], g_hi[:, q].bitcast(F32), ALU.subtract).then_inc(gu_lo, 1)
                dve.wait_ge(gu_hi, 2 * n + 2)
                nc.vector.tensor_tensor(u_lo[:, q], raw_u[:], u_hi[:, q].bitcast(F32), ALU.subtract).then_inc(gu_lo, 1)

            def split_down(n, q):
                dve.wait_ge(dn_hi, n + 1)
                nc.vector.tensor_tensor(d_lo[:, q], raw_d[:], d_hi[:, q].bitcast(F32), ALU.subtract).then_inc(dn_lo, 1)

            def add_down(n, q, outs=range(NO)):
                for o in outs:
                    dve.wait_ge(down, NO * n + o + 1)
                    if not known(n, 1):
                        dve.wait_ge(added, NO * (n - 1) + o + 1)
                    xs = x[:, o // 2, (o % 2) * 512:(o % 2) * 512 + 512]
                    nc.vector.scalar_tensor_tensor(out=xs, in0=p_down[(NO * q + o) % 4][:], scalar=0.5, in1=xs,
                                                   op0=ALU.mult, op1=ALU.add).then_inc(added, 1)

            def finish_group(g):
                norm.scales(dve, NG + g)
                if g == 0:
                    dve.wait_ge(last_gain_in, 16)
                for t in range(g * norm.TILES, (g + 1) * norm.TILES):
                    nc.vector.scalar_tensor_tensor(out=x[:, t, :], in0=x[:, t, :], scalar=norm.rstd[:, t:t + 1],
                                                   in1=norm.gain_b[:], op0=ALU.mult, op1=ALU.mult).then_inc(y_ready, 1)

            def step(n, q):
                for g in range(NG):
                    slot = (NG * q + g) % 2
                    dve.wait_ge(silu_done, NG * n + g + 1)
                    if not (known(n, 1) and g < 2):
                        dve.wait_ge(act_lo, NG * n + g - 1)
                    nc.vector.tensor_tensor(prod[:, slot], silu[:, slot], p_up[slot][:, 0:TG],
                                            ALU.mult).then_inc(prod_done, 1)
                    if g == NG - 1 and not known(n, 1):
                        add_down(n - 1, 1 - q, [0])
                    dve.wait_ge(act_hi, NG * n + g + 1)
                    mine = slice(g * TG, (g + 1) * TG)
                    nc.vector.tensor_tensor(a_lo[:, q, mine], prod[:, slot], a_hi[:, q, mine].bitcast(F32),
                                            ALU.subtract).then_inc(act_lo, 1)
                if not known(n, 1):
                    add_down(n - 1, 1 - q, range(1, NO))
                if not known(n, NF) or n + 2 < NF:
                    split_gate_up(n + 2, q)
                if not known(n, NF) or n + 1 < NF:
                    split_down(n + 1, 1 - q)

            split_gate_up(0, 0)
            for g in range(NG):
                norm.vector(dve, g)
            split_gate_up(1, 1)
            split_down(0, 0)
            in_steps(dve, step, 0, NF - 2, lead=2)
            in_steps(dve, step, NF - 2, NF)
            if not finish:
                add_down(NF - 1, (NF - 1) % 2)
            else:
                per_group = NO // NG
                for g in range(NG):
                    add_down(NF - 1, (NF - 1) % 2, range(g * per_group, (g + 1) * per_group))
                    if g:
                        finish_group(g - 1)
                finish_group(NG - 1)

        @block.tensor
        def _(pe):
            def gate_and_up(n, q):
                for g in range(NG):
                    slot, mine = (NG * q + g) % 2, slice(g * TG, (g + 1) * TG)
                    if g == 0:
                        pe.wait_ge(gu_lo, 2 * n + 1)
                    if not (known(n, 1) and g < 2):
                        pe.wait_ge(silu_done, NG * n + g - 1)
                    three_passes(nc, p_gate[slot][:, 0:TG], lambda k: (g_hi[:, q, k, :], g_lo[:, q, k, :]),
                                 lambda k: (hT_hi[:, k, mine], hT_lo[:, k, mine]), range(KD))
                    if g == 0:
                        pe.wait_ge(gu_lo, 2 * n + 2)
                    if not (known(n, 1) and g < 2):
                        pe.wait_ge(prod_done, NG * n + g - 1)
                    three_passes(nc, p_up[slot][:, 0:TG], lambda k: (u_hi[:, q, k, :], u_lo[:, q, k, :]),
                                 lambda k: (hT_hi[:, k, mine], hT_lo[:, k, mine]), range(KD)).then_inc(gate_up, 1)

            def gate_and_up_first():
                for i in range(norm.UNITS):
                    norm.turn(pe, i)
                for g in range(NG):
                    mine, at = slice(g * TG, (g + 1) * TG), 0
                    pe.wait_ge(norm.lo_ready, norm.UNITS * (g + 1))
                    for j, (bank, hi, lo) in enumerate(((p_gate, g_hi, g_lo), (p_up, u_hi, u_lo))):
                        if g == 0:
                            pe.wait_ge(gu_lo, j + 1)
                        if g >= 2:
                            pe.wait_ge((silu_done, prod_done)[j], g - 1)
                        for k in range(KD):
                            mm = three_passes(nc, bank[g % 2][:, 0:TG], lambda k: (hi[:, 0, k, :], lo[:, 0, k, :]),
                                              lambda k: (hT_hi[:, k, mine], hT_lo[:, k, mine]), [k], start=(k == 0),
                                              stop=(k == KD - 1))
                            if j == 1 and k == KD - 1:
                                mm.then_inc(gate_up, 1)
                            if g + 1 < NG and (KD * j + k + 1) * norm.UNITS // (2 * KD) > at:
                                norm.turn(pe, norm.UNITS * (g + 1) + at)
                                at += 1

            def down_proj(n, q):
                pe.wait_ge(dn_lo, n + 1)
                for o in range(NO):
                    tokens, cols = slice(o // 2 * P, (o // 2 + 1) * P), slice(o % 2 * 512, o % 2 * 512 + 512)
                    if o % 6 == 0:
                        pe.wait_ge(act_lo, NG * n + o // 6 + 1)
                    if not (known(n, 1) and o < 4):
                        pe.wait_ge(added, NO * n + o - 3)
                    elif o == 0:
                        pe.wait_ge(norm.lo_ready, 2 * NT)
                    three_passes(nc, p_down[(NO * q + o) % 4][:], lambda k: (a_hi[:, q, tokens], a_lo[:, q, tokens]),
                                 lambda k: (d_hi[:, q, cols], d_lo[:, q, cols]), [0]).then_inc(down, 1)

            def step(n, q):
                gate_and_up(n, q)
                down_proj(n - 1, 1 - q)

            if start:
                pe.wait_ge(const_ready, 16)
            gate_and_up_first()
            in_steps(pe, step, 1, NF)
            down_proj(NF - 1, (NF - 1) % 2)


def diagonal(flat):
    return flat.rearrange("p (b c) -> p b c", b=BATCH_S)[:, :, 0:SEQ_S]


def project_small(nc, x, const, gain, hT_hi, hT_lo, w_in, va, small, new_k, new_v, new_ki, new_ks, new_vs, new_kis):
    with Scope(nc, "ps_") as s:
        raw = s.sbuf("raw", [P, KD, SMALL])
        w_hi, w_lo = s.sbuf("w_hi", [P, KD, SMALL], F32R), s.sbuf("w_lo", [P, KD, SMALL], F32R)
        out = s.sbuf("out", [P, 2, SMALL])
        norm = NormTurn(nc, s, x, const, hT_hi, hT_lo, gain, [s.psum(f"pT{i}", (P, 4, P)) for i in range(4)])
        p_out = [s.psum(f"p_out{i}") for i in range(4)]
        w_raw, w_split_hi, w_split_lo, projected, kept, copied = (
            s.sem(n) for n in ("w_raw", "w_split_hi", "w_split_lo", "projected", "kept", "copied"))
        stored = s.sem("stored0"), s.sem("stored1")
        w = w_in.rearrange("(k p) c -> p k c", p=P)
        block = s.block()
        LAG = 3
        spans = ((0, C_K, S_KI), (S_KI, C_KI, S_BB - S_KI), (S_BB, C_BB, SMALL - S_BB))

        @block.sync
        def _(sp):
            norm.load_gain(sp)
            for at, column, n in spans:
                sp.dma_start(raw[:, :, at:at + n], w[:, :, column:column + n]).then_inc(w_raw, 16)
            for t in range(NT):
                sp.wait_ge(copied, t + 1)
                if t < NTP:
                    rows = slice(t * P, (t + 1) * P)
                    outs = (new_k[0, 0, rows, :, :].rearrange("s n d -> s (n d)"),
                            new_v[0, 0, rows, :, :].rearrange("s n d -> s (n d)"), new_ki[0, 0, rows, :])
                else:
                    outs = (new_ks[0].rearrange("b s n d -> (b s) (n d)"), new_vs[0].rearrange("b s n d -> (b s) (n d)"),
                            new_kis[0].rearrange("b s d -> (b s) d"))
                for dst, cols in zip(outs, (slice(0, S_V), slice(S_V, S_KI), slice(S_KI, S_WI))):
                    sp.dma_start(dst, out[:, t % 2, cols]).then_inc(stored[t % 2], 16)
            for q in range(2):
                sp.wait_ge(stored[q], 48 * ((NT + 1 - q) // 2))

        @block.scalar
        def _(act):
            def keep(t):
                act.wait_ge(projected, t + 1)
                if t >= 2:
                    act.wait_ge(stored[t % 2], 48 * (t // 2))
                    act.wait_ge(kept, t - 1)
                nc.scalar.copy(out[:, t % 2, :], p_out[t % 4][:, 0:SMALL]).then_inc(copied, 1)

            for t in range(norm.TILES):
                norm.square(t)
            norm.roots(act, 0)
            act.wait_ge(w_raw, 16 * len(spans))
            nc.scalar.copy(w_hi[:], raw[:]).then_inc(w_split_hi, 1)
            for t in range(NT):
                norm.keep_hi(act, t)
                if t + norm.TILES < NT:
                    norm.square(t + norm.TILES)
                if t >= LAG:
                    keep(t - LAG)
                if t % norm.TILES == norm.TILES - 1 and t + 1 < NT:
                    norm.roots(act, (t + 1) // norm.TILES)
            for t in range(NT - LAG, NT):
                keep(t)

        @block.gpsimd
        def _(pool):
            pool.wait_ge(w_split_hi, 1)
            ks = slice(0, KD // 4)
            nc.gpsimd.tensor_tensor(w_lo[:, ks], raw[:, ks], w_hi[:, ks].bitcast(F32), ALU.subtract).then_inc(w_split_lo, 1)

        @block.vector
        def _(dve):
            def take(t):
                dve.wait_ge(copied, t + 1)
                nc.vector.tensor_copy(va[:, t, :], out[:, t % 2, S_V:S_KI])
                nc.vector.tensor_copy(small[:, t, :], out[:, t % 2, S_WI:SMALL]).then_inc(kept, 1)

            def after_tile(t):
                if t == 0:
                    dve.wait_ge(w_split_hi, 1)
                    ks = slice(KD // 4, KD)
                    nc.vector.tensor_tensor(w_lo[:, ks], raw[:, ks], w_hi[:, ks].bitcast(F32), ALU.subtract).then_inc(
                        w_split_lo, 1)
                if t >= LAG:
                    take(t - LAG)

            for g in range(NG):
                norm.vector(dve, g, after_tile)
            for t in range(NT - LAG, NT):
                take(t)

        @block.tensor
        def _(pe):
            for i in range(4):
                norm.turn(pe, i)
            pe.wait_ge(w_split_lo, 2)
            for t in range(NT):
                pe.wait_ge(norm.lo_ready, 2 * t + 2)
                if t >= 4:
                    pe.wait_ge(copied, t - 3)
                tokens = slice(t * P, (t + 1) * P)
                for half in range(2):
                    ks = range(half * KD // 2, (half + 1) * KD // 2)
                    mm = three_passes(nc, p_out[t % 4][:, 0:SMALL], lambda k: (hT_hi[:, k, tokens], hT_lo[:, k, tokens]),
                                      lambda k: (w_hi[:, k, :], w_lo[:, k, :]), ks, start=(half == 0), stop=(half == 1))
                    if half:
                        mm.then_inc(projected, 1)
                    if t + 2 < NT:
                        norm.turn(pe, 2 * (t + 2) + half)


def project_turned(nc, const, decays, small, a_log, dt_bias, hT_hi, hT_lo, w_in, qkT, qiT):
    with Scope(nc, "pt_") as s:
        raw = s.sbuf("raw", [P, KD, P])
        w_hi, w_lo = s.sbuf("w_hi", [P, 2, KD, P], F32R), s.sbuf("w_lo", [P, 2, KD, P], F32R)
        p_out = [s.psum(f"p_out{i}") for i in range(2 * NG)]
        decays.open(s, const, small, a_log, dt_bias)
        w_raw, w_split_hi, w_split_lo, projected, copied, upper_zero = (
            s.sem(n) for n in ("w_raw", "w_split_hi", "w_split_lo", "projected", "copied", "upper_zero"))
        w = w_in.rearrange("(k p) c -> p k c", p=P)
        block = s.block()

        @block.gpsimd
        def _(pool):
            nc.gpsimd.memset(qiT[HD:P, 2, :], 0.0).then_inc(upper_zero, 1)
            pool.wait_ge(upper_zero, 1)
            nc.gpsimd.memset(qiT[0:HD, 3, :], 0.0)

        starts = [(C_Q + HD * j, C_Q + HD * (4 + j)) for j in range(4)]
        starts += [(C_K, C_K + HD), (C_QI, C_QI + HD), (C_QI + 2 * HD, C_QI + 3 * HD), (C_KI, C_KI)]
        NB = len(starts)

        @block.sync
        def _(sp):
            for n, pair in enumerate(starts):
                if n:
                    sp.wait_ge(w_split_lo, n)
                for i, c in enumerate(pair):
                    sp.dma_start(raw[:, :, i * HD:(i + 1) * HD], w[:, :, c:c + HD]).then_inc(w_raw, 16)
                if n == 0:
                    decays.load(sp)

        @block.scalar
        def _(act):
            def split(n):
                act.wait_ge(w_raw, 32 * (n + 1))
                if n >= 2:
                    act.wait_ge(projected, NG * (n - 1))
                nc.scalar.copy(w_hi[:, n % 2], raw[:]).then_inc(w_split_hi, 1)

            split(0)
            split(1)
            decays.scalar(act)
            for n in range(NB):
                if n == 2:
                    decays.scalar_end(act)
                for g in range(NG):
                    act.wait_ge(projected, NG * n + g + 1)
                    mine, bank = slice(g * TG, (g + 1) * TG), p_out[NG * (n % 2) + g]
                    if n < NB - 1:
                        dst = qkT[:, n, mine] if n < 5 else qiT[:, n - 5, mine]
                        nc.scalar.copy(dst, bank[:, 0:TG]).then_inc(copied, 1)
                    else:
                        nc.scalar.copy(qiT[0:HD, 2, mine], bank[0:HD, 0:TG])
                        nc.scalar.copy(qiT[HD:P, 3, mine], bank[HD:P, 0:TG]).then_inc(copied, 1)
                if n + 2 < NB:
                    split(n + 2)

        @block.vector
        def _(dve):
            for n in range(NB):
                dve.wait_ge(w_split_hi, n + 1)
                nc.vector.tensor_tensor(w_lo[:, n % 2], raw[:], w_hi[:, n % 2].bitcast(F32),
                                        ALU.subtract).then_inc(w_split_lo, 1)
                if n == 1:
                    decays.vector(dve)
                if n == 3:
                    decays.vector_end(dve)

        @block.tensor
        def _(pe):
            for n in range(NB):
                if n == 1:
                    decays.tensor(pe)
                pe.wait_ge(w_split_lo, n + 1)
                for g in range(NG):
                    if n >= 2:
                        pe.wait_ge(copied, NG * (n - 2) + g + 1)
                    mine = slice(g * TG, (g + 1) * TG)
                    three_passes(nc, p_out[NG * (n % 2) + g][:, 0:TG],
                                 lambda k: (w_hi[:, n % 2, k, :], w_lo[:, n % 2, k, :]),
                                 lambda k: (hT_hi[:, k, mine], hT_lo[:, k, mine]), range(KD)).then_inc(projected, 1)


def score(nc, const, qiT, small, cache_idx_k, scores):
    with Scope(nc, "sc_") as s:
        weight = s.sbuf("weight", [P, NT, IH])
        cache = s.sbuf("cache", [P, 2, 2, P])
        keysT = s.sbuf("keysT", [P, BATCH_S, KEYS_S])
        spread = s.sbuf("spread", [P, 2, BATCH_S * (P + SEQ_S)])
        relu = s.sbuf("relu", [P, 2, 512])
        p_logit = [s.psum(f"p_logit{i}") for i in range(4)]
        p_keys = [s.psum(f"p_keys{i}", (P, 2, PAST)) for i in range(2)]
        names = ("cache_in0", "cache_in1", "weighted", "cleared", "spread_ready", "keys_turned", "keys_ready",
                 "new_keys", "logits", "rectified", "summed", "masked")
        (cache_in0, cache_in1, weighted, cleared, spread_ready, keys_turned, keys_ready, new_keys, logits, rectified,
         summed, masked) = (
            s.sem(n) for n in names)
        cache_in = (cache_in0, cache_in1)
        units = [(t, c, min(512, WIDTH[t] - c), h) for t in range(2, NTP) for c in range(0, WIDTH[t], 512)
                 for h in range(IH)] + [(NTP, 0, KEYS_S, h) for h in range(IH)]
        TURN_AT = [8 + 4 * i for i in range(BATCH_S // 2)]
        block = s.block()

        @block.sync
        def _(sp):
            for b in range(BATCH_S):
                if b >= 2:
                    sp.wait_ge(keys_turned, b - 1)
                for i in range(2):
                    sp.dma_start(cache[:, b % 2, :, i * HD:(i + 1) * HD],
                                 cache_idx_k[0, b].rearrange("(c p) d -> p c d", p=P)).then_inc(cache_in[b % 2], 16)

        @block.gpsimd
        def _(pool):
            nc.gpsimd.tensor_scalar(weight[:], small[:, :, 0:IH], 1.0 / 16.0, None, ALU.mult).then_inc(weighted, 1)
            nc.gpsimd.memset(spread[:], 0.0).then_inc(cleared, 1)
            pool.wait_ge(weighted, 1)
            pool.wait_ge(cleared, 1)
            for i in range(2):
                rows = slice(HD * i, HD * i + HD)
                if i:
                    pool.wait_ge(new_keys, i)
                nc.gpsimd.tensor_copy(keysT[rows, :, PAST:KEYS_S], qiT[rows, 2 + i, SEQ:TOK].rearrange(
                    "p (b j) -> p b j", b=BATCH_S)).then_inc(new_keys, 1)
            pool.wait_ge(new_keys, 2)
            for h in range(IH):
                if h:
                    pool.wait_ge(spread_ready, h)
                if h >= 2:
                    pool.wait_ge(logits, len(units) - IH + h - 1)
                rows = slice(HD * (h % 2), HD * (h % 2) + HD)
                nc.gpsimd.tensor_copy(diagonal(spread[rows, h % 2, :]), qiT[rows, h // 2, SEQ:TOK].rearrange(
                    "p (b j) -> p b j", b=BATCH_S)).then_inc(spread_ready, 1)

        @block.scalar
        def _(act):
            for u, (t, c, n, h) in enumerate(units):
                if u in TURN_AT:
                    i = TURN_AT.index(u)
                    act.wait_ge(keys_turned, 2 * i + 2)
                    nc.scalar.copy(keysT[:, 2 * i:2 * i + 2, 0:PAST], p_keys[i % 2][:]).then_inc(keys_ready, 1)
                act.wait_ge(logits, u + 1)
                if u >= 2:
                    act.wait_ge(summed, u - 1)
                nc.scalar.activation(relu[:, u % 2, 0:n], p_logit[u % 4][:, 0:n], ACT.Relu).then_inc(rectified, 1)

        @block.vector
        def _(dve):
            nc.vector.memset(scores[:, AT[0]:AT[2]], 0.0).then_inc(masked, 1)
            nc.vector.memset(scores[:, AT[NTP] + KEYS_S:SCORES], FILL)
            dve.wait_ge(masked, 1)
            for t in range(2):
                nc.vector.memset(scores[0:CHUNK, AT[t] + WIDTH[t] - CHUNK:AT[t] + WIDTH[t]], UNSELECTED)
            dve.wait_ge(weighted, 1)
            for u, (t, c, n, h) in enumerate(units):
                dve.wait_ge(rectified, u + 1)
                dst, w = scores[:, AT[t] + c:AT[t] + c + n], weight[:, t, h:h + 1]
                if h == 0:
                    nc.vector.tensor_scalar(dst, relu[:, u % 2, 0:n], w, None, ALU.mult).then_inc(summed, 1)
                else:
                    dve.wait_ge(summed, u)
                    nc.vector.scalar_tensor_tensor(out=dst, in0=relu[:, u % 2, 0:n], scalar=w, in1=dst,
                                                   op0=ALU.mult, op1=ALU.add).then_inc(summed, 1)
            dve.wait_ge(summed, len(units))
            for t in range(2, NTP):
                nc.vector.memset(scores[0:CHUNK, AT[t] + WIDTH[t] - CHUNK:AT[t] + WIDTH[t]], INADMISSIBLE)

        @block.tensor
        def _(pe):
            def turn_cache(b):
                pe.wait_ge(cache_in[b % 2], 32 * (b // 2 + 1))
                if b % 2 == 0 and b >= 4:
                    pe.wait_ge(keys_ready, b // 2 - 1)
                for c in range(2):
                    mm = nc.tensor.transpose(p_keys[(b // 2) % 2][:, b % 2, c * P:(c + 1) * P], cache[:, b % 2, c, :],
                                             const[:, IDENT, :])
                mm.then_inc(keys_turned, 1)

            for u, (t, c, n, h) in enumerate(units):
                if u in TURN_AT:
                    turn_cache(2 * TURN_AT.index(u))
                    turn_cache(2 * TURN_AT.index(u) + 1)
                if u >= 4:
                    pe.wait_ge(rectified, u - 3)
                if t < NTP:
                    nc.tensor.matmul(p_logit[u % 4][:, 0:n], qiT[:, h // 2, t * P:(t + 1) * P],
                                     qiT[:, 2 + h % 2, c:c + n], start=True, stop=True).then_inc(logits, 1)
                else:
                    pe.wait_ge(spread_ready, h + 1)
                    pe.wait_ge(keys_ready, BATCH_S // 2)
                    pe.wait_ge(new_keys, 2)
                    for b in range(BATCH_S):
                        mm = nc.tensor.matmul(p_logit[u % 4][:, 0:n], spread[:, h % 2, b * P:(b + 1) * P],
                                              keysT[:, b, :], start=(b == 0), stop=(b == BATCH_S - 1))
                    mm.then_inc(logits, 1)


def select_and_project(nc, const, hT_hi, hT_lo, w_in, scores, conv_w, state_conv, projected_d, conv_d, sums, tail):
    HIST = CONV_W - 1
    RUN_S = HIST + SEQ_S
    PAD = HIST + SEQ
    ADDS = CONV_W - 1
    NB = NC + HB + 2 * KD
    PAIRS = NC
    with Scope(nc, "sp_") as s:
        raw = s.sbuf("raw", [P, KD, P])
        w_hi, w_lo = s.sbuf("w_hi", [P, 2, KD, P], F32R), s.sbuf("w_lo", [P, 2, KD, P], F32R)
        stage = s.sbuf("stage", [P, 2, TOK])
        padded = s.sbuf("padded", [P, PAD + BATCH_S * RUN_S])
        square, third = s.sbuf("square", [P, TOK]), s.sbuf("third", [P, TOK])
        taps = s.sbuf("taps", [P, NC, CONV_W])
        state = tail[:, :, HIST:]
        best = s.sbuf("best", [P, NT, 8])
        p_out = [s.psum(f"p_out{i}") for i in range(2 * NG)]
        p_small, p_sum = s.psum("p_small"), s.psum("p_sum")
        names = ("w_raw", "w_split_hi", "w_split_lo", "projected", "copied", "stored0", "stored1", "small_in",
                 "small_turned", "small_ready", "cleared", "filled", "old_filled", "tailed", "multiplied", "conv_done", "silu_done",
                 "squared", "summed", "sums_kept")
        (w_raw, w_split_hi, w_split_lo, projected, copied, stored0, stored1, small_in, small_turned, small_ready,
         cleared, filled, old_filled, tailed, multiplied, conv_done, silu_done, squared, summed, sums_kept) = (
            s.sem(n) for n in names)
        stored = (stored0, stored1)
        w = w_in.rearrange("(k p) c -> p k c", p=P)
        landing = stage[:].rearrange("p a t -> p (a t)")
        state_in, taps_in = landing[0:BATCH_S * HIST, 0:CONV_CH], landing[0:CONV_W * NC, CONV_CH:CONV_CH + P]
        decode_part = padded[:, PAD:].rearrange("p (b c) -> p b c", b=BATCH_S)
        block = s.block()

        def in_pairs(eng, pair):
            pair(0, "z", False)
            with eng.Fori(1, HB) as i:
                pair(i, "z", True)
            with eng.Fori(HB, 2 * HB) as i:
                pair(i, "gate", True)
            pair(2 * HB, "gate", True)
            with eng.Fori(2 * HB + 1, PAIRS) as i:
                pair(i, "gate", False)

        @block.sync
        def _(sp):
            def load(n, column):
                if not known(n, 1):
                    sp.wait_ge(w_split_lo, n)
                sp.dma_start(raw[:], w[:, :, bass.ds(column, P)]).then_inc(w_raw, 16)

            def pair(i, kind, sums_due):
                load(2 * i, i * P + C_CONV)
                load(2 * i + 1, i * P + C_Z if kind == "z" else (i - HB) * P + C_GATE)

            sp.dma_start(taps_in, conv_w.rearrange("j (n p) -> (j n) p", p=P)).then_inc(small_in, 16)
            sp.dma_start(state_in, state_conv[0].rearrange("b j c -> (b j) c")).then_inc(small_in, 16)
            in_pairs(sp, pair)
            in_steps(sp, lambda n, q: load(n, (n - PAIRS - HB) * P + C_GATE), 2 * PAIRS, NB, lead=0)
            for q in range(2):
                sp.wait_ge(stored[q], 16 * (NB // 2))

        @block.scalar
        def _(act):
            def split(n, q):
                act.wait_ge(w_raw, 16 * n + 16)
                if not known(n, 2):
                    act.wait_ge(projected, NG * (n - 1))
                nc.scalar.copy(w_hi[:, q], raw[:]).then_inc(w_split_hi, 1)

            def keep_channels(i):
                n = 2 * i
                if not known(i, 1):
                    act.wait_ge(tailed, i)
                for g in range(NG):
                    act.wait_ge(projected, NG * n + g + 1)
                    first, last = g * TG, min((g + 1) * TG, SEQ)
                    if last < (g + 1) * TG:
                        nc.scalar.copy(decode_part[:, :, HIST:RUN_S], p_out[g][:, last - first:TG].rearrange(
                            "p (b c) -> p b c", b=BATCH_S)).then_inc(filled, 1)
                    nc.scalar.copy(padded[:, HIST + first:HIST + last], p_out[g][:, 0:last - first]).then_inc(copied, 1)

            def multiply(i, j):
                if j == 0:
                    act.wait_ge(copied, 2 * NG * i + NG)
                    act.wait_ge(filled, i + 1)
                    act.wait_ge(old_filled, i + 1)
                    if known(i, 1):
                        act.wait_ge(small_ready, 2)
                    else:
                        act.wait_ge(stored[0], 16 * i)
                elif j == 1:
                    if not known(i, 1):
                        act.wait_ge(conv_done, ADDS * i)
                elif j == 3:
                    act.wait_ge(conv_done, ADDS * i + 1)
                dst = (stage[:, 0], square, third, square)[j]
                nc.scalar.activation(dst[:, 0:SEQ], padded[:, j:j + SEQ], ACT.Copy, scale=taps[:, i, j:j + 1])
                nc.scalar.activation(dst[:, SEQ:TOK].rearrange("p (b c) -> p b c", b=BATCH_S),
                                     decode_part[:, :, j:j + SEQ_S], ACT.Copy,
                                     scale=taps[:, i, j:j + 1]).then_inc(multiplied, 1)

            def keep_gates(n, q, func, at, after_first=None):
                if not known(n, 2):
                    act.wait_ge(stored[q], 8 * (n - q))
                for g in range(NG):
                    act.wait_ge(projected, NG * n + g + 1)
                    nc.scalar.activation(stage[:, q, g * TG:(g + 1) * TG], p_out[NG * q + g][:, 0:TG],
                                         func).then_inc(copied, 1)
                    if g == 0 and after_first:
                        after_first()
                act.wait_ge(copied, NG * n + NG)
                act.dma_start(projected_d[bass.ds(at, 1)].rearrange("a p t -> p (a t)"), stage[:, q]).then_inc(stored[q], 16)

            def keep_sums(i):
                act.wait_ge(summed, i)
                nc.scalar.copy(sums[:, i - 1, :], p_sum[:, 0:NT]).then_inc(sums_kept, 1)

            def silu_and_square(i, sums_due):
                act.wait_ge(conv_done, ADDS * (i + 1))
                nc.scalar.activation(stage[:, 0], stage[:, 0], ACT.Silu).then_inc(silu_done, 1)
                act.wait_ge(silu_done, i + 1)
                act.dma_start(conv_d[bass.ds(i, 1)].rearrange("a p t -> p (a t)"), stage[:, 0]).then_inc(stored[0], 16)
                if known(i, 2 * HB + 1) and i == 2 * HB or not (sums_due or known(i, 1)):
                    return
                if not known(i, 1):
                    act.wait_ge(summed, i)
                nc.scalar.activation(square[:], stage[:, 0], ACT.Square).then_inc(squared, 1)

            def pair(i, kind, sums_due):
                keep_channels(i)
                split(2 * i + 2, 0)
                if sums_due:
                    keep_sums(i)
                for j in range(3):
                    multiply(i, j)
                keep_gates(2 * i + 1, 1, ACT.Silu if kind == "z" else ACT.Sigmoid, i, lambda: multiply(i, 3))
                split(2 * i + 3, 1)
                silu_and_square(i, sums_due)

            def rest(n, q):
                keep_gates(n, q, ACT.Sigmoid, n - PAIRS)
                if not known(n, NB) or n + 2 < NB:
                    split(n + 2, q)

            split(0, 0)
            split(1, 1)
            act.wait_ge(small_turned, 2)
            nc.scalar.copy(taps[:], p_small[:, 0:CONV_W * NC].rearrange("p (j n) -> p n j", n=NC)).then_inc(small_ready, 1)
            nc.scalar.copy(state, p_small[:, CONV_W * NC:CONV_W * NC + NC * BATCH_S * HIST].rearrange(
                "p (n c) -> p n c", n=NC)).then_inc(small_ready, 1)
            in_pairs(act, pair)
            in_steps(act, rest, 2 * PAIRS, NB - 2, lead=0)
            in_steps(act, rest, NB - 2, NB)

        @block.gpsimd
        def _(pool):
            def split(n, q):
                pool.wait_ge(w_split_hi, n + 1)
                nc.gpsimd.tensor_tensor(w_lo[:, q], raw[:], w_hi[:, q].bitcast(F32), ALU.subtract).then_inc(w_split_lo, 1)

            def convolve(i):
                if not known(i, 1):
                    pool.wait_ge(multiplied, CONV_W * i)
                nc.gpsimd.tensor_copy(decode_part[:, :, 0:HIST], state[:, i, :].rearrange(
                    "p (b j) -> p b j", b=BATCH_S)).then_inc(old_filled, 1)
                pool.wait_ge(copied, 2 * NG * i + NG)
                pool.wait_ge(filled, i + 1)
                pool.wait_ge(old_filled, i + 1)
                nc.gpsimd.tensor_copy(tail[:, i, 0:HIST], padded[:, PAD - HIST:PAD])
                nc.gpsimd.tensor_copy(tail[:, i, HIST:].rearrange("p (b j) -> p b j", b=BATCH_S),
                                      decode_part[:, :, SEQ_S:RUN_S]).then_inc(tailed, 1)
                for j, product in ((1, square), (2, third), (3, square)):
                    pool.wait_ge(multiplied, CONV_W * i + j + 1)
                    if j > 1:
                        pool.wait_ge(conv_done, ADDS * i + j - 1)
                    nc.gpsimd.tensor_tensor(stage[:, 0], stage[:, 0], product[:], ALU.add).then_inc(conv_done, 1)

            def pair(i, kind, sums_due):
                split(2 * i + 2, 0)
                convolve(i)
                split(2 * i + 3, 1)

            nc.gpsimd.memset(padded[:, 0:HIST], 0.0).then_inc(cleared, 1)
            split(0, 0)
            split(1, 1)
            pool.wait_ge(small_ready, 2)
            pool.wait_ge(cleared, 1)
            in_pairs(pool, pair)
            in_steps(pool, split, 2 * PAIRS + 2, NB)

        @block.vector
        def _(dve):
            def row(t):
                return scores[:, AT[t]:AT[t] + WIDTH[t] + (PAD_S if t == NTP else 0)]

            def find(tiles):
                for t in tiles:
                    nc.vector.max(best[:, t, :], row(t))
                dve.drain()

            def take(tiles):
                for t in tiles:
                    nc.vector.match_replace(row(t), best[:, t, :], row(t), TAKEN)
                dve.drain()

            for tiles in ((2, 3), (4, 5), (6, 7)):
                with dve.Fori(0, TOPK_P // 8):
                    find(tiles)
                    take(tiles)
            with dve.Fori(0, TOPK_S // 8):
                find([NTP])
                take([NTP])
            find([NTP])
            nc.vector.memset(best[:, NTP, TOPK_S % 8:8], FILL)
            dve.drain()
            take([NTP])
            todo = scores[:, AT[2]:SCORES]
            nc.vector.tensor_scalar(todo, todo, TAKEN, UNSELECTED, ALU.not_equal, ALU.mult)

        @block.tensor
        def _(pe):
            def project(n, q):
                pe.wait_ge(w_split_lo, n + 1)
                for g in range(NG):
                    if not known(n, 2):
                        pe.wait_ge(copied, NG * (n - 2) + g + 1)
                    mine = slice(g * TG, (g + 1) * TG)
                    three_passes(nc, p_out[NG * q + g][:, 0:TG], lambda k: (w_hi[:, q, k, :], w_lo[:, q, k, :]),
                                 lambda k: (hT_hi[:, k, mine], hT_lo[:, k, mine]), range(KD)).then_inc(projected, 1)

            def sum_squares(i):
                pe.wait_ge(squared, i)
                if not known(i, 2):
                    pe.wait_ge(sums_kept, i - 1)
                for t in range(NT):
                    mm = nc.tensor.matmul(p_sum[:, t:t + 1], square[:, t * P:(t + 1) * P], const[:, ONES, 0:1],
                                          start=True, stop=True)
                mm.then_inc(summed, 1)

            def pair(i, kind, sums_due):
                project(2 * i, 0)
                if sums_due:
                    sum_squares(i)
                project(2 * i + 1, 1)

            pe.wait_ge(small_in, 32)
            nc.tensor.transpose(p_small[:, 0:CONV_W * NC], taps_in, const[0:CONV_W * NC, IDENT, 0:CONV_W * NC]).then_inc(
                small_turned, 1)
            H = BATCH_S * HIST
            for n in range(NC):
                mm = nc.tensor.transpose(p_small[:, CONV_W * NC + n * H:CONV_W * NC + (n + 1) * H],
                                         state_in[:, n * P:(n + 1) * P], const[0:H, IDENT, 0:H])
            mm.then_inc(small_turned, 1)
            in_pairs(pe, pair)
            in_steps(pe, project, 2 * PAIRS, NB, lead=0)


def attend(nc, const, qkT, va, scores, cache_k, cache_v, attended_d, sums, inv_norm, tail, new_conv, new_conv_s):
    HIST = CONV_W - 1
    LAST = HIST * (1 + BATCH_S)
    with Scope(nc, "at_") as s:
        parts, swapped = s.sbuf("parts", [P, KV, 5, SEQ], F32R), s.sbuf("swapped", [P, KV, SEQ], F32R)
        cache, keysT = s.sbuf("cache", [P, 2, 2, 2, P]), s.sbuf("keysT", [P, BATCH_S, KEYS_S])
        values, own_values = s.sbuf("values", [P, BATCH_S, 2, P]), s.sbuf("own_values", [SEQ_S, BATCH_S, P])
        spread = s.sbuf("spread", [P, BATCH_S, P])
        pick = s.sbuf("pick", [P, BATCH_S, P])
        masked, prob, probT = (s.sbuf(n, [P, 2 * SEQ]) for n in ("masked", "prob", "probT"))
        o_tok, oT = s.sbuf("o_tok", [P, 2, 512]), s.sbuf("oT", [P, 2, 4, P])
        o_dec = s.sbuf("o_dec", [P, 2, HD])
        root, tail_tok = s.sbuf("root", [P, NT, 2 * HB]), s.sbuf("tail_tok", [LAST, 512])
        oT_dec = masked[0:HD, 0:HEADS * P].rearrange("p (h t) -> p h t", h=HEADS)
        top, shift, total, rtotal = (s.sbuf(n, [P, 4]) for n in ("top", "shift", "total", "rtotal"))
        p_s = s.psum("p_s", (P, 2 * SEQ))
        p_pT = [s.psum(f"p_pT{i}", (P, 4, P)) for i in range(2)]
        p_o, p_oT = s.psum("p_o"), s.psum("p_oT", (P, 4, P))
        names = ("cache_in0", "cache_in1", "values_in", "own_in", "cleared", "spread_ready", "picks_ready", "keys_turned",
                 "keys_ready", "new_keys", "split_hi", "split_lo", "scored", "topped", "shifted", "exped", "prob_turned",
                 "probT_ready", "weighed", "inverted", "normed", "o_turned", "oT_ready", "stored0", "stored1", "stored_dec",
                 "squares_in", "rooted", "root_inverted", "tail_turned", "tail_kept", "tail_stored")
        (cache_in0, cache_in1, values_in, own_in, cleared, spread_ready, picks_ready, keys_turned, keys_ready, new_keys, split_hi,
         split_lo, scored, topped, shifted, exped, prob_turned, probT_ready, weighed, inverted, normed, o_turned,
         oT_ready, stored0, stored1, stored_dec, squares_in, rooted, root_inverted, tail_turned, tail_kept,
         tail_stored) = (s.sem(n) for n in names)
        cache_in, stored = (cache_in0, cache_in1), (stored0, stored1)
        units = [(t, j, kv) for t in range(NTP) for j in range(4) for kv in range(KV)] + [
            (NTP, b, 0) for b in range(BATCH_S)]
        U, DEC = len(units), HEADS * NTP

        def cols(u):
            width = WIDTH[units[u][0]]
            at = (u % 2) * SEQ if width > 512 else (u % 4) * 512
            return at, width

        def same_place(u):
            def place(v):
                at, width = cols(v)
                return set(range(at // 512, (at + width + 511) // 512))
            return max([v + 1 for v in range(u) if place(v) & place(u)], default=0)

        def coming(slot):
            return [v for v in range(U) if max(v - (1 if cols(v)[1] > 512 else 2), -1) == slot]

        groups = [(1 if t == NTP else (WIDTH[t] // P + 3) // 4) for t, _, _ in units]
        before = [sum(groups[:u]) for u in range(U + 1)]
        own, other = (slice(0, HD), slice(HD, P)), (slice(HD, P), slice(0, HD))
        block = s.block()

        @block.sync
        def _(sp):
            for i in range(BATCH_S // 2):
                if i >= 2:
                    sp.wait_ge(keys_turned, i - 1)
                sp.dma_start(cache[:, i % 2], cache_k[0, 2 * i:2 * i + 2].rearrange(
                    "b (c p) n d -> p b c (n d)", p=P)).then_inc(cache_in[i % 2], 16)
            sp.dma_start(values[:], cache_v[0].rearrange("b (c p) n d -> p b c (n d)", p=P)).then_inc(values_in, 16)
            for b in range(BATCH_S):
                sp.dma_start(own_values[:, b, :], va[b * SEQ_S:(b + 1) * SEQ_S, NTP, :]).then_inc(own_in, 16)
            for i in range(3):
                cols = slice(i * 512, (i + 1) * 512)
                sp.wait_ge(tail_kept, i + 1)
                sp.dma_start(new_conv[0, 0][:, cols], tail_tok[0:HIST, :]).then_inc(tail_stored, 16)
                sp.dma_start(new_conv_s[0].rearrange("b j c -> (b j) c")[:, cols], tail_tok[HIST:, :]).then_inc(
                    tail_stored, 16)
            sp.wait_ge(tail_stored, 96)
            for t in range(NTP):
                sp.wait_ge(oT_ready, t + 1)
                sp.dma_start(attended_d[:, :, t * P:(t + 1) * P].rearrange("j p t -> p j t"), oT[:, t % 2]).then_inc(
                    stored[t % 2], 16)
            sp.wait_ge(oT_ready, NTP + 2)
            sp.dma_start(attended_d.rearrange("j (i d) t -> d (j i) t", d=HD)[:, :, SEQ:TOK], oT_dec[:]).then_inc(
                stored_dec, 16)
            for q in range(2):
                sp.wait_ge(stored[q], 16 * (NTP // 2))
            sp.wait_ge(stored_dec, 16)

        @block.gpsimd
        def _(pool):
            def split(t):
                mine = slice(t * P, (t + 1) * P)
                for kv in range(KV):
                    pool.wait_ge(split_hi, 2 * t + kv + 1)
                    if t or kv:
                        pool.wait_ge(split_lo, 4 * t + 2 * kv)
                    hi = parts[own[kv], kv, :, mine].bitcast(F32)
                    nc.gpsimd.tensor_tensor(parts[other[kv], kv, :, mine], qkT[own[kv], :, mine], hi,
                                            ALU.subtract).then_inc(split_lo, 1)
                    pool.wait_ge(split_lo, 4 * t + 2 * kv + 1)
                    nc.gpsimd.tensor_tensor(swapped[own[kv], kv, mine], qkT[own[kv], 4, mine],
                                            parts[own[kv], kv, 4, mine].bitcast(F32), ALU.subtract).then_inc(split_lo, 1)

            split(0)
            split(1)
            pool.wait_ge(split_lo, 8)
            nc.gpsimd.memset(spread[:], 0.0).then_inc(cleared, 1)
            pool.wait_ge(cleared, 1)
            for kv in range(KV):
                if kv:
                    pool.wait_ge(spread_ready, kv)
                nc.gpsimd.tensor_copy(
                    spread[own[kv], :, own[kv]].rearrange("p b (j c) -> p b j c", j=4),
                    qkT[own[kv], 0:4, SEQ:TOK].rearrange("p j (b c) -> p b j c", b=BATCH_S)).then_inc(spread_ready, 1)
            pool.wait_ge(spread_ready, KV)
            nc.gpsimd.tensor_copy(keysT[:, :, PAST:KEYS_S], qkT[:, 4, SEQ:TOK].rearrange(
                "p (b c) -> p b c", b=BATCH_S)).then_inc(new_keys, 1)
            nc.gpsimd.tensor_copy(pick[:].rearrange("p b (h c) -> p b h c", h=HEADS), const[:, IDENT, :].rearrange(
                "p (b a c) -> p b a c", b=BATCH_S, a=1).to_broadcast([P, BATCH_S, HEADS, SEQ_S])).then_inc(picks_ready, 1)
            pool.wait_ge(new_keys, 1)
            pool.wait_ge(picks_ready, 1)
            for t in range(2, NTP):
                split(t)

        @block.tensor
        def _(pe):
            def turn_cache(i):
                pe.wait_ge(cache_in[i % 2], 16 * (i // 2 + 1))
                if i:
                    pe.wait_ge(keys_ready, i)
                for k in range(4):
                    mm = nc.tensor.transpose(p_oT[:, k, :], cache[:, i % 2, k // 2, k % 2, :], const[:, IDENT, :])
                mm.then_inc(keys_turned, 1)

            def turn_tail(i):
                if i == 0:
                    pe.wait_ge(keys_ready, BATCH_S // 2)
                else:
                    pe.wait_ge(tail_kept, i)
                for n in range(4):
                    mm = nc.tensor.transpose(p_oT[0:LAST, n, :], tail[:, 4 * i + n, :], const[:, IDENT, :])
                mm.then_inc(tail_turned, 1)

            def query_keys(u):
                t, j, kv = units[u]
                at, width = cols(u)
                if same_place(u):
                    pe.wait_ge(topped, same_place(u))
                    if same_place(u) > DEC:
                        pe.wait_ge(exped, same_place(u))
                if t < NTP:
                    pe.wait_ge(split_lo, 4 * t + 4)
                    queries = parts[:, kv, j, t * P:(t + 1) * P]
                    for c in range(0, width, 512):
                        keys = slice(c, min(c + 512, width))
                        out = p_s[:, at + keys.start:at + keys.stop]
                        nc.tensor.matmul(out, queries, parts[:, kv, 4, keys], start=True, stop=False)
                        mm = nc.tensor.matmul(out, queries, swapped[:, kv, keys], start=False, stop=True)
                else:
                    pe.wait_ge(spread_ready, KV)
                    pe.wait_ge(new_keys, 1)
                    pe.wait_ge(keys_ready, BATCH_S // 2)
                    out = p_s[:, at:at + KEYS_S]
                    nc.tensor.matmul(out, spread[:, j, :], keysT[:, j, :], start=True, stop=False)
                    pe.wait_ge(picks_ready, 1)
                    mm = nc.tensor.matmul(out, pick[:, j, :],
                        scores[:, AT[NTP]:AT[NTP] + KEYS_S], start=False, stop=True)
                mm.then_inc(scored, 1)

            def turn(u):
                at, width = cols(u)
                pe.wait_ge(exped, u + 1)
                n = (width + P - 1) // P
                for g in range(groups[u]):
                    if before[u] + g >= 2:
                        pe.wait_ge(probT_ready, before[u] + g - 1)
                    for k in range(4 * g, min(4 * g + 4, n)):
                        rows = min(P, width - k * P)
                        mm = nc.tensor.transpose(p_pT[(before[u] + g) % 2][0:rows, k - 4 * g, :],
                                                 prob[:, at + k * P:at + k * P + rows], const[:, IDENT, :])
                    mm.then_inc(prob_turned, 1)

            def weigh(u):
                t, j, kv = units[u]
                at, width = cols(u)
                pe.wait_ge(probT_ready, before[u + 1])
                if u >= 1:
                    pe.wait_ge(normed, u)
                if t == NTP:
                    pe.wait_ge(values_in, 16)
                    pe.wait_ge(own_in, 16 * BATCH_S)
                n = (width + P - 1) // P
                for k in range(n):
                    rows = min(P, width - k * P)
                    v = va[:, k, :] if t < NTP else values[:, j, k, :] if k < 2 else own_values[:, j, :]
                    mm = nc.tensor.matmul(p_o[:, 0:P], probT[0:rows, at + k * P:at + (k + 1) * P], v, start=(k == 0),
                                          stop=(k == n - 1))
                mm.then_inc(weighed, 1)

            def turn_out(t):
                pe.wait_ge(normed, HEADS * (t + 1))
                if t == 0:
                    pe.wait_ge(tail_kept, 3)
                else:
                    pe.wait_ge(oT_ready, t)
                for j in range(4):
                    mm = nc.tensor.transpose(p_oT[:, j, :], o_tok[:, t % 2, j * P:(j + 1) * P], const[:, IDENT, :])
                mm.then_inc(o_turned, 1)

            def turn_out_dec(b):
                pe.wait_ge(normed, DEC + b + 1)
                if b % 4 == 0:
                    pe.wait_ge(oT_ready, NTP + b // 4)
                nc.tensor.transpose(p_oT[0:HD, b % 4, :], o_dec[:, b % 2, :], const[:, IDENT, :]).then_inc(o_turned, 1)

            for v in coming(-1):
                query_keys(v)
            for u in range(U):
                for v in coming(u):
                    query_keys(v)
                turn(u)
                if u >= 1:
                    weigh(u - 1)
                if 1 <= u <= BATCH_S // 2:
                    turn_cache(u - 1)
                if BATCH_S // 2 < u <= BATCH_S // 2 + 3:
                    turn_tail(u - BATCH_S // 2 - 1)
                if u % HEADS == 2 and HEADS < u <= DEC + 2:
                    turn_out(u // HEADS - 1)
                if u >= DEC + 3:
                    turn_out_dec(u - DEC - 3)
            weigh(U - 1)
            for b in range(BATCH_S - 3, BATCH_S):
                turn_out_dec(b)

        @block.vector
        def _(dve):
            def mask_and_top(u):
                t = units[u][0]
                at, width = cols(u)
                q = slice(u % 4, u % 4 + 1)
                dve.wait_ge(scored, u + 1)
                if max(same_place(u), u - 3) > 0:
                    dve.wait_ge(exped, max(same_place(u), u - 3))
                if t < NTP:
                    nc.vector.tensor_tensor_reduce(masked[:, at:at + width], p_s[:, at:at + width],
                                                   scores[:, AT[t]:AT[t] + width], 1.0, -3.4e38, ALU.add, ALU.max,
                                                   top[:, q]).then_inc(topped, 1)
                else:
                    nc.vector.tensor_reduce(top[:, q], p_s[:, at:at + width], AX.X, ALU.max).then_inc(topped, 1)
                dve.wait_ge(topped, u + 1)
                nc.vector.tensor_scalar(shift[:, q], top[:, q], -HD ** -0.5, None, ALU.mult).then_inc(shifted, 1)

            def norm(u):
                t, j, kv = units[u]
                q = slice(u % 4, u % 4 + 1)
                dve.wait_ge(exped, u + 1)
                nc.vector.reciprocal(rtotal[:, q], total[:, q]).then_inc(inverted, 1)
                dve.wait_ge(inverted, u + 1)
                dve.wait_ge(weighed, u + 1)
                if t < NTP:
                    head = j + 4 * kv
                    if u % HEADS == 0 and t >= 2:
                        dve.wait_ge(o_turned, t - 1)
                    nc.vector.tensor_scalar(o_tok[:, t % 2, head * HD:(head + 1) * HD], p_o[:, own[kv]], rtotal[:, q],
                                            None, ALU.mult).then_inc(normed, 1)
                else:
                    if j >= 2:
                        dve.wait_ge(o_turned, NTP + j - 1)
                    for half in own:
                        mul = nc.vector.tensor_scalar(o_dec[half, j % 2, :], p_o[half, half], rtotal[half, q], None,
                                                      ALU.mult)
                    mul.then_inc(normed, 1)

            nc.vector.tensor_scalar(inv_norm[:], sums[:, 0:2 * HB, :].rearrange("p n t -> p t n"), EPS, None,
                                    ALU.add).then_inc(squares_in, 1)
            for v in coming(-1):
                mask_and_top(v)
            for u in range(U):
                for v in coming(u):
                    mask_and_top(v)
                if u >= 1:
                    norm(u - 1)
            norm(U - 1)
            dve.wait_ge(rooted, 1)
            nc.vector.reciprocal(inv_norm[:], root[:]).then_inc(root_inverted, 1)
            dve.wait_ge(root_inverted, 1)
            nc.vector.tensor_scalar(inv_norm[:, :, 0:HB], inv_norm[:, :, 0:HB], DK ** -0.5, None, ALU.mult)

        @block.scalar
        def _(act):
            def split(t):
                mine = slice(t * P, (t + 1) * P)
                for kv in range(KV):
                    nc.scalar.copy(swapped[other[kv], kv, mine], qkT[own[kv], 4, mine])
                    nc.scalar.copy(parts[own[kv], kv, :, mine], qkT[own[kv], :, mine]).then_inc(split_hi, 1)

            def exp(u):
                at, width = cols(u)
                q = slice(u % 4, u % 4 + 1)
                act.wait_ge(shifted, u + 1)
                if same_place(u):
                    act.wait_ge(prob_turned, before[same_place(u)])
                if u >= 4:
                    act.wait_ge(inverted, u - 3)
                src = masked if units[u][0] < NTP else p_s
                nc.scalar.activation(prob[:, at:at + width], src[:, at:at + width], ACT.Exp, bias=shift[:, q],
                                     scale=HD ** -0.5, accum_out=total[:, q]).then_inc(exped, 1)

            def keep_turned(u):
                at, width = cols(u)
                if same_place(u):
                    act.wait_ge(weighed, same_place(u))
                for g in range(groups[u]):
                    act.wait_ge(prob_turned, before[u] + g + 1)
                    bank = p_pT[(before[u] + g) % 2]
                    full = min(4, width // P - 4 * g)
                    first = at + 4 * g * P
                    if units[u][0] < NTP:
                        nc.scalar.copy(probT[:, first:first + full * P].rearrange("p (k q) -> p k q", k=full),
                                       bank[:, 0:full, :]).then_inc(probT_ready, 1)
                    else:
                        nc.scalar.copy(probT[:, first:first + full * P].rearrange("p (k q) -> p k q", k=full),
                                       bank[:, 0:full, :])
                        nc.scalar.copy(probT[0:SEQ_S, first + full * P:first + (full + 1) * P],
                                       bank[0:SEQ_S, full, :]).then_inc(probT_ready, 1)

            def keep_out(t):
                act.wait_ge(o_turned, t + 1)
                if t >= 2:
                    act.wait_ge(stored[t % 2], 16 * (t // 2))
                nc.scalar.copy(oT[:, t % 2], p_oT[:]).then_inc(oT_ready, 1)

            def keep_out_dec(i):
                act.wait_ge(o_turned, NTP + 4 * i + 4)
                nc.scalar.copy(oT_dec[:, :, 4 * i * SEQ_S:4 * (i + 1) * SEQ_S].rearrange("p h (b c) -> p b h c", b=4),
                               p_oT[0:HD].rearrange("p b (h c) -> p b h c", h=HEADS)).then_inc(oT_ready, 1)

            split(0)
            split(1)
            exp(0)
            for u in range(U):
                if u + 1 < U:
                    exp(u + 1)
                keep_turned(u)
                if 1 <= u <= BATCH_S // 2:
                    act.wait_ge(keys_turned, u)
                    nc.scalar.copy(keysT[:, 2 * u - 2:2 * u, 0:PAST].rearrange("p b (c s) -> p b c s", c=2),
                                   p_oT[:].rearrange("p (b c) s -> p b c s", b=2)).then_inc(keys_ready, 1)
                if BATCH_S // 2 < u <= BATCH_S // 2 + 3:
                    i = u - BATCH_S // 2 - 1
                    act.wait_ge(tail_turned, i + 1)
                    if i:
                        act.wait_ge(tail_stored, 32 * i)
                    nc.scalar.copy(tail_tok[:].rearrange("p (n c) -> p n c", n=4), p_oT[0:LAST]).then_inc(tail_kept, 1)
                if u % HEADS == 0 and 2 <= u // HEADS + 2 < NTP:
                    split(u // HEADS + 2)
                if u % HEADS == 3 and HEADS < u <= DEC + 3:
                    keep_out(u // HEADS - 1)
                if u == DEC + 7:
                    keep_out_dec(0)
            act.wait_ge(squares_in, 1)
            nc.scalar.activation(root[:], inv_norm[:], ACT.Sqrt).then_inc(rooted, 1)
            keep_out_dec(1)


class Decays:

    def __init__(self, nc, kept):
        self.nc = nc
        self.beta, self.g, self.cum, self.c_key, self.c_last = (
            kept.sbuf(n, [P, NT, HB]) for n in ("beta", "g", "cum", "c_key", "c_last"))
        self.last_p, self.last_s = kept.sbuf("last_p", [P, NTP, HB]), kept.sbuf("last_s", [P, HB, BATCH_S])

    def open(self, s, const, small, a_log, dt_bias):
        self.const, self.small, self.a_log, self.dt_bias = const, small, a_log, dt_bias
        self.bias, self.rate = s.sbuf("bias", [P, HB]), s.sbuf("rate", [P, HB])
        self.a, self.absa, self.e, self.ln, self.e_cum, self.diff = (
            s.sbuf(n, [P, NT, HB]) for n in ("a", "absa", "e", "ln", "e_cum", "diff"))
        self.g_of = s.sbuf("g_of", [P, HB, BATCH_S])
        bank, n = s.psum("p_decays"), NT * HB
        self.p_cum, self.p_last, self.p_last_s = bank[:, 0:n], bank[:, n:2 * n], bank[:, 2 * n:2 * n + HB * BATCH_S]
        self.param_in, self.done_v, self.done_a, self.done_p = (
            s.sem(n) for n in ("param_in", "done_v", "done_a", "done_p"))

    def load(self, sp):
        sp.dma_start(self.bias[:], self.dt_bias.to_broadcast([P, HB])).then_inc(self.param_in, 16)
        sp.dma_start(self.rate[:], self.a_log.to_broadcast([P, HB])).then_inc(self.param_in, 16)

    def vector(self, dve):
        nc, a, e, rate, cum, count = self.nc, self.a, self.e, self.rate, self.cum, [0]

        def then(ins):
            count[0] += 1
            ins.then_inc(self.done_v, 1)
            dve.wait_ge(self.done_v, count[0])

        dve.wait_ge(self.param_in, 32)
        then(nc.vector.tensor_tensor(a[:], self.small[:, :, 8:12], self.bias[:].rearrange(
            "p (a h) -> p a h", a=1).to_broadcast([P, NT, HB]), ALU.add))
        then(nc.vector.scalar_tensor_tensor(out=self.absa[:], in0=a[:], scalar=-1.0, in1=a[:], op0=ALU.mult,
                                            op1=ALU.max))
        dve.wait_ge(self.done_a, 2)
        then(nc.vector.tensor_scalar(e[:], e[:], 1.0, None, ALU.add))
        then(nc.vector.tensor_scalar(a[:], a[:], 0.0, None, ALU.max))
        dve.wait_ge(self.done_a, 3)
        then(nc.vector.tensor_tensor(a[:], a[:], self.ln[:], ALU.add))
        then(nc.vector.tensor_scalar(rate[:], rate[:], -1.0, None, ALU.mult))
        then(nc.vector.tensor_tensor(self.g[:], a[:], rate[:].rearrange("p (a h) -> p a h", a=1).to_broadcast(
            [P, NT, HB]), ALU.mult))
        then(nc.vector.tensor_tensor(self.g_of[:], self.g[:, NTP, :].rearrange("p (h a) -> p h a", a=1).to_broadcast(
            [P, HB, BATCH_S]), self.const[:, BATCH_OF, 0:BATCH_S].rearrange("p (a b) -> p a b", a=1).to_broadcast(
            [P, HB, BATCH_S]), ALU.mult))

    def vector_end(self, dve):
        nc = self.nc
        dve.wait_ge(self.done_p, 1)
        nc.vector.tensor_copy(self.cum[:], self.p_cum.rearrange("p (t h) -> p t h", h=HB)).then_inc(self.done_v, 1)
        dve.wait_ge(self.done_v, 9)
        nc.vector.tensor_tensor(self.diff[:], self.p_last.rearrange("p (t h) -> p t h", h=HB), self.cum[:],
                                ALU.subtract).then_inc(self.done_v, 1)
        dve.wait_ge(self.done_a, 5)
        nc.vector.scalar_tensor_tensor(out=self.c_key[:], in0=self.beta[:], scalar=-1.0, in1=self.e_cum[:], op0=ALU.mult,
                                       op1=ALU.mult)

    def scalar(self, act):
        nc = self.nc
        act.wait_ge(self.param_in, 32)
        act.wait_ge(self.done_v, 2)
        nc.scalar.activation(self.e[:], self.absa[:], ACT.Exp, scale=-1.0).then_inc(self.done_a, 1)
        nc.scalar.activation(self.rate[:], self.rate[:], ACT.Exp).then_inc(self.done_a, 1)
        act.wait_ge(self.done_v, 3)
        nc.scalar.activation(self.ln[:], self.e[:], ACT.Ln).then_inc(self.done_a, 1)

    def scalar_end(self, act):
        nc = self.nc
        act.wait_ge(self.done_v, 9)
        nc.scalar.activation(self.e_cum[:], self.cum[:], ACT.Exp).then_inc(self.done_a, 1)
        act.wait_ge(self.done_v, 10)
        nc.scalar.activation(self.c_last[:], self.diff[:], ACT.Exp)
        nc.scalar.activation(self.last_p[:], self.p_last[:, 0:NTP * HB].rearrange("p (t h) -> p t h", h=HB), ACT.Exp)
        nc.scalar.activation(self.last_s[:], self.p_last_s.rearrange("p (h b) -> p h b", h=HB), ACT.Exp)
        nc.scalar.activation(self.beta[:], self.small[:, :, 4:8], ACT.Sigmoid).then_inc(self.done_a, 1)

    def tensor(self, pe):
        nc, const, NP = self.nc, self.const, NTP * HB
        pe.wait_ge(self.done_v, 8)
        prompt, own = self.g[:, 0:NTP, :].rearrange("p t h -> p (t h)"), self.g[:, NTP, :]
        nc.tensor.matmul(self.p_cum[:, 0:NP], const[:, UPTO, :], prompt, start=True, stop=True)
        nc.tensor.matmul(self.p_cum[:, NP:NP + HB], const[:, UPTO_S, :], own, start=True, stop=True)
        nc.tensor.matmul(self.p_last[:, 0:NP], const[:, ONES, :], prompt, start=True, stop=True)
        nc.tensor.matmul(self.p_last[:, NP:NP + HB], const[:, SAME_S, :], own, start=True, stop=True)
        nc.tensor.matmul(self.p_last_s, const[:, ONES, :], self.g_of[:].rearrange("p h b -> p (h b)"), start=True,
                         stop=True).then_inc(self.done_p, 1)


def over_heads(ap, n=P):
    return ap.rearrange("p (h a) -> p h a", a=1).to_broadcast([P, ap.shape[-1], n])


def for_heads(ap, n):
    return ap.rearrange("p (a c) -> p a c", a=1).to_broadcast([P, n, ap.shape[-1]])


def delta(nc, const, decays, inv_norm, conv_d, state_delta, out_d,
          new_state, new_state_s):
    beta, g, cum, c_key, c_last, last_p, last_s = (decays.beta, decays.g, decays.cum, decays.c_key, decays.c_last,
                                                   decays.last_p, decays.last_s)
    with Scope(nc, "dl_") as s:
        H2 = HB // 2
        qkv = s.sbuf("qkv", [P, 2, NC, P])
        khat, qhat, kT, qT, e_row, gap, E_up, E_low, low, g_cols = (s.sbuf(n, [P, HB, P]) for n in (
            "khat", "qhat", "kT", "qT", "e_row", "gap", "E_up", "E_low", "low", "g_cols"))
        Z = s.sbuf("Z", [P, HB, P])
        below = s.sbuf("below", [P, 2, LEVELS_P, HB, P])
        X, vb, kbg, kdec, qTe, attn, Y, wT = (s.sbuf(n, [P, 2, HB, P]) for n in (
            "X", "vb", "kbg", "kdec", "qTe", "attn", "Y", "wT"))
        V, S = s.sbuf("V", [P, HB, P]), s.sbuf("S", [P, HB, P])
        outT = s.sbuf("outT", [P, 2, HB, P])
        S_s = s.sbuf("S_s", [P, BATCH_S, HB, P])
        VT, V_of = s.sbuf("VT", [P, HB, P]), s.sbuf("V_of", [P, 2, BATCH_S, P])
        S_new = s.sbuf("S_new", [P, 2, BATCH_S, P])
        p_z, p_yx = ([s.psum(f"p_{n}{p}", (P, 4, P)) for p in range(2)] for n in ("z", "yx"))
        front_0, front_1, p_v, p_o = (s.psum(n, (P, HB, P)) for n in ("front_0", "front_1", "p_v", "p_o"))

        (k_turned, q_turned, v_turned, khat_turned, qhat_turned, rows_done, gram_k, gram_q, b0_turned, khat_ready,
         qhat_ready, vb_ready, kT_kept, qT_kept, gap_ready, clamped, e_row_done, e_done, low_ready, attn_ready,
         y_first, x_first, k_scaled, k_faded, q_scaled, attn_masked, g_spread) = (s.sem(n) for n in (
             "k_turned", "q_turned", "v_turned", "khat_turned", "qhat_turned", "rows_done", "gram_k", "gram_q",
             "b0_turned", "khat_ready", "qhat_ready", "vb_ready", "kT_kept", "qT_kept", "gap_ready", "clamped",
             "e_row_done", "e_done", "low_ready", "attn_ready", "y_first", "x_first", "k_scaled", "k_faded",
             "q_scaled", "attn_masked", "g_spread"))
        b_made = s.sem("b_made")
        z_done, z_kept, y_done, y_kept, x_done, x_kept, w_done, w_kept = ([s.sem(f"{n}{p}") for p in range(2)] for n in (
            "z_done", "z_kept", "y_done", "y_kept", "x_done", "x_kept", "w_done", "w_kept"))
        v_done, v_kept, o_done, o_kept, s_done, s_kept, cleared, final_stored = (s.sem(n) for n in (
            "v_done", "v_kept", "o_done", "o_kept", "s_done", "s_kept", "cleared", "final_stored"))
        state_in, vt_done, vt_kept, v_spread, ss_done, ss_kept = (s.sem(n) for n in (
            "state_in", "vt_done", "vt_kept", "v_spread", "ss_done", "ss_kept"))
        qkv_in, out_stored, new_stored = ([s.sem(f"{n}{q}") for q in range(2)] for n in (
            "qkv_in", "out_stored", "new_stored"))
        LP, LS = LEVELS_P, LEVELS_S
        STATE_AT = 5
        pair = [slice(H2 * p, H2 * p + H2) for p in range(2)]
        block = s.block()

        @block.sync
        def _(sp):
            def load(m, q):
                if not known(m, 2):
                    sp.wait_ge(v_turned, m - 1)
                sp.dma_start(qkv[:, q], conv_d[:, :, bass.ts(m, P)].rearrange("n p t -> p n t")).then_inc(qkv_in[q], 16)

            def store(n, q):
                sp.wait_ge(o_kept, n + 1)
                sp.dma_start(out_d[:, :, bass.ts(n, P)].rearrange("n p t -> p n t"), outT[:, q]).then_inc(
                    out_stored[q], 16)

            load(0, 0)
            load(1, 1)
            sp.dma_start(S_s[:], state_delta[0].rearrange("b h k v -> k b h v")).then_inc(state_in, 16)

            def step(n, q):
                load(n + 1, 1 - q)
                store(n - 1, 1 - q)

            in_steps(sp, step, 1, NTP)
            store(NTP - 1, 1)
            sp.wait_ge(s_kept, NTP)
            sp.dma_start(new_state[0, 0].rearrange("h k v -> k h v"), S[:]).then_inc(final_stored, 16)
            for h in range(HB):
                sp.wait_ge(ss_kept, 2 * (h + 1))
                sp.dma_start(new_state_s[0, :, h].rearrange("b k v -> k b v"), S_new[:, h % 2]).then_inc(
                    new_stored[h % 2], 16)
                if h == HB - 2:
                    store(NTP, 0)
            sp.wait_ge(final_stored, 16)
            for q in range(2):
                sp.wait_ge(new_stored[q], 32)
                sp.wait_ge(out_stored[q], 16 * ((NT + 1 - q) // 2))

        @block.tensor
        def _(pe):
            ident = const[:, IDENT, :]

            def turn_in(m, q, bank, at, done):
                pe.wait_ge(qkv_in[q], 8 * (m - q) + 16)
                for h in range(HB):
                    mm = nc.tensor.transpose(bank[:, h, :], qkv[:, q, at + h, :], ident)
                mm.then_inc(done, 1)

            def rows_and_k(m, q, decode):
                pe.wait_ge(g_spread, m + 1)
                if not known(m, 1):
                    pe.wait_ge(attn_ready, m)
                    pe.wait_ge(y_first, m)
                for h in range(HB):
                    mm = nc.tensor.matmul(front_1[:, h, :], g_cols[:, h, :], const[:, UPTO_S if decode else UPTO, :],
                                          start=True, stop=True)
                mm.then_inc(rows_done, 1)
                turn_in(m, q, front_0, HB, k_turned)

            def q_and_v(m, q):
                pe.wait_ge(e_row_done, m + 1)
                turn_in(m, q, front_1, 0, q_turned)
                pe.wait_ge(khat_ready, m + 1)
                turn_in(m, q, front_0, 2 * HB, v_turned)

            def turn_hats(m):
                pe.wait_ge(khat_ready, m + 1)
                pe.wait_ge(qhat_ready, m + 1)
                for h in range(HB):
                    mm = nc.tensor.transpose(front_1[:, h, :], khat[:, h, :], ident)
                mm.then_inc(khat_turned, 1)
                pe.wait_ge(vb_ready, m + 1)
                for h in range(HB):
                    mm = nc.tensor.transpose(front_0[:, h, :], qhat[:, h, :], ident)
                mm.then_inc(qhat_turned, 1)

            def grams_k(m):
                pe.wait_ge(kT_kept, m + 1)
                pe.wait_ge(qT_kept, m + 1)
                for h in range(HB):
                    mm = nc.tensor.matmul(front_0[:, h, :], kT[:, h, :], kT[:, h, :], start=True, stop=True)
                mm.then_inc(gram_k, 1)

            def grams_q(m):
                for h in range(HB):
                    mm = nc.tensor.matmul(front_1[:, h, :], kT[:, h, :], qT[:, h, :], start=True, stop=True)
                mm.then_inc(gram_q, 1)

            def turn_first(m, q):
                pe.wait_ge(b_made, LP * m + 1)
                pe.wait_ge(low_ready, m + 1)
                for h in range(HB):
                    mm = nc.tensor.transpose(front_0[:, h, :], below[:, q, 0, h, :], ident)
                mm.then_inc(b0_turned, 1)

            def z(n, q, i, p):
                if i == 1:
                    pe.wait_ge(y_first, n + 1)
                    if not known(n, 1):
                        pe.wait_ge(w_kept[p], n)
                else:
                    pe.wait_ge(y_kept[p], (LP - 1) * n + i - 1)
                pe.wait_ge(b_made, LP * n + i + 1)
                for h in range(H2):
                    mm = nc.tensor.matmul(p_z[p][:, h, :], below[:, q, i, H2 * p + h, :], Y[:, q, H2 * p + h, :],
                                          start=True, stop=True)
                mm.then_inc(z_done[p], 1)

            def y(n, q, i, p):
                pe.wait_ge(z_kept[p], (LP - 1) * n + i)
                if i == 1:
                    pe.wait_ge(x_first, n + 1)
                else:
                    pe.wait_ge(x_kept[p], (LP - 2) * n + i - 1)
                for h in range(H2):
                    mm = nc.tensor.matmul(p_yx[p][:, h, :], X[:, q, H2 * p + h, :], Z[:, H2 * p + h, :], start=True,
                                          stop=True)
                mm.then_inc(y_done[p], 1)

            def x(n, q, i, p):
                pe.wait_ge(y_kept[p], (LP - 1) * n + i)
                for h in range(H2):
                    mm = nc.tensor.matmul(p_yx[p][:, H2 + h, :], Z[:, H2 * p + h, :], X[:, q, H2 * p + h, :], start=True,
                                          stop=True)
                mm.then_inc(x_done[p], 1)

            def weights(n, q, levels):
                pe.wait_ge(k_scaled, n + 1)
                for p in range(2):
                    pe.wait_ge(y_kept[p], (LP - 1) * n + levels - 1)
                    for h in range(H2):
                        mm = nc.tensor.matmul(p_z[p][:, h, :], kbg[:, q, H2 * p + h, :], Y[:, q, H2 * p + h, :],
                                              start=True, stop=True)
                    mm.then_inc(w_done[p], 1)

            def new_values(n, q):
                for p in range(2):
                    pe.wait_ge(w_kept[p], n + 1)
                if known(n, 1):
                    pe.wait_ge(cleared, 1)
                else:
                    pe.wait_ge(s_kept, n)
                for h in range(HB):
                    nc.tensor.matmul(p_v[:, h, :], Y[:, q, h, :], vb[:, q, h, :], start=True, stop=False)
                    mm = nc.tensor.matmul(p_v[:, h, :], wT[:, q, h, :], S[:, h, :], start=False, stop=True)
                mm.then_inc(v_done, 1)

            def outputs(n, q):
                pe.wait_ge(v_kept, n + 1)
                if not known(n, 1):
                    pe.wait_ge(o_kept, n)
                pe.wait_ge(q_scaled, n + 1)
                pe.wait_ge(attn_masked, n + 1)
                for h in range(HB):
                    nc.tensor.matmul(p_o[:, h, :], S[:, h, :], qTe[:, q, h, :], start=True, stop=False)
                    mm = nc.tensor.matmul(p_o[:, h, :], V[:, h, :], attn[:, q, h, :], start=False, stop=True)
                mm.then_inc(o_done, 1)

            def state(n, q):
                pe.wait_ge(k_faded, n + 1)
                pe.wait_ge(v_kept, n + 1)
                for h in range(HB):
                    mm = nc.tensor.matmul(p_v[:, h, :], kdec[:, q, h, :], V[:, h, :], start=True, stop=True)
                mm.then_inc(s_done, 1)

            def step(n, q, ahead="prompt"):
                levels = LP if ahead else LS
                for i in range(1, levels):
                    z(n, q, i, 0)
                    if i > 1:
                        x(n, q, i - 1, 1)
                    z(n, q, i, 1)
                    if ahead and i == 1:
                        rows_and_k(n + 1, 1 - q, ahead == "decode")
                    if ahead and i == 2:
                        q_and_v(n + 1, 1 - q)
                    if ahead and i == 3:
                        turn_hats(n + 1)
                    if ahead and i == 4:
                        grams_k(n + 1)
                    if ahead and i == 6:
                        turn_first(n + 1, 1 - q)
                    y(n, q, i, 0)
                    y(n, q, i, 1)
                    if not known(n, 1):
                        if i == 1:
                            new_values(n - 1, 1 - q)
                        if i == 2:
                            outputs(n - 1, 1 - q)
                        if i == min(STATE_AT, levels - 1):
                            state(n - 1, 1 - q)
                    if ahead and i == 4:
                        grams_q(n + 1)
                    if i < levels - 1:
                        x(n, q, i, 0)
                weights(n, q, levels)

            rows_and_k(0, 0, False)
            q_and_v(0, 0)
            turn_hats(0)
            grams_k(0)
            grams_q(0)
            turn_first(0, 0)
            in_steps(pe, step, 0, NTP - 1)
            step(NTP - 1, 1, "decode")
            step(NTP, 0, None)
            for p in range(2):
                pe.wait_ge(w_kept[p], NT)
            pe.wait_ge(q_scaled, NT)
            pe.wait_ge(attn_masked, NT)
            pe.wait_ge(k_faded, NT)
            pe.wait_ge(s_kept, NTP)
            pe.wait_ge(state_in, 16)
            for h in range(HB):
                nc.tensor.matmul(p_v[:, h, :], vb[:, 0, h, :], Y[:, 0, h, :], start=True, stop=False)
                for b in range(BATCH_S):
                    mine = slice(b * SEQ_S, (b + 1) * SEQ_S)
                    mm = nc.tensor.matmul(p_v[:, h, mine], S_s[:, b, h, :], wT[:, 0, h, mine], start=False,
                                          stop=(b == BATCH_S - 1))
            mm.then_inc(vt_done, 1)
            pe.wait_ge(vt_kept, 1)
            for h in range(HB):
                mm = nc.tensor.transpose(p_v[:, h, :], VT[:, h, :], ident)
            mm.then_inc(v_done, 1)
            pe.wait_ge(v_kept, NT)
            pe.wait_ge(o_kept, NTP)
            for h in range(HB):
                nc.tensor.matmul(p_o[:, h, :], V[:, h, :], attn[:, 0, h, :], start=True, stop=False)
                for b in range(BATCH_S):
                    mine = slice(b * SEQ_S, (b + 1) * SEQ_S)
                    mm = nc.tensor.matmul(p_o[:, h, mine], S_s[:, b, h, :], qTe[:, 0, h, mine], start=False,
                                          stop=(b == BATCH_S - 1))
                if h == HB - 1:
                    mm.then_inc(o_done, 1)
                pe.wait_ge(v_spread, h + 1)
                for c, bank in enumerate((front_0, front_1)):
                    if h >= 1:
                        pe.wait_ge(ss_kept, 2 * (h - 1) + c + 1)
                    nc.tensor.matmul(bank[:], kdec[:, 0, h, :], V_of[:, h % 2, 4 * c:4 * c + 4, :], start=True,
                                     stop=True).then_inc(ss_done, 1)

        @block.vector
        def _(dve):
            def gaps(m):
                dve.wait_ge(rows_done, m + 1)
                nc.vector.tensor_tensor(gap[:], front_1[:], over_heads(cum[:, m, :]), ALU.subtract).then_inc(gap_ready, 1)
                dve.wait_ge(gap_ready, m + 1)
                nc.vector.tensor_scalar(E_up[:], gap[:], 0.0, None, ALU.min)
                nc.vector.tensor_scalar(E_low[:], gap[:], -1.0, 0.0, ALU.mult, ALU.min).then_inc(clamped, 1)

            def hat_k(m):
                dve.wait_ge(k_turned, m + 1)
                if not known(m, 1):
                    dve.wait_ge(khat_turned, m)
                    dve.wait_ge(k_scaled, m)
                    dve.wait_ge(k_faded, m)
                nc.vector.tensor_tensor(khat[:], front_0[:], over_heads(inv_norm[:, m, HB:2 * HB]), ALU.mult).then_inc(
                    khat_ready, 1)

            def hat_q_and_v(m, q):
                dve.wait_ge(q_turned, m + 1)
                if not known(m, 1):
                    dve.wait_ge(qhat_turned, m)
                nc.vector.tensor_tensor(qhat[:], front_1[:], over_heads(inv_norm[:, m, 0:HB]), ALU.mult).then_inc(
                    qhat_ready, 1)
                dve.wait_ge(v_turned, m + 1)
                if not known(m, 2):
                    dve.wait_ge(v_done, m - 1)
                nc.vector.tensor_tensor(vb[:, q], front_0[:], over_heads(beta[:, m, :]), ALU.mult).then_inc(vb_ready, 1)

            def lower(m):
                dve.wait_ge(gram_k, m + 1)
                dve.wait_ge(e_done, m + 1)
                if not known(m, 1):
                    dve.wait_ge(b_made, LP * m)
                for h in range(HB):
                    ins = nc.vector.scalar_tensor_tensor(out=low[:, h, :], in0=front_0[:, h, :], scalar=beta[:, m, h:h + 1],
                                                         in1=E_low[:, h, :], op0=ALU.mult, op1=ALU.mult)
                ins.then_inc(low_ready, 1)

            def attend_in_tile(m, q):
                dve.wait_ge(gram_q, m + 1)
                if not known(m, 2):
                    dve.wait_ge(o_done, m - 1)
                nc.vector.tensor_tensor(attn[:, q], front_1[:], E_up[:], ALU.mult).then_inc(attn_ready, 1)

            def first_y(m, q):
                dve.wait_ge(b0_turned, m + 1)
                if not known(m, 2):
                    dve.wait_ge(v_done, m - 1)
                nc.vector.tensor_tensor(Y[:, q], for_heads(const[:, IDENT, :], HB), front_0[:], ALU.subtract).then_inc(
                    y_first, 1)

            def keep_y(n, q, i, p):
                dve.wait_ge(y_done[p], (LP - 1) * n + i)
                if i == 1:
                    dve.wait_ge(y_first, n + 1)
                else:
                    dve.wait_ge(y_kept[p], (LP - 1) * n + i - 1)
                nc.vector.tensor_tensor(Y[:, q, pair[p]], Y[:, q, pair[p]], p_yx[p][:, 0:H2], ALU.subtract).then_inc(
                    y_kept[p], 1)

            def keep_x(n, q, i, p):
                dve.wait_ge(x_done[p], (LP - 2) * n + i)
                if i == 1:
                    dve.wait_ge(x_first, n + 1)
                else:
                    dve.wait_ge(x_kept[p], (LP - 2) * n + i - 1)
                nc.vector.tensor_tensor(X[:, q, pair[p]], X[:, q, pair[p]], p_yx[p][:, H2:2 * H2], ALU.subtract).then_inc(
                    x_kept[p], 1)

            def next_state(n):
                dve.wait_ge(s_done, n + 1)
                dve.wait_ge(o_done, n + 1)
                if known(n, 1):
                    dve.wait_ge(cleared, 1)
                else:
                    dve.wait_ge(s_kept, n)
                for h in range(HB):
                    ins = nc.vector.scalar_tensor_tensor(out=S[:, h, :], in0=S[:, h, :], scalar=last_p[:, n, h:h + 1],
                                                         in1=p_v[:, h, :], op0=ALU.mult, op1=ALU.add)
                ins.then_inc(s_kept, 1)

            def step(n, q, ahead="prompt"):
                levels = LP if ahead else LS
                for i in range(1, levels):
                    if i > 1:
                        keep_x(n, q, i - 1, 1)
                    if ahead and i == 5:
                        attend_in_tile(n + 1, 1 - q)
                    if i == STATE_AT + 1 and not known(n, 1):
                        next_state(n - 1)
                    keep_y(n, q, i, 0)
                    keep_y(n, q, i, 1)
                    if i < levels - 1:
                        keep_x(n, q, i, 0)
                    if ahead and i == 1:
                        gaps(n + 1)
                        hat_k(n + 1)
                    if ahead and i == 2:
                        hat_q_and_v(n + 1, 1 - q)
                    if ahead and i == 4:
                        lower(n + 1)
                    if ahead and i == 6:
                        first_y(n + 1, 1 - q)
                if not ahead:
                    next_state(n - 1)

            gaps(0)
            hat_k(0)
            hat_q_and_v(0, 0)
            lower(0)
            attend_in_tile(0, 0)
            first_y(0, 0)
            in_steps(dve, step, 0, NTP - 1)
            step(NTP - 1, 1, "decode")
            step(NTP, 0, None)
            for h in range(HB):
                if h == 0:
                    dve.wait_ge(v_kept, NT)
                if h >= 2:
                    dve.wait_ge(ss_done, 2 * (h - 1))
                nc.vector.tensor_tensor(V_of[:, h % 2], for_heads(V[:, h, :], BATCH_S),
                                        over_heads(const[:, BATCH_OF, 0:BATCH_S]), ALU.mult).then_inc(v_spread, 1)
                if h >= 1:
                    decode_state(nc, dve, h - 1, S_new, S_s, last_s, (front_0, front_1), ss_done, ss_kept, new_stored)
            decode_state(nc, dve, HB - 1, S_new, S_s, last_s, (front_0, front_1), ss_done, ss_kept, new_stored)

        @block.scalar
        def _(act):
            def row_exp(m):
                act.wait_ge(gap_ready, m + 1)
                if not known(m, 1):
                    act.wait_ge(q_scaled, m)
                nc.scalar.activation(e_row[:], front_1[:], ACT.Exp).then_inc(e_row_done, 1)

            def exps(m):
                act.wait_ge(clamped, m + 1)
                nc.scalar.activation(E_up[:], E_up[:], ACT.Exp)
                nc.scalar.activation(E_low[:], E_low[:], ACT.Exp).then_inc(e_done, 1)

            def keep_hats(m):
                act.wait_ge(khat_turned, m + 1)
                if not known(m, 1):
                    act.wait_ge(gram_q, m)
                nc.scalar.copy(kT[:], front_1[:]).then_inc(kT_kept, 1)
                act.wait_ge(qhat_turned, m + 1)
                if not known(m, 1):
                    act.wait_ge(q_scaled, m)
                nc.scalar.copy(qT[:], front_0[:]).then_inc(qT_kept, 1)

            def keep_z(n, i, p):
                act.wait_ge(z_done[p], (LP - 1) * n + i)
                nc.scalar.copy(Z[:, pair[p]], p_z[p][:, 0:H2]).then_inc(z_kept[p], 1)

            def keep_values(n):
                act.wait_ge(v_done, n + 1)
                nc.scalar.copy(V[:], p_v[:]).then_inc(v_kept, 1)

            def keep_outputs(n, q):
                act.wait_ge(o_done, n + 1)
                if not known(n, 2):
                    act.wait_ge(out_stored[q], 8 * (n - q))
                nc.scalar.copy(outT[:, q], p_o[:]).then_inc(o_kept, 1)

            def step(n, q, ahead="prompt"):
                levels = LP if ahead else LS
                for i in range(1, levels):
                    if i == 2 and not known(n, 1):
                        keep_values(n - 1)
                    if i == 3 and not known(n, 1):
                        keep_outputs(n - 1, 1 - q)
                    keep_z(n, i, 0)
                    keep_z(n, i, 1)
                    if ahead and i == 1:
                        row_exp(n + 1)
                    if ahead and i == 2:
                        exps(n + 1)
                    if ahead and i == 3:
                        keep_hats(n + 1)
                for p in range(2):
                    act.wait_ge(w_done[p], n + 1)
                    nc.scalar.copy(wT[:, q, pair[p]], p_z[p][:, 0:H2]).then_inc(w_kept[p], 1)

            row_exp(0)
            exps(0)
            keep_hats(0)
            in_steps(act, step, 0, NTP - 1)
            step(NTP - 1, 1, "decode")
            step(NTP, 0, None)
            act.wait_ge(vt_done, 1)
            nc.scalar.copy(VT[:], p_v[:]).then_inc(vt_kept, 1)
            keep_values(NTP)
            keep_outputs(NTP, 0)

        @block.gpsimd
        def _(pool):
            nc.gpsimd.memset(S[:], 0.0).then_inc(cleared, 1)

            def spread_g(m):
                if not known(m, 1):
                    pool.wait_ge(rows_done, m)
                nc.gpsimd.tensor_tensor(g_cols[:], over_heads(g[:, m, :]), for_heads(const[:, ONES, :], HB),
                                        ALU.mult).then_inc(g_spread, 1)

            def front(m, q, decode=False):
                levels = LS if decode else LP
                pool.wait_ge(khat_ready, m + 1)
                if not known(m, 2):
                    for p in range(2):
                        pool.wait_ge(w_done[p], m - 1)
                nc.gpsimd.tensor_tensor(kbg[:, q], khat[:], over_heads(c_key[:, m, :]), ALU.mult).then_inc(k_scaled, 1)
                if not decode:
                    spread_g(m + 1)
                pool.wait_ge(qT_kept, m + 1)
                pool.wait_ge(e_row_done, m + 1)
                if not known(m, 2):
                    pool.wait_ge(o_done, m - 1)
                nc.gpsimd.tensor_tensor(qTe[:, q], qT[:], e_row[:], ALU.mult).then_inc(q_scaled, 1)
                pool.wait_ge(low_ready, m + 1)
                if not known(m, 2):
                    for p in range(2):
                        pool.wait_ge(y_done[p], (LP - 1) * (m - 1))

                def blocks(i):
                    nc.gpsimd.tensor_tensor(below[:, q, i], low[:], for_heads(const[:, LEVEL + i, :], HB),
                                            ALU.mult).then_inc(b_made, 1)

                blocks(0)
                blocks(1)
                pool.wait_ge(b_made, LP * m + 1)
                nc.gpsimd.tensor_tensor(X[:, q], for_heads(const[:, IDENT, :], HB), below[:, q, 0],
                                        ALU.subtract).then_inc(x_first, 1)
                for i in range(2, levels):
                    blocks(i)
                if not known(m, 2):
                    pool.wait_ge(s_done, m - 1)
                pool.wait_ge(attn_ready, m + 1)
                nc.gpsimd.tensor_tensor(attn[:, q], attn[:, q], for_heads(const[:, UPTO_S if decode else UPTO, :], HB),
                                        ALU.mult).then_inc(attn_masked, 1)
                nc.gpsimd.tensor_tensor(kdec[:, q], khat[:], over_heads(c_last[:, m, :]), ALU.mult).then_inc(k_faded, 1)

            spread_g(0)
            in_steps(pool, front, 0, NTP)
            front(NTP, 0, True)


def decode_state(nc, dve, h, S_new, S_s, last_s, bank, ss_done, ss_kept, new_stored):
    for c in range(2):
        dve.wait_ge(ss_done, 2 * h + c + 1)
        if h >= 2:
            dve.wait_ge(new_stored[h % 2], 16)
        for b in range(4 * c, 4 * c + 4):
            ins = nc.vector.scalar_tensor_tensor(out=S_new[:, h % 2, b, :], in0=S_s[:, b, h, :],
                                                 scalar=last_s[:, h, b:b + 1],
                                                 in1=bank[c][:, b % 4, :], op0=ALU.mult,
                                                 op1=ALU.add)
        ins.then_inc(ss_kept, 1)


class MergeWeights:

    def __init__(self, nc, s, w_branch_a, w_branch_b, w_out):
        self.nc = nc
        self.wa, self.wb = (w.rearrange("(k p) d -> p k d", p=P) for w in (w_branch_a, w_branch_b))
        self.w_out = w_out
        self.raw_a, self.raw_b, self.raw_o = s.sbuf("raw_a", [P, HB, P]), s.sbuf("raw_b", [P, HB, P]), s.sbuf("raw_o", [P, D])
        self.wa_hi, self.wa_lo, self.wb_hi, self.wb_lo = (
            s.sbuf(n, [P, 2, HB, P], F32R) for n in ("wa_hi", "wa_lo", "wb_hi", "wb_lo"))
        self.wo_hi, self.wo_lo = (s.sbuf(n, [P, 2, D], F32R) for n in ("wo_hi", "wo_lo"))
        self.a_in, self.b_in, self.o_in, self.ab_hi, self.ab_lo, self.o_hi, self.o_lo = (s.sem(n) for n in (
            "a_in", "b_in", "o_in", "ab_hi", "ab_lo", "o_hi", "o_lo"))

    def load_branches(self, sp, n):
        cols = slice(n * P, (n + 1) * P)
        if n:
            sp.wait_ge(self.ab_lo, 2 * n)
        sp.dma_start(self.raw_a[:], self.wa[:, :, cols]).then_inc(self.a_in, 16)
        sp.dma_start(self.raw_b[:], self.wb[:, :, cols]).then_inc(self.b_in, 16)

    def load_out(self, sp, n):
        if n:
            sp.wait_ge(self.o_lo, n)
        sp.dma_start(self.raw_o[:], self.w_out[n * P:(n + 1) * P, :]).then_inc(self.o_in, 16)

    def branches_hi(self, act, n):
        act.wait_ge(self.a_in, 16 * n + 16)
        self.nc.scalar.copy(self.wa_hi[:, n % 2], self.raw_a[:]).then_inc(self.ab_hi, 1)
        act.wait_ge(self.b_in, 16 * n + 16)
        self.nc.scalar.copy(self.wb_hi[:, n % 2], self.raw_b[:]).then_inc(self.ab_hi, 1)

    def out_hi(self, act, n):
        act.wait_ge(self.o_in, 16 * n + 16)
        self.nc.scalar.copy(self.wo_hi[:, n % 2], self.raw_o[:]).then_inc(self.o_hi, 1)

    def branches_lo(self, eng, engine, n):
        eng.wait_ge(self.ab_hi, 2 * n + 1)
        engine.tensor_tensor(self.wa_lo[:, n % 2], self.raw_a[:], self.wa_hi[:, n % 2].bitcast(F32),
                             ALU.subtract).then_inc(self.ab_lo, 1)
        eng.wait_ge(self.ab_hi, 2 * n + 2)
        engine.tensor_tensor(self.wb_lo[:, n % 2], self.raw_b[:], self.wb_hi[:, n % 2].bitcast(F32),
                             ALU.subtract).then_inc(self.ab_lo, 1)

    def out_lo(self, eng, engine, n):
        eng.wait_ge(self.o_hi, n + 1)
        engine.tensor_tensor(self.wo_lo[:, n % 2], self.raw_o[:], self.wo_hi[:, n % 2].bitcast(F32),
                             ALU.subtract).then_inc(self.o_lo, 1)


def split_branches(nc, const, weights, delta_norm, attended_d, out_d, projected_d, a_hi, a_lo, b_hi, b_lo):
    with Scope(nc, "sb_") as s:
        att, z = s.sbuf("att", [P, 2, TOK]), s.sbuf("z", [P, 2, TOK])
        o = s.sbuf("o", [P, HB, TOK])
        square, spread = s.sbuf("square", [P, TOK]), s.sbuf("spread", [P, TOK])
        rms, rstd = s.sbuf("rms", [P, HB, NT]), s.sbuf("rstd", [P, HB, NT])
        gain = s.sbuf("gain", [P, 1])
        p_sum = s.psum("p_sum")
        p_rstd = [s.psum(f"p_rstd{i}") for i in range(2 * NG)]
        gain_in = s.sem("gain_in")
        a_in, z_in = ((s.sem(f"{n}0"), s.sem(f"{n}1")) for n in ("a_in", "z_in"))
        o_in = [s.sem(f"o_in{h}") for h in range(HB)]
        (a_hi_done, a_lo_done, squared, summed, averaged, rooted, inverted, spread_done, on_rows, scaled, gated, hi_done,
         lo_done) = (s.sem(n) for n in ("a_hi_done", "a_lo_done", "squared", "summed", "averaged", "rooted", "inverted",
                                        "spread_done", "on_rows", "scaled", "gated", "hi_done", "lo_done"))
        block = s.block()

        @block.sync
        def _(sp):
            for h in range(HB):
                sp.dma_start(o[:, h], out_d[h]).then_inc(o_in[h], 16)
            sp.dma_start(gain[:], delta_norm.rearrange("(p a) -> p a", a=1)).then_inc(gain_in, 16)
            for h in range(HB):
                if h >= 2:
                    sp.wait_ge(a_lo_done, h - 1)
                sp.dma_start(att[:, h % 2], attended_d[h]).then_inc(a_in[h % 2], 16)
                if h < 2:
                    sp.dma_start(z[:, h % 2], projected_d[h]).then_inc(z_in[h % 2], 16)
            weights.load_branches(sp, 0)
            weights.load_out(sp, 0)
            weights.load_branches(sp, 1)
            for h in range(2, HB):
                sp.wait_ge(gated, h - 1)
                sp.dma_start(z[:, h % 2], projected_d[h]).then_inc(z_in[h % 2], 16)

        @block.scalar
        def _(act):
            def attended_hi(h):
                act.wait_ge(a_in[h % 2], 16 * (h // 2 + 1))
                nc.scalar.copy(a_hi[:, h], att[:, h % 2]).then_inc(a_hi_done, 1)

            for h in range(HB):
                act.wait_ge(o_in[h], 16)
                if h >= 2:
                    act.wait_ge(summed, h - 1)
                nc.scalar.activation((square, spread)[h % 2][:], o[:, h], ACT.Square).then_inc(squared, 1)
                if h >= 1:
                    attended_hi(h - 1)
            act.wait_ge(averaged, 1)
            nc.scalar.activation(rms[:], rms[:], ACT.Sqrt).then_inc(rooted, 1)
            attended_hi(HB - 1)
            weights.branches_hi(act, 0)
            weights.out_hi(act, 0)
            weights.branches_hi(act, 1)
            for h in range(HB):
                act.wait_ge(gated, h + 1)
                nc.scalar.copy(b_hi[:, h], o[:, h]).then_inc(hi_done, 1)

        @block.tensor
        def _(pe):
            for h in range(HB):
                pe.wait_ge(squared, h + 1)
                for t in range(NT):
                    mm = nc.tensor.matmul(p_sum[:, h * NT + t:h * NT + t + 1],
                                          (square, spread)[h % 2][:, t * P:(t + 1) * P], const[:, ONES, 0:1], start=True,
                                          stop=True)
                mm.then_inc(summed, 1)
            for h in range(HB):
                pe.wait_ge(spread_done, h + 1)
                if h >= 2:
                    pe.wait_ge(scaled, h - 1)
                for t in range(NT):
                    g, at = t * P // TG, t * P % TG
                    mm = nc.tensor.matmul(p_rstd[NG * (h % 2) + g][:, at:at + P],
                                          (square, spread)[h % 2][:, t * P:(t + 1) * P], const[:, IDENT, :], start=True,
                                          stop=True)
                mm.then_inc(on_rows, 1)

        @block.gpsimd
        def _(pool):
            for h in range(HB):
                pool.wait_ge(a_hi_done, h + 1)
                nc.gpsimd.tensor_tensor(a_lo[:, h], att[:, h % 2], a_hi[:, h].bitcast(F32), ALU.subtract).then_inc(
                    a_lo_done, 1)
            weights.branches_lo(pool, nc.gpsimd, 0)
            weights.out_lo(pool, nc.gpsimd, 0)
            weights.branches_lo(pool, nc.gpsimd, 1)

        @block.vector
        def _(dve):
            def spread_rstd(h):
                if h >= 2:
                    dve.wait_ge(on_rows, h - 1)
                nc.vector.tensor_copy((square, spread)[h % 2][:].rearrange("p (t c) -> p t c", t=NT),
                                      over_heads(rstd[:, h, :])).then_inc(spread_done, 1)

            dve.wait_ge(summed, HB)
            nc.vector.tensor_scalar(rms[:], p_sum[:, 0:HB * NT].rearrange("p (h t) -> p h t", h=HB), 1.0 / P, EPS,
                                    ALU.mult, ALU.add).then_inc(averaged, 1)
            dve.wait_ge(rooted, 1)
            nc.vector.reciprocal(rstd[:], rms[:]).then_inc(inverted, 1)
            dve.wait_ge(inverted, 1)
            spread_rstd(0)
            spread_rstd(1)
            dve.wait_ge(gain_in, 16)
            for h in range(HB + 1):
                if h < HB:
                    dve.wait_ge(on_rows, h + 1)
                    for g in range(NG):
                        mine = slice(g * TG, (g + 1) * TG)
                        ins = nc.vector.tensor_tensor(o[:, h, mine], p_rstd[NG * (h % 2) + g][:, 0:TG], o[:, h, mine],
                                                      ALU.mult)
                    ins.then_inc(scaled, 1)
                    if h + 2 < HB:
                        spread_rstd(h + 2)
                    dve.wait_ge(scaled, h + 1)
                    dve.wait_ge(z_in[h % 2], 16 * (h // 2 + 1))
                    nc.vector.scalar_tensor_tensor(out=o[:, h], in0=o[:, h], scalar=gain[:], in1=z[:, h % 2],
                                                   op0=ALU.mult, op1=ALU.mult).then_inc(gated, 1)
                if h:
                    dve.wait_ge(hi_done, h)
                    nc.vector.tensor_tensor(b_lo[:, h - 1], o[:, h - 1], b_hi[:, h - 1].bitcast(F32),
                                            ALU.subtract).then_inc(lo_done, 1)


def merge(nc, x, weights, a_hi, a_lo, b_hi, b_lo, projected_d):
    KB = HB
    FIRST_GATE = HB
    with Scope(nc, "mg_") as s:
        wa_hi, wa_lo, wb_hi, wb_lo, wo_hi, wo_lo = (weights.wa_hi, weights.wa_lo, weights.wb_hi, weights.wb_lo,
                                                    weights.wo_hi, weights.wo_lo)
        gate_a, gate_b = s.sbuf("gate_a", [P, 2, TOK]), s.sbuf("gate_b", [P, 2, TOK])
        part_a, part_b = s.sbuf("part_a", [P, 2, TG]), s.sbuf("part_b", [P, 2, TG])
        m_hi, m_lo = (s.sbuf(n, [P, 2, TOK], F32R) for n in ("m_hi", "m_lo"))
        p_a = [s.psum(f"p_a{i}") for i in range(2)]
        p_b = [s.psum(f"p_b{i}") for i in range(2)]
        p_out = [s.psum(f"p_out{i}") for i in range(4)]
        gates_in = s.sem("gates_in0"), s.sem("gates_in1")
        branches, gated_a, gated_b, summed, mhi_done, mlo_done, projected, added = (s.sem(n) for n in (
            "branches", "gated_a", "gated_b", "summed", "mhi_done", "mlo_done", "projected", "added"))
        NO = 2 * NT
        block = s.block()

        @block.sync
        def _(sp):
            for n in range(1, KD):
                if n >= 2:
                    weights.load_branches(sp, n)
                weights.load_out(sp, n)

        @block.gpsimd
        def _(pool):
            for n in range(KD):
                if n >= 2:
                    pool.wait_ge(gated_b, NG * (n - 1))
                pool.dma_start(gate_a[:, n % 2], projected_d[FIRST_GATE + n]).then_inc(gates_in[n % 2], 16)
                pool.dma_start(gate_b[:, n % 2], projected_d[FIRST_GATE + KD + n]).then_inc(gates_in[n % 2], 16)

        @block.scalar
        def _(act):
            def split_branch(n):
                if n >= 2:
                    act.wait_ge(branches, NG * (n - 1))
                weights.branches_hi(act, n)

            def split_out(n):
                if n >= 2:
                    act.wait_ge(projected, NO * (n - 1))
                weights.out_hi(act, n)

            for n in range(KD):
                for g in range(NG):
                    act.wait_ge(summed, NG * n + g + 1)
                    if g == 0 and n >= 2:
                        act.wait_ge(projected, NO * (n - 1))
                    nc.scalar.copy(m_hi[:, n % 2, g * TG:(g + 1) * TG], part_a[:, (NG * n + g) % 2]).then_inc(mhi_done, 1)
                if n + 2 < KD:
                    split_branch(n + 2)
                if n + 1 < KD:
                    split_out(n + 1)

        @block.vector
        def _(dve):
            def add_out(n, outs=range(NO)):
                for o in outs:
                    dve.wait_ge(projected, NO * n + o + 1)
                    if n:
                        dve.wait_ge(added, NO * (n - 1) + o + 1)
                    xs = x[:, o // 2, o % 2 * 512:o % 2 * 512 + 512]
                    nc.vector.tensor_tensor(xs, p_out[(NO * n + o) % 4][:], xs, ALU.add).then_inc(added, 1)

            for n in range(KD):
                dve.wait_ge(gates_in[n % 2], 32 * (n // 2 + 1))
                for g in range(NG):
                    u, mine = NG * n + g, slice(g * TG, (g + 1) * TG)
                    dve.wait_ge(branches, u + 1)
                    if u >= 2:
                        dve.wait_ge(mlo_done, u - 1)
                        dve.wait_ge(summed, u - 1)
                    nc.vector.tensor_tensor(part_a[:, u % 2], p_a[u % 2][:, 0:TG], gate_a[:, n % 2, mine],
                                            ALU.mult).then_inc(gated_a, 1)
                    nc.vector.tensor_tensor(part_b[:, u % 2], p_b[u % 2][:, 0:TG], gate_b[:, n % 2, mine],
                                            ALU.mult).then_inc(gated_b, 1)
                    dve.wait_ge(gated_b, u + 1)
                    nc.vector.tensor_tensor(part_a[:, u % 2], part_a[:, u % 2], part_b[:, u % 2], ALU.add).then_inc(summed, 1)
                    if g == NG - 1 and n:
                        add_out(n - 1, [0])
                    dve.wait_ge(mhi_done, u + 1)
                    nc.vector.tensor_tensor(m_lo[:, n % 2, mine], part_a[:, u % 2], m_hi[:, n % 2, mine].bitcast(F32),
                                            ALU.subtract).then_inc(mlo_done, 1)
                if n:
                    add_out(n - 1, range(1, NO))
                if n + 2 < KD:
                    weights.branches_lo(dve, nc.vector, n + 2)
                if n + 1 < KD:
                    weights.out_lo(dve, nc.vector, n + 1)
            add_out(KD - 1)

        @block.tensor
        def _(pe):
            def branch(n):
                for g in range(NG):
                    u, mine = NG * n + g, slice(g * TG, (g + 1) * TG)
                    pe.wait_ge(weights.ab_lo, 2 * n + 2)
                    if u >= 2:
                        pe.wait_ge(gated_b, u - 1)
                    three_passes(nc, p_a[u % 2][:, 0:TG], lambda k: (wa_hi[:, n % 2, k, :], wa_lo[:, n % 2, k, :]),
                                 lambda k: (a_hi[:, k, mine], a_lo[:, k, mine]), range(KB))
                    three_passes(nc, p_b[u % 2][:, 0:TG], lambda k: (wb_hi[:, n % 2, k, :], wb_lo[:, n % 2, k, :]),
                                 lambda k: (b_hi[:, k, mine], b_lo[:, k, mine]), range(KB)).then_inc(branches, 1)

            def out(n):
                pe.wait_ge(weights.o_lo, n + 1)
                for o in range(NO):
                    tokens, cols = slice(o // 2 * P, (o // 2 + 1) * P), slice(o % 2 * 512, o % 2 * 512 + 512)
                    if o % 6 == 0:
                        pe.wait_ge(mlo_done, NG * n + o // 6 + 1)
                    if NO * n + o >= 4:
                        pe.wait_ge(added, NO * n + o - 3)
                    three_passes(nc, p_out[(NO * n + o) % 4][:], lambda k: (m_hi[:, n % 2, tokens], m_lo[:, n % 2, tokens]),
                                 lambda k: (wo_hi[:, n % 2, cols], wo_lo[:, n % 2, cols]), [0]).then_inc(projected, 1)

            for n in range(KD):
                branch(n)
                if n:
                    out(n - 1)
            out(KD - 1)


INPUTS = ["x_prompt", "x_sample", "cache_attn_k", "cache_attn_v", "cache_idx_k", "state_conv", "state_delta",
          "ffn1_norm", "ffn1_w_gate", "ffn1_w_up", "ffn1_w_down", "mix_norm", "w_in", "conv_w", "a_log", "dt_bias",
          "delta_norm", "w_branch_a", "w_branch_b", "w_out", "ffn2_norm", "ffn2_w_gate", "ffn2_w_up", "ffn2_w_down",
          "final_norm"]
OUTPUTS = [("y_prompt", (1, SEQ, D)), ("y_sample", (BATCH_S, SEQ_S, D)),
           ("new_k", (1, 1, SEQ, KV, HD)), ("new_v", (1, 1, SEQ, KV, HD)), ("new_idx_k", (1, 1, SEQ, HD)),
           ("new_conv", (1, 1, CONV_W - 1, CONV_CH)), ("new_delta", (1, 1, HB, DK, DK)),
           ("new_k_s", (1, BATCH_S, SEQ_S, KV, HD)), ("new_v_s", (1, BATCH_S, SEQ_S, KV, HD)),
           ("new_idx_k_s", (1, BATCH_S, SEQ_S, HD)), ("new_conv_s", (1, BATCH_S, CONV_W - 1, CONV_CH)),
           ("new_delta_s", (1, BATCH_S, HB, DK, DK))]


def encoder_step(nc, i, o, const_in):
    projected_d = nc.dram_tensor("projected_d", (HB + 2 * KD, P, TOK), F32, kind="Internal").ap()
    conv_d = nc.dram_tensor("conv_d", (NC, P, TOK), F32, kind="Internal").ap()
    delta_d = nc.dram_tensor("delta_d", (HB, P, TOK), F32, kind="Internal").ap()
    attended_d = nc.dram_tensor("attended_d", (HB, P, TOK), F32, kind="Internal").ap()
    w_in = i["w_in"][0]
    with Scope(nc, "") as top:
        x, const = top.sbuf("x", [P, NT, D]), top.sbuf("const", [P, CONSTS, P])
        ffn(nc, x, const, i["ffn1_norm"][0], i["ffn1_w_gate"][0], i["ffn1_w_up"][0], i["ffn1_w_down"][0], "ffn1_",
            start=(i["x_prompt"], i["x_sample"], const_in))

        with Scope(nc, "mx_") as mix:
            small = mix.sbuf("small", [P, NT, 12])
            decays, inv_norm = Decays(nc, mix), mix.sbuf("inv_norm", [P, NT, 2 * HB])
            sums, tail = mix.sbuf("sums", [P, NC, NT]), mix.sbuf("tail", [P, NC, (CONV_W - 1) * (1 + BATCH_S)])
            with Scope(nc, "sa_") as sparse:
                qkT, va = sparse.sbuf("qkT", [P, 5, TOK]), sparse.sbuf("va", [P, NT, P])
                scores = sparse.sbuf("scores", [P, SCORES])
                with Scope(nc, "h_") as s:
                    hT_hi, hT_lo = s.sbuf("hT_hi", [P, KD, TOK], F32R), s.sbuf("hT_lo", [P, KD, TOK], F32R)
                    project_small(nc, x, const, i["mix_norm"][0], hT_hi, hT_lo, w_in, va, small, o["new_k"], o["new_v"], o["new_idx_k"],
                                  o["new_k_s"], o["new_v_s"], o["new_idx_k_s"])
                    with Scope(nc, "ix_") as index:
                        qiT = index.sbuf("qiT", [P, 4, TOK])
                        project_turned(nc, const, decays, small, i["a_log"], i["dt_bias"], hT_hi, hT_lo, w_in, qkT, qiT)
                        score(nc, const, qiT, small, i["cache_idx_k"], scores)
                    select_and_project(nc, const, hT_hi, hT_lo, w_in, scores, i["conv_w"][0], i["state_conv"],
                                       projected_d, conv_d, sums, tail)
                attend(nc, const, qkT, va, scores, i["cache_attn_k"], i["cache_attn_v"], attended_d, sums, inv_norm,
                       tail, o["new_conv"], o["new_conv_s"])
            delta(nc, const, decays, inv_norm, conv_d, i["state_delta"], delta_d, o["new_delta"], o["new_delta_s"])
            with Scope(nc, "br_") as s:
                a_hi, a_lo, b_hi, b_lo = (s.sbuf(n, [P, HB, TOK], F32R) for n in ("a_hi", "a_lo", "b_hi", "b_lo"))
                weights = MergeWeights(nc, s, i["w_branch_a"][0], i["w_branch_b"][0], i["w_out"][0])
                split_branches(nc, const, weights, i["delta_norm"][0], attended_d, delta_d, projected_d, a_hi, a_lo, b_hi, b_lo)
                merge(nc, x, weights, a_hi, a_lo, b_hi, b_lo, projected_d)

        ffn(nc, x, const, i["ffn2_norm"][0], i["ffn2_w_gate"][0], i["ffn2_w_up"][0], i["ffn2_w_down"][0], "ffn2_",
            finish=(i["final_norm"], o["y_prompt"], o["y_sample"]))


def kernel(**inputs):
    import concourse.bacc as bacc
    from concourse.bass_utils import run_bass_kernel_spmd

    nc = bacc.Bacc("TRN2", target_bir_lowering=False, num_devices=1)
    arrays, ins, outs = {}, {}, {}
    for name in INPUTS:
        a = np.ascontiguousarray(inputs[name])
        arrays[f"in_{name}"] = a
        ins[name] = nc.dram_tensor(f"in_{name}", a.shape, mybir.dt.from_np(a.dtype), kind="ExternalInput").ap()
    arrays["in_constants"] = constants()
    const_in = nc.dram_tensor("in_constants", (P, CONSTS, P), F32, kind="ExternalInput").ap()
    for name, shape in OUTPUTS:
        outs[name] = nc.dram_tensor(f"out_{name}", shape, F32, kind="ExternalOutput").ap()
    encoder_step(nc, ins, outs, const_in)
    got = run_bass_kernel_spmd(nc, [arrays], core_ids=[0]).results[0]
    return tuple(got[f"out_{name}"] for name, _ in OUTPUTS)
```
